# Optimizing a Trainium2 kernel written in Bass

```python
import numpy as np
import jax, jax.numpy as jnp
from jax import lax

D_MODEL = 1024
BATCH = 1
SEQ = 256
DEPTH = 2

GRID_W = 64
CTX_LEN = 256
N_MIXERS = 2
N_HEADS = 16
HEAD_DIM = D_MODEL // N_HEADS
NA_KH = 8
NA_KW = 16
NA_QCB = NA_KW
NA_KCB = 2 * NA_KW
WA_KV_HEADS = 4
WA_GROUPS = N_HEADS // WA_KV_HEADS
WA_WINDOW = 128
WA_BLOCK = 128
D_FF = 2816
FFN_RES = 0.5
ROPE_BASE = 10000.0
N_MOD = 9
ALPHA = (2 * DEPTH) ** 0.25
BETA = (8 * DEPTH) ** -0.25
LN_EPS = 1e-5
NEG_INF = -1e30
N_NA_LAYERS = (DEPTH + 1) // 2
N_WA_LAYERS = DEPTH // 2


def layer_norm(x, g, b):
    xf = x.astype(jnp.float32)
    mu = jnp.mean(xf, axis=-1, keepdims=True)
    var = jnp.mean(jnp.square(xf - mu), axis=-1, keepdims=True)
    return ((xf - mu) * lax.rsqrt(var + LN_EPS)).astype(x.dtype) * g + b

def modulate(h, shift, scale):
    return h * (1.0 + scale) + shift

def swiglu(u, w_in, w_out):
    a, v = jnp.split(u @ w_in, 2, axis=-1)
    return (jax.nn.silu(a) * v) @ w_out

def ffn_sublayer(h, shift, scale, gate, w_in, w_out, g, b):
    y = swiglu(modulate(h, shift, scale), w_in, w_out)
    return layer_norm(ALPHA * h + FFN_RES * gate * y, g, b)

def axial_rope(x):
    S = x.shape[1]
    t = jnp.arange(S, dtype=jnp.int32)
    rows = (t // GRID_W).astype(jnp.float32)
    cols = (t % GRID_W).astype(jnp.float32)
    n = HEAD_DIM // 4
    inv_freq = ROPE_BASE ** (-jnp.arange(n, dtype=jnp.float32) / n)
    half = HEAD_DIM // 2

    def rot(xa, pos):
        ang = pos[:, None] * inv_freq[None, :]
        cos = jnp.cos(ang)[None, :, None, :].astype(x.dtype)
        sin = jnp.sin(ang)[None, :, None, :].astype(x.dtype)
        x1, x2 = xa[..., :n], xa[..., n:]
        return jnp.concatenate([x1 * cos - x2 * sin, x2 * cos + x1 * sin], axis=-1)

    return jnp.concatenate([rot(x[..., :half], rows), rot(x[..., half:], cols)], axis=-1)

def ctx_attention(qc, kc, vc, sink):
    B, C, H, d = qc.shape
    hk = kc.shape[2]
    g = H // hk
    qg = qc.reshape(B, C, hk, g, d)
    s = jnp.einsum('bqhgd,bkhd->bhgqk', qg, kc).astype(jnp.float32)
    if sink is not None:
        sk = jnp.broadcast_to(sink.astype(jnp.float32).reshape(1, hk, g, 1, 1), s.shape[:-1] + (1,))
        s = jnp.concatenate([s, sk], axis=-1)
    p = jax.nn.softmax(s, axis=-1)[..., :C].astype(vc.dtype)
    o = jnp.einsum('bhgqk,bkhd->bqhgd', p, vc)
    return o.reshape(B, C, H * d)

def neighborhood_attention(u_lat, u_ctx, w_qkv, w_o, rpb, with_ctx_out):
    B, S, _ = u_lat.shape
    C = u_ctx.shape[1]
    rows = S // GRID_W
    kh = min(NA_KH, rows)
    scale = HEAD_DIM ** -0.5
    qkv = (u_lat @ w_qkv).reshape(B, rows, GRID_W, 3, N_HEADS, HEAD_DIM)
    q = qkv[:, :, :, 0] * scale
    k = qkv[:, :, :, 1]
    v = qkv[:, :, :, 2]
    kvc = (u_ctx @ w_qkv[:, D_MODEL:]).reshape(B, C, 2, N_HEADS, HEAD_DIM)
    kc, vc = kvc[:, :, 0], kvc[:, :, 1]

    ncb = GRID_W // NA_QCB
    qcol = np.arange(GRID_W).reshape(ncb, NA_QCB)
    blk_start = np.clip(np.arange(ncb) * NA_QCB - NA_KW // 2, 0, GRID_W - NA_KCB)
    kcol = blk_start[:, None] + np.arange(NA_KCB)[None, :]
    win_start = np.clip(qcol - NA_KW // 2, 0, GRID_W - NA_KW)
    col_valid = (kcol[:, None, :] >= win_start[..., None]) & (kcol[:, None, :] < win_start[..., None] + NA_KW)
    col_off = np.clip(kcol[:, None, :] - qcol[..., None], -(NA_KW - 1), NA_KW - 1) + NA_KW - 1
    bias_cols = jnp.where(col_valid, rpb[:, :, col_off].astype(jnp.float32), NEG_INF)
    n_win = kh * NA_KCB

    def row_block(r):
        rs = jnp.clip(r - kh // 2, 0, rows - kh)
        q_r = lax.dynamic_index_in_dim(q, r, axis=1, keepdims=False).reshape(B, ncb, NA_QCB, N_HEADS, HEAD_DIM)
        k_r = lax.dynamic_slice_in_dim(k, rs, kh, axis=1)[:, :, kcol]
        v_r = lax.dynamic_slice_in_dim(v, rs, kh, axis=1)[:, :, kcol]
        row_idx = rs + jnp.arange(kh) - r + NA_KH - 1
        bias = jnp.take(bias_cols, row_idx, axis=1).transpose(0, 2, 3, 1, 4)[None]
        s_win = jnp.einsum('bcqhd,bicjhd->bhcqij', q_r, k_r).astype(jnp.float32) + bias
        s_win = s_win.reshape(B, N_HEADS, ncb, NA_QCB, n_win)
        s_ctx = jnp.einsum('bcqhd,bkhd->bhcqk', q_r, kc).astype(jnp.float32)
        p = jax.nn.softmax(jnp.concatenate([s_win, s_ctx], axis=-1), axis=-1).astype(v.dtype)
        p_win = p[..., :n_win].reshape(B, N_HEADS, ncb, NA_QCB, kh, NA_KCB)
        p_ctx = p[..., n_win:]
        o = (jnp.einsum('bhcqij,bicjhd->bcqhd', p_win, v_r)
             + jnp.einsum('bhcqk,bkhd->bcqhd', p_ctx, vc))
        return o.reshape(B, GRID_W, D_MODEL)

    out = lax.map(row_block, jnp.arange(rows, dtype=jnp.int32))
    y_lat = out.transpose(1, 0, 2, 3).reshape(B, S, D_MODEL) @ w_o
    y_ctx = None
    if with_ctx_out:
        qc = (u_ctx @ w_qkv[:, :D_MODEL]).reshape(B, C, N_HEADS, HEAD_DIM) * scale
        y_ctx = ctx_attention(qc, kc, vc, None) @ w_o
    return y_lat, y_ctx

def window_gqa(u_lat, u_ctx, w_qkv, w_o, sinks, with_ctx_out):
    B, S, _ = u_lat.shape
    C = u_ctx.shape[1]
    dq = N_HEADS * HEAD_DIM
    dkv = WA_KV_HEADS * HEAD_DIM
    scale = HEAD_DIM ** -0.5
    qkv = u_lat @ w_qkv
    q = axial_rope(qkv[..., :dq].reshape(B, S, N_HEADS, HEAD_DIM)) * scale
    k = axial_rope(qkv[..., dq:dq + dkv].reshape(B, S, WA_KV_HEADS, HEAD_DIM))
    v = qkv[..., dq + dkv:].reshape(B, S, WA_KV_HEADS, HEAD_DIM)
    kvc = u_ctx @ w_qkv[:, dq:]
    kc = kvc[..., :dkv].reshape(B, C, WA_KV_HEADS, HEAD_DIM)
    vc = kvc[..., dkv:].reshape(B, C, WA_KV_HEADS, HEAD_DIM)

    nb = S // WA_BLOCK
    pad = ((0, 0), (WA_BLOCK, WA_BLOCK), (0, 0), (0, 0))
    k_pad = jnp.pad(k, pad)
    v_pad = jnp.pad(v, pad)
    q_blk = q.reshape(B, nb, WA_BLOCK, WA_KV_HEADS, WA_GROUPS, HEAD_DIM)
    sink = sinks.astype(jnp.float32).reshape(1, WA_KV_HEADS, WA_GROUPS, 1, 1)
    qi = jnp.arange(WA_BLOCK, dtype=jnp.int32)
    kj = jnp.arange(3 * WA_BLOCK, dtype=jnp.int32)
    n_win = 3 * WA_BLOCK

    def band_block(b):
        qb = lax.dynamic_index_in_dim(q_blk, b, axis=1, keepdims=False)
        kb = lax.dynamic_slice_in_dim(k_pad, b * WA_BLOCK, n_win, axis=1)
        vb = lax.dynamic_slice_in_dim(v_pad, b * WA_BLOCK, n_win, axis=1)
        pos_q = b * WA_BLOCK + qi
        pos_k = (b - 1) * WA_BLOCK + kj
        valid = ((jnp.abs(pos_q[:, None] - pos_k[None, :]) <= WA_WINDOW)
                 & (pos_k >= 0)[None, :] & (pos_k < S)[None, :])
        s_win = jnp.where(valid, jnp.einsum('bqhgd,bkhd->bhgqk', qb, kb).astype(jnp.float32), NEG_INF)
        s_ctx = jnp.einsum('bqhgd,bkhd->bhgqk', qb, kc).astype(jnp.float32)
        s_sink = jnp.broadcast_to(sink, s_win.shape[:-1] + (1,))
        p = jax.nn.softmax(jnp.concatenate([s_win, s_ctx, s_sink], axis=-1), axis=-1).astype(v.dtype)
        o = (jnp.einsum('bhgqk,bkhd->bqhgd', p[..., :n_win], vb)
             + jnp.einsum('bhgqk,bkhd->bqhgd', p[..., n_win:n_win + C], vc))
        return o.reshape(B, WA_BLOCK, D_MODEL)

    out = lax.map(band_block, jnp.arange(nb, dtype=jnp.int32))
    y_lat = out.transpose(1, 0, 2, 3).reshape(B, S, D_MODEL) @ w_o
    y_ctx = None
    if with_ctx_out:
        qc = (u_ctx @ w_qkv[:, :dq]).reshape(B, C, N_HEADS, HEAD_DIM) * scale
        y_ctx = ctx_attention(qc, kc, vc, sinks) @ w_o
    return y_lat, y_ctx

def first_inputs(seed: int = 0) -> dict:
    key = jax.random.key(seed)
    ks = jax.random.split(key, 16)
    f32 = jnp.float32
    dq = N_HEADS * HEAD_DIM
    dkv = WA_KV_HEADS * HEAD_DIM

    def nrm(k, shape, s):
        return jax.random.normal(k, shape, f32) * s

    return {
        "x": nrm(ks[0], (BATCH, SEQ, D_MODEL), 1.0),
        "c": nrm(ks[1], (BATCH, D_MODEL), 1.0),
        "ctx": nrm(ks[2], (BATCH, CTX_LEN, D_MODEL), 1.0),
        "c_ctx": nrm(ks[3], (D_MODEL,), 1.0),
        "w_mod": nrm(ks[4], (DEPTH, D_MODEL, N_MOD * D_MODEL), 0.5 * D_MODEL ** -0.5),
        "b_mod": nrm(ks[5], (DEPTH, N_MOD * D_MODEL), 0.02),
        "ln_g": 1.0 + nrm(ks[6], (DEPTH, 3, D_MODEL), 0.02),
        "ln_b": nrm(ks[7], (DEPTH, 3, D_MODEL), 0.02),
        "ffn_w_in": nrm(ks[8], (DEPTH, 2, D_MODEL, 2 * D_FF), D_MODEL ** -0.5),
        "ffn_w_out": nrm(ks[9], (DEPTH, 2, D_FF, D_MODEL), BETA * D_FF ** -0.5),
        "na_w_qkv": nrm(ks[10], (N_NA_LAYERS, D_MODEL, 3 * dq), D_MODEL ** -0.5),
        "na_w_o": nrm(ks[11], (N_NA_LAYERS, dq, D_MODEL), BETA * dq ** -0.5),
        "na_rpb": nrm(ks[12], (N_NA_LAYERS, N_HEADS, 2 * NA_KH - 1, 2 * NA_KW - 1), 0.1),
        "wa_w_qkv": nrm(ks[13], (N_WA_LAYERS, D_MODEL, dq + 2 * dkv), D_MODEL ** -0.5),
        "wa_w_o": nrm(ks[14], (N_WA_LAYERS, dq, D_MODEL), BETA * dq ** -0.5),
        "wa_sinks": nrm(ks[15], (N_WA_LAYERS, N_HEADS), 0.5),
    }

def first_block(x, c, ctx, c_ctx, w_mod, b_mod, ln_g, ln_b, ffn_w_in, ffn_w_out,
              na_w_qkv, na_w_o, na_rpb, wa_w_qkv, wa_w_o, wa_sinks):
    h_lat, h_ctx = x, ctx
    silu_c = jax.nn.silu(c)
    silu_cc = jax.nn.silu(c_ctx)
    for i in range(DEPTH):
        ctx_needed = i < DEPTH - 1
        m_lat = jnp.split((silu_c @ w_mod[i] + b_mod[i])[:, None, :], N_MOD, axis=-1)
        m_ctx = jnp.split((silu_cc @ w_mod[i] + b_mod[i])[None, None, :], N_MOD, axis=-1)

        h_lat = ffn_sublayer(h_lat, m_lat[0], m_lat[1], m_lat[2], ffn_w_in[i, 0], ffn_w_out[i, 0], ln_g[i, 0], ln_b[i, 0])
        h_ctx = ffn_sublayer(h_ctx, m_ctx[0], m_ctx[1], m_ctx[2], ffn_w_in[i, 0], ffn_w_out[i, 0], ln_g[i, 0], ln_b[i, 0])

        u_lat = modulate(h_lat, m_lat[3], m_lat[4])
        u_ctx = modulate(h_ctx, m_ctx[3], m_ctx[4])
        j = i // N_MIXERS
        if i % N_MIXERS == 0:
            y_lat, y_ctx = neighborhood_attention(u_lat, u_ctx, na_w_qkv[j], na_w_o[j], na_rpb[j], ctx_needed)
        else:
            y_lat, y_ctx = window_gqa(u_lat, u_ctx, wa_w_qkv[j], wa_w_o[j], wa_sinks[j], ctx_needed)
        h_lat = layer_norm(ALPHA * h_lat + m_lat[5] * y_lat, ln_g[i, 1], ln_b[i, 1])

        h_lat = ffn_sublayer(h_lat, m_lat[6], m_lat[7], m_lat[8], ffn_w_in[i, 1], ffn_w_out[i, 1], ln_g[i, 2], ln_b[i, 2])
        if ctx_needed:
            h_ctx = layer_norm(ALPHA * h_ctx + m_ctx[5] * y_ctx, ln_g[i, 1], ln_b[i, 1])
            h_ctx = ffn_sublayer(h_ctx, m_ctx[6], m_ctx[7], m_ctx[8], ffn_w_in[i, 1], ffn_w_out[i, 1], ln_g[i, 2], ln_b[i, 2])
    return h_lat


SGU_HEADS = 4
SGU_HEAD_DIM = 64
SGU_W = SGU_HEADS * SGU_HEAD_DIM
CHUNK = 128
FNET_GROUPS = 4
FNET_GROUP_DIM = 64
FNET_W = FNET_GROUPS * FNET_GROUP_DIM
MLA_HEADS = 4
QK_NOPE_DIM = 128
QK_ROPE_DIM = 64
QK_DIM = QK_NOPE_DIM + QK_ROPE_DIM
V_DIM = 128
Q_LORA = 256
KV_LORA = 128
MLA_W = MLA_HEADS * V_DIM
Q_BLOCK = 128
ROPE_THETA = 10000.0
OFF_U = 0
OFF_V = OFF_U + SGU_W
OFF_F = OFF_V + SGU_W
OFF_Q = OFF_F + FNET_W
OFF_KV = OFF_Q + Q_LORA
OFF_KR = OFF_KV + KV_LORA
IN_W = OFF_KR + QK_ROPE_DIM
MIX_W = SGU_W + FNET_W + MLA_W
N_EXPERTS = 16
EC_FACTOR = 2
D_EXPERT = 512
EPS = 1e-6


def rms_norm(x):
    xf = x.astype(jnp.float32)
    return (xf * lax.rsqrt(jnp.mean(xf * xf, axis=-1, keepdims=True) + EPS)).astype(x.dtype)

def ada_modulation(cond, w_ada, b_ada):
    m = (jax.nn.silu(cond) @ w_ada + b_ada)[:, None, :]
    return jnp.split(m, 6, axis=-1)

def modulate_2(x, shift, scale):
    return rms_norm(x) * (1 + scale) + shift

def rope_1d(x, pos):
    half = x.shape[-1] // 2
    freqs = ROPE_THETA ** (-jnp.arange(half, dtype=jnp.float32) / half)
    ang = pos.astype(jnp.float32)[:, None] * freqs
    cos = jnp.cos(ang)[:, None, :]
    sin = jnp.sin(ang)[:, None, :]
    xf = x.astype(jnp.float32)
    x1, x2 = xf[..., :half], xf[..., half:]
    return jnp.concatenate([x1 * cos - x2 * sin, x1 * sin + x2 * cos], axis=-1).astype(x.dtype)

def rope_2d(x, pos_row, pos_col):
    half = x.shape[-1] // 2
    return jnp.concatenate([rope_1d(x[..., :half], pos_row), rope_1d(x[..., half:], pos_col)], axis=-1)

def with_rope(t, pos_row, pos_col):
    return jnp.concatenate([t[..., :QK_NOPE_DIM], rope_2d(t[..., QK_NOPE_DIM:], pos_row, pos_col)], axis=-1)

def chunk_mlp(pu, pv, sgu_norm, w_sgu, b_sgu):
    b, n, _ = pu.shape
    u = jax.nn.gelu(pu)
    v = rms_norm(jax.nn.gelu(pv)) * sgu_norm
    v = v.reshape(b, n // CHUNK, CHUNK, SGU_HEADS, SGU_HEAD_DIM)
    z = jnp.einsum('hpq,bcqhd->bcphd', w_sgu, v) + b_sgu.T[:, :, None]
    return u * z.reshape(b, n, SGU_W)

def fourier_mix(pf):
    b, n, _ = pf.shape
    f = pf.reshape(b, n, FNET_GROUPS, FNET_GROUP_DIM).astype(jnp.float32)
    y = jnp.fft.fft2(f, axes=(1, 3), norm="ortho").real
    return y.reshape(b, n, FNET_W).astype(pf.dtype)

def mla_queries(pq, q_lora_norm, w_uq, q_norm):
    b, n, _ = pq.shape
    cq = rms_norm(pq) * q_lora_norm
    q = (cq @ w_uq).reshape(b, n, MLA_HEADS, QK_DIM)
    return rms_norm(q) * q_norm

def mla_keys_values(pkv, pkr, kv_lora_norm, w_ukv, k_norm):
    b, n, _ = pkv.shape
    ckv = rms_norm(pkv) * kv_lora_norm
    kv = (ckv @ w_ukv).reshape(b, n, MLA_HEADS, QK_NOPE_DIM + V_DIM)
    k_nope, v = kv[..., :QK_NOPE_DIM], kv[..., QK_NOPE_DIM:]
    k_rope = jnp.broadcast_to(pkr[:, :, None, :], (b, n, MLA_HEADS, QK_ROPE_DIM))
    k = rms_norm(jnp.concatenate([k_nope, k_rope], axis=-1)) * k_norm
    return k, v

def block_attention(q, k, v):
    b, n, h, _ = q.shape
    scale = QK_DIM ** -0.5
    qb = jnp.moveaxis(q.reshape(b, n // Q_BLOCK, Q_BLOCK, h, QK_DIM), 1, 0)

    def one_block(qblk):
        s = jnp.einsum('bqhd,bkhd->bhqk', qblk, k).astype(jnp.float32) * scale
        p = jax.nn.softmax(s, axis=-1).astype(v.dtype)
        return jnp.einsum('bhqk,bkhv->bqhv', p, v)

    o = lax.map(one_block, qb)
    return jnp.moveaxis(o, 0, 1).reshape(b, n, h * V_DIM)

def local_head_groups(p, sgu_norm, w_sgu, b_sgu, q_lora_norm, w_uq, q_norm):
    ya = chunk_mlp(p[..., OFF_U:OFF_V], p[..., OFF_V:OFF_F], sgu_norm, w_sgu, b_sgu)
    yb = fourier_mix(p[..., OFF_F:OFF_Q])
    q = mla_queries(p[..., OFF_Q:OFF_KV], q_lora_norm, w_uq, q_norm)
    return ya, yb, q

def expert_choice_moe(h, w_router, w_gate, w_up, w_down):
    b, n, d = h.shape
    cap = EC_FACTOR * n // N_EXPERTS
    aff = jax.nn.softmax(jnp.einsum('bnd,de->bne', h, w_router).astype(jnp.float32), axis=-1)
    g, idx = lax.top_k(jnp.swapaxes(aff, 1, 2), cap)
    xs = jax.vmap(lambda hb, ib: hb[ib])(h, idx)
    hid = jax.nn.silu(jnp.einsum('becd,edf->becf', xs, w_gate)) * jnp.einsum('becd,edf->becf', xs, w_up)
    y = jnp.einsum('becf,efd->becd', hid, w_down) * g[..., None].astype(h.dtype)
    return jax.vmap(lambda yb, ib: jnp.zeros((n, d), h.dtype).at[ib.reshape(-1)].add(yb.reshape(-1, d)))(y, idx)

def second_inputs(seed: int = 0) -> dict:
    key = jax.random.key(seed)
    ks = jax.random.split(key, 22)

    def nrm(k, shape, scale):
        return jax.random.normal(k, shape, jnp.float32) * scale

    return {
        "x": nrm(ks[0], (BATCH, SEQ, D_MODEL), 1.0),
        "c": nrm(ks[1], (BATCH, D_MODEL), 1.0),
        "ctx": nrm(ks[2], (BATCH, CTX_LEN, D_MODEL), 1.0),
        "c_ctx": nrm(ks[3], (D_MODEL,), 1.0),
        "w_ada": nrm(ks[4], (DEPTH, D_MODEL, 6 * D_MODEL), 0.5 * D_MODEL ** -0.5),
        "b_ada": nrm(ks[5], (DEPTH, 6 * D_MODEL), 0.01),
        "w_in": nrm(ks[6], (DEPTH, D_MODEL, IN_W), D_MODEL ** -0.5),
        "sgu_norm": 1.0 + nrm(ks[7], (DEPTH, SGU_W), 0.01),
        "w_sgu": nrm(ks[8], (DEPTH, SGU_HEADS, CHUNK, CHUNK), CHUNK ** -0.5),
        "b_sgu": 1.0 + nrm(ks[9], (DEPTH, SGU_HEADS, CHUNK), 0.01),
        "q_lora_norm": 1.0 + nrm(ks[10], (DEPTH, Q_LORA), 0.01),
        "w_uq": nrm(ks[11], (DEPTH, Q_LORA, MLA_HEADS * QK_DIM), Q_LORA ** -0.5),
        "kv_lora_norm": 1.0 + nrm(ks[12], (DEPTH, KV_LORA), 0.01),
        "w_ukv": nrm(ks[13], (DEPTH, KV_LORA, MLA_HEADS * (QK_NOPE_DIM + V_DIM)), KV_LORA ** -0.5),
        "q_norm": 1.0 + nrm(ks[14], (DEPTH, QK_DIM), 0.01),
        "k_norm": 1.0 + nrm(ks[15], (DEPTH, QK_DIM), 0.01),
        "w_out": nrm(ks[16], (DEPTH, MIX_W, D_MODEL), MIX_W ** -0.5),
        "w_router": nrm(ks[17], (DEPTH, D_MODEL, N_EXPERTS), D_MODEL ** -0.5),
        "w_gate": nrm(ks[18], (DEPTH, N_EXPERTS, D_MODEL, D_EXPERT), D_MODEL ** -0.5),
        "w_up": nrm(ks[19], (DEPTH, N_EXPERTS, D_MODEL, D_EXPERT), D_MODEL ** -0.5),
        "w_down": nrm(ks[20], (DEPTH, N_EXPERTS, D_EXPERT, D_MODEL), D_EXPERT ** -0.5),
    }

def second_block(x, c, ctx, c_ctx, w_ada, b_ada, w_in, sgu_norm, w_sgu, b_sgu, q_lora_norm, w_uq,
              kv_lora_norm, w_ukv, q_norm, k_norm, w_out, w_router, w_gate, w_up, w_down):
    n = x.shape[1]
    rows = n // GRID_W
    pos_row = jnp.repeat(jnp.arange(rows, dtype=jnp.int32), GRID_W)
    pos_col = jnp.tile(jnp.arange(GRID_W, dtype=jnp.int32), rows)
    xc = ctx
    for l in range(DEPTH):
        last = l == DEPTH - 1
        sh1, sc1, g1, sh2, sc2, g2 = ada_modulation(c, w_ada[l], b_ada[l])
        csh1, csc1, cg1, csh2, csc2, cg2 = ada_modulation(c_ctx[None], w_ada[l], b_ada[l])

        hx = modulate_2(x, sh1, sc1)
        hc = modulate_2(xc, csh1, csc1)
        col0 = OFF_KV if last else 0
        pc = hc @ w_in[l][:, col0:]
        k_ctx, v_ctx = mla_keys_values(pc[..., OFF_KV - col0:OFF_KR - col0], pc[..., OFF_KR - col0:],
                                       kv_lora_norm[l], w_ukv[l], k_norm[l])

        px = hx @ w_in[l]
        ya, yb, q = local_head_groups(px, sgu_norm[l], w_sgu[l], b_sgu[l], q_lora_norm[l], w_uq[l], q_norm[l])
        k, v = mla_keys_values(px[..., OFF_KV:OFF_KR], px[..., OFF_KR:], kv_lora_norm[l], w_ukv[l], k_norm[l])
        q = with_rope(q, pos_row, pos_col)
        k = with_rope(k, pos_row, pos_col)
        yc = block_attention(q, jnp.concatenate([k_ctx, k], axis=1), jnp.concatenate([v_ctx, v], axis=1))
        x = x + g1 * (jnp.concatenate([ya, yb, yc], axis=-1) @ w_out[l])

        if not last:
            ya_c, yb_c, q_c = local_head_groups(pc, sgu_norm[l], w_sgu[l], b_sgu[l], q_lora_norm[l], w_uq[l], q_norm[l])
            yc_c = block_attention(q_c, k_ctx, v_ctx)
            xc = xc + cg1 * (jnp.concatenate([ya_c, yb_c, yc_c], axis=-1) @ w_out[l])

        x = x + g2 * expert_choice_moe(modulate_2(x, sh2, sc2), w_router[l], w_gate[l], w_up[l], w_down[l])
        if not last:
            xc = xc + cg2 * expert_choice_moe(modulate_2(xc, csh2, csc2), w_router[l], w_gate[l], w_up[l], w_down[l])
    return x


def setup_inputs(seed=0):
    out = dict(first_inputs(seed))
    for name, value in second_inputs(seed + 1).items():
        if name != "x":
            out[name + "_2"] = value
    return out


def reference(
    x, c, ctx, c_ctx, w_mod, b_mod, ln_g, ln_b, ffn_w_in, ffn_w_out, na_w_qkv, na_w_o, na_rpb,
    wa_w_qkv, wa_w_o, wa_sinks, c_2, ctx_2, c_ctx_2, w_ada_2, b_ada_2, w_in_2, sgu_norm_2,
    w_sgu_2, b_sgu_2, q_lora_norm_2, w_uq_2, kv_lora_norm_2, w_ukv_2, q_norm_2, k_norm_2,
    w_out_2, w_router_2, w_gate_2, w_up_2, w_down_2,
):
    x = first_block(
        x, c, ctx, c_ctx, w_mod, b_mod, ln_g, ln_b, ffn_w_in, ffn_w_out, na_w_qkv, na_w_o,
        na_rpb, wa_w_qkv, wa_w_o, wa_sinks,
    )
    return second_block(
        x, c_2, ctx_2, c_ctx_2, w_ada_2, b_ada_2, w_in_2, sgu_norm_2, w_sgu_2, b_sgu_2,
        q_lora_norm_2, w_uq_2, kv_lora_norm_2, w_ukv_2, q_norm_2, k_norm_2, w_out_2, w_router_2,
        w_gate_2, w_up_2, w_down_2,
    )


_drawn_inputs = setup_inputs


def setup_inputs(seed=0):
    import zlib

    import numpy as np

    out = dict(_drawn_inputs(seed))
    spreads = {}
    factors = {'ctx': 3.528,
     'b_mod': 7.356,
     'na_rpb': 8.0,
     'wa_sinks': 8.0,
     'ctx_2': 3.392,
     'b_ada_2': 4.233,
     'sgu_norm_2': 8.0,
     'b_sgu_2': 8.0,
     'q_lora_norm_2': 8.0,
     'kv_lora_norm_2': 8.0,
     'q_norm_2': 8.0,
     'k_norm_2': 8.0}
    for name, (base, spread) in spreads.items():
        noise = np.random.default_rng([zlib.crc32(name.encode()), seed]).standard_normal(out[name].shape)
        drawn = base * np.exp(spread * noise) if base else spread * noise
        out[name] = __import__('jax').numpy.asarray(drawn.astype(out[name].dtype))
    for name, factor in factors.items():
        out[name] = (out[name] * factor).astype(out[name].dtype)
    return out
```

```python
from contextlib import ExitStack, contextmanager

import numpy as np
import concourse.bass as bass
from concourse import mybir

F32 = mybir.dt.float32
F32R = mybir.dt.float32r
ALU = mybir.AluOpType
ACT = mybir.ActivationFunctionType
AXX = mybir.AxisListType.X
ds = bass.ds

P = 128
D = 1024
KD = D // P
S = 256
C = 256
T = S + C
LAT, CTX = slice(0, S), slice(S, T)
GROUPS = (LAT, CTX)
DEPTH = 2
FF = 2816
FT = FF // P
HALVES = ((0, 12), (12, 10))
GRID_W = 64
ROWS = S // GRID_W
HEADS = 16
HD = 64
NA_KH, NA_KW = 8, 16
RPB_PAD = 48
RPB_W = 2 * NA_KW - 1 + 2 * RPB_PAD
ALPHA = float((2 * DEPTH) ** 0.25)
LN_EPS, RMS_EPS = 1e-5, 1e-6
NEG = -1e30
RING = 4
AHEAD = 3
UNIT = 1024

IN_W = 1216
N_EXP = 16
CAP = 32
D_EXP = 512
QK_NOPE, QK_ROPE = 128, 64
MLA_HEADS = 4
QK_DIM = QK_NOPE + QK_ROPE


def table_layout():
    at, out = 0, {}
    for name, width in (("ident", P), ("mean_d", P), ("mean_256", P), ("mean_128", P), ("mean_192", P),
                        ("half0", P), ("half1", P), ("ones", P), ("rot", P), ("flip", P), ("cos", S),
                        ("sin", S), ("na_mask", GRID_W), ("wa_mask", 2 * S), ("dft_d", 2 * P),
                        ("dft_n", 4 * S), ("slots", CAP)):
        out[name] = (at, width)
        at += width
    return out, at


def make_tables():
    lay, width = table_layout()
    t = np.zeros((P, width), np.float32)

    def put(name, a):
        at, w = lay[name]
        t[:, at:at + w] = a

    p = np.arange(P)
    put("ident", np.eye(P))
    put("ones", 1.0)
    for name, n in (("mean_d", D), ("mean_256", 256), ("mean_128", 128), ("mean_192", QK_DIM)):
        put(name, 1.0 / n)
    for e in range(2):
        put(f"half{e}", np.repeat((p // HD == e)[:, None] / QK_DIM, P, 1))
    rot = np.zeros((P, P))
    for i in range(P):
        if i % 32 < 16:
            rot[i + 16, i] = -1.0
        else:
            rot[i - 16, i] = 1.0
    put("rot", rot)
    flip = np.zeros((P, P))
    flip[p, (p // GRID_W) * GRID_W + GRID_W - 1 - p % GRID_W] = 1.0
    put("flip", flip)
    tok = np.arange(S)
    freq = 10000.0 ** (-(p % 16) / 16.0)
    pos = np.where((p % HD < 32)[:, None], (tok // GRID_W)[None, :], (tok % GRID_W)[None, :])
    put("cos", np.cos(pos * freq[:, None]))
    put("sin", np.sin(pos * freq[:, None]))
    qc = GRID_W - 1 - p % GRID_W
    start = np.clip(qc - NA_KW // 2, 0, GRID_W - NA_KW)
    kc = np.arange(GRID_W)
    put("na_mask", np.where((kc >= start[:, None]) & (kc < start[:, None] + NA_KW), 0.0, NEG))
    put("wa_mask", np.concatenate([np.where(np.abs(i * P + p[:, None] - tok) <= 128, 0.0, NEG) for i in range(2)], 1))
    d = np.arange(HD)
    ang = 2 * np.pi * np.outer(d, d) / HD
    blk = np.zeros((P, 2 * P))
    for g in range(2):
        blk[g * HD:(g + 1) * HD, g * HD:(g + 1) * HD] = np.cos(ang) / 8
        blk[g * HD:(g + 1) * HD, P + g * HD:P + (g + 1) * HD] = -np.sin(ang) / 8
    put("dft_d", blk)
    ang = 2 * np.pi * ((tok[:, None] * tok[None, :]) % S) / S
    cs = np.stack([np.cos(ang), np.sin(ang)], 0) / 16
    put("dft_n", cs.reshape(2, 2, P, S).transpose(2, 0, 1, 3).reshape(P, 4 * S))
    put("slots", np.arange(CAP)[None, :])
    return t


VEC_TILES = (
    (("b_mod0", 72), ("c", 8), ("c_ctx", 8), ("c_2", 8), ("c_ctx_2", 8)),
    (("b_mod1", 72), ("sgu", 4), ("qlora", 4), ("kvlora", 2)),
    (("b_ada", 96), ("qn", 2), ("kn", 2), ("qr", 2), ("kr", 2)),
    (("ln_g", 48), ("ln_b", 48)),
)
VEC = {}
for _i, _tile in enumerate(VEC_TILES):
    _row = 0
    for _name, _n in _tile:
        VEC[_name] = (_i, _row, _n)
        _row += _n


class Counts:

    def __init__(self, sems, start=()):
        self.sems, self.n, self.var, self.last = sems, dict(start), {}, None

    def sem(self, key):
        return self.sems[key.split(":")[0]]

    def value(self, key, more=0):
        return self.n.get(key, 0) + self.var.get(key, 0) + more

    def next(self, key, k=1):
        self.n[key] = self.n.get(key, 0) + k
        return self.sem(key), self.value(key)

    def peek(self, key, more=0):
        return self.sem(key), self.value(key, more)

    def filled(self, b):
        return self.sems[f"bank_ready{b}"], self.value(f"bank_read{b}")

    def mark(self, key, k=1):
        self.last = self.next(key, k)
        return self.last[0], k

    @contextmanager
    def loop(self, eng, reps, strides):
        self.settle(eng)
        before = dict(self.n)
        with eng.Fori(0, reps) as i:
            self.var = {key: i * k for key, k in strides.items()}
            yield i
            self.settle(eng)
        self.var = {}
        for key, n in self.n.items():
            grown = n - before.get(key, 0)
            assert grown == strides.get(key, 0), (key, grown)
            self.n[key] = before.get(key, 0) + grown * reps

    def settle(self, eng):
        if self.last is not None:
            eng.wait_ge(*self.last)
        self.last = None


SEMS = (
    [f"raw_full{r}" for r in range(RING)]
    + ["hi_ready", "split_ready", "units_done"]
    + [f"bank_ready{b}" for b in range(8)]
    + [f"bank_read{b}" for b in range(8)]
    + ["act", "dve", "pe_passed", "act_passed",
       "zeroed", "inputs_loaded", "vec_ready", "cs_ready", "cond_ready", "mod_ready",
       "out_ready", "hm_ready", "xhi_ready", "x_ready", "hidden_ready", "h_ready",
       "centered", "squared", "max_ready", "p_ready", "ao_hi", "stored",
       "bias_loaded", "bias_ready", "sink_ready", "sink_exp",
       "small_loaded", "ctx_loaded", "moe_in_ready", "norm_ready", "q_ready", "ya_ready", "logits_moved", "softmax_in", "softmax_exp",
       "slots_ready", "slots_used", "est_hi", "est_ready", "gate_low", "gate_in", "gate_ready", "up_low", "hid_ready", "hidT_hi",
       "y_low", "y_stored", "y_free", "y_loaded"]
)



N_LOADS = DEPTH + 4 + 2 + 1 + 2 + 1 + 6 + 4


def build(nc, a, out):
    lay, _ = table_layout()
    base = (nc.sbuf_base + 31) // 32 * 32
    top = [base]

    def at(name, shape, dt, offset):
        return nc.alloc_sbuf_tensor_at(name, shape, dt, offset=offset)

    def new(name, shape, dt=F32):
        t = at(name, shape, dt, top[0])
        top[0] += 4 * int(np.prod(shape[1:]))
        assert top[0] <= nc.sbuf_usable_end, (name, top[0], nc.sbuf_usable_end)
        return t

    raw = new("raw", [P, RING, UNIT])
    whi = new("whi", [P, RING, UNIT], F32R)
    wlo = new("wlo", [P, RING, UNIT], F32R)
    h = new("h", [P, KD, T])
    xin_at = top[0]
    xhi = new("xhi", [P, KD, T], F32R)
    xlo = new("xlo", [P, KD, T], F32R)
    big = top[0]
    top[0] += 64 * 1024
    tables = new("tables", [P, table_layout()[1]])
    vec = new("vec", [P, 4, P])
    mod = new("mod", [P, 72, 2])
    cs = new("cs", [P, KD, 2])
    cond = new("cond", [P, KD, P], F32R)
    tmp = new("tmp", [P, 4, T])
    mrow = tmp[:, 0, :]
    mt = new("mt", [P, 16])
    small = new("small", [P, 64])
    eps_ln, eps_rms = small[:, 61:62], small[:, 62:63]
    sinks, nsinks = small[:, 8:24], small[:, 24:40]
    KB = 1024
    vrow = at("vrow", [P, 4, P], F32, big)
    xtok = at("xtok", [P, 4, D], F32, big + 2 * KB)
    hhi = at("hhi", [P, 12, T], F32R, big)
    hlo = at("hlo", [P, 12, T], F32R, big + 24 * KB)
    hm = at("hm", [P, KD, T], F32, big + 48 * KB)
    aohi = at("aohi", [P, KD, T], F32R, big)
    aolo = at("aolo", [P, KD, T], F32R, big + 16 * KB)
    qS = at("qS", [P, 2, T], F32, big + 32 * KB)
    kS = at("kS", [P, T], F32, big + 36 * KB)
    vF = at("vF", [P, T], F32, big + 38 * KB)
    vS = at("vS", [P, 4, P], F32, big + 40 * KB)
    bt = at("bt", [P, 2, 2, S], F32, big + 42 * KB)
    prob = at("prob", [P, 2, T], F32, big + 46 * KB)
    pT = at("pT", [P, 2, 4, S], F32, big + 50 * KB)
    outT = at("outT", [P, 2, D], F32, big)
    px = at("px", [P, 10, T], F32, big)
    vtok = at("vtok", [P, 4, 2 * P], F32, big + 20 * KB)
    fd = at("fd", [P, 4, 4 * P], F32, big + 24 * KB)
    wsT = at("wsT", [P, 4, P], F32, big + 32 * KB)
    qn = at("qn", [P, 4, T], F32, big + 20 * KB)
    qr = at("qr", [P, 2, T], F32, big + 28 * KB)
    kn = at("kn", [P, 4, T], F32, big + 32 * KB)
    kr = at("kr", [P, 2, T], F32, big + 40 * KB)
    vt = at("vt", [P, 4, T], F32, big + 44 * KB)
    sq = at("sq", [P, 6, T], F32, big + 52 * KB)
    prob2 = at("prob2", [P, 2, T], F32, big + 52 * KB)
    pT2 = at("pT2", [P, 2, 4, S], F32, big + 56 * KB)
    xsT = at("xsT", [P, KD, N_EXP, 2 * CAP], F32, big)
    est = at("est", [P, KD, P], F32R, big + 32 * KB)
    hidT = at("hidT", [P, 4, P], F32R, big + 36 * KB)
    hid = at("hid", [P, D_EXP], F32, big + 38 * KB)
    ysb = at("ysb", [P, D], F32, big + 40 * KB)
    htok = at("htok", [P, 4, D], F32, xin_at)
    oh = at("oh", [P, 4, N_EXP, CAP], F32, xin_at + 16 * KB)
    ohw = at("ohw", [P, 4, N_EXP * CAP], F32, xin_at + 24 * KB)
    yp = at("yp", [P, 2, 4, D], F32, xin_at)
    small_at = top[0]
    wuq = new("wuq", [P, 2, 768])
    wukv = new("wukv", [P, D])
    wsgu = new("wsgu", [P, 4, P])
    bsgu = new("bsgu", [P, 4 * P])
    wr = new("wr", [P, KD, N_EXP])
    st = at("st", [P, 2, 4, S], F32, small_at)
    aff = new("aff", [P, 4, N_EXP])
    pos = new("pos", [P, 4, N_EXP])
    top8 = new("top8", [P, 8])
    yscr = nc.dram_tensor("y_scratch", (N_EXP, 2 * CAP, D), F32, kind="Internal").ap()

    def tab(name, *cols):
        at0, w = lay[name]
        return tables[:, at0:at0 + w] if not cols else tables[:, at0 + cols[0]:at0 + cols[1]]

    def v(name, i=0, n=None):
        tile, row, cnt = VEC[name]
        return vec[:, tile, row + i:row + i + (cnt - i if n is None else n)]

    def mcol(j, k, g):
        return mod[:, j * KD + k, g:g + 1]

    SHIFT1, SCALE1, GATE1, SHIFT2, SCALE2, GATE2, SHIFT3, SCALE3, GATE3 = range(9)

    with ExitStack() as ctx:
        s = {name: ctx.enter_context(nc.semaphore(name)) for name in SEMS}
        bank = [ctx.enter_context(nc.psum_tensor(f"bank{b}", [P, T], F32)) for b in range(8)]
        block = ctx.enter_context(nc.Block())
        BANKS = {f"bank_read{b}": 1 for b in range(8)}

        def heads_pair_plan(wa):
            items, pvs, outs = [], {}, {}
            group = 0
            for qq in range(2 if wa else 1):
                for e in range(2):
                    rows = slice(e * HD, (e + 1) * HD)
                    for g in range(1 if wa else 2):
                        for tt in range(2):
                            t = 2 * g + tt
                            items.append(dict(
                                nk=4 if g == 0 else 2, key0=0 if g == 0 else S,
                                ops=[(qS[rows, qq, t * P:(t + 1) * P], kS[rows, 0 if g == 0 else S:T])],
                                bias=(None if g else (tab("ident"), tab("wa_mask", tt * S, (tt + 1) * S)) if wa
                                      else (tab("flip"), bt[:, e, tt, :])),
                                wait_bias=(not wa and tt == 0), pg=group % 2, tt=tt, qhead=2 * qq + e, sink=wa))
                        m = len(items) - 1
                        v0 = 0 if g == 0 else 2
                        cols = slice(g * S, (g + 1) * S)
                        vc = slice(0, HD) if wa else rows
                        pvs.setdefault(m + 1, []).append(dict(
                            nk=items[-1]["nk"], pg=group % 2, v0=v0, vc=vc, out=(rows, cols),
                            new=(e == 0 and g == 0), done=(e == 1 and g == (0 if wa else 1))))
                        group += 1
                outs.setdefault(len(items), []).append(qq)
            n = len(items)
            last = {k: x for k, x in pvs.items() if k >= n}
            for k, x in last.items():
                pvs.setdefault(n - 1, []).extend(pvs.pop(k))
            last = {k: x for k, x in outs.items() if k >= n}
            for k in last:
                outs.setdefault(n - 1, []).extend(outs.pop(k))
            return items, pvs, outs, (LAT if wa else slice(0, T))

        def mla_plan(ctx_too):
            items, pvs, outs = [], {}, {}
            group = 0
            for hh in range(MLA_HEADS):
                rows = slice(hh % 2 * HD, hh % 2 * HD + HD)
                for g in range(2 if ctx_too else 1):
                    for tt in range(2):
                        q = slice((2 * g + tt) * P, (2 * g + tt + 1) * P)
                        keys = slice(0 if g == 0 else S, T)
                        items.append(dict(
                            nk=4 if g == 0 else 2, bias=None, wait_bias=False, pg=group % 2, tt=tt, sink=False,
                            ops=[(qn[:, hh, q], kn[:, hh, keys]), (qr[rows, hh // 2, q], kr[rows, hh // 2, keys])]))
                    pvs.setdefault(len(items), []).append(dict(
                        nk=items[-1]["nk"], pg=group % 2, v0=0 if g == 0 else 2, vc=slice(hh * P, (hh + 1) * P),
                        out=(slice(0, P), slice(g * S, (g + 1) * S)), new=(g == 0), done=(g == 1 or not ctx_too)))
                    group += 1
                outs.setdefault(len(items), []).append(hh)
            last = len(items) - 1
            for by_step in (pvs, outs):
                by_step.setdefault(last, []).extend(by_step.pop(last + 1, []))
            return items, pvs, outs, (slice(0, T) if ctx_too else LAT)

        NA, WA = heads_pair_plan(False), heads_pair_plan(True)
        BLOCK1 = (prob, pT, vS, aohi, aolo)
        BLOCK2 = (prob2, pT2, vt, xhi, xlo)

        @block.sync
        def _(sp):
            n = Counts(s)
            unit_no = [0]

            def unit(src, width):
                slot = unit_no[0] % RING
                unit_no[0] += 1
                sp.wait_ge(*n.next("split_ready"))
                kt, cols = src.shape[1], src.shape[2]
                dst = raw[:, slot, 0:kt * cols].rearrange("p (k c) -> p k c", k=kt)
                sp.dma_start(dst, src).then_inc(s[f"raw_full{slot}"], 16)

            def mods(w, nblocks):
                view = w.rearrange("(q k p) n -> q p k n", k=2, p=P)
                with n.loop(sp, nblocks, dict(split_ready=4)) as i:
                    for q in range(4):
                        unit(view[q][:, :, ds(i * 512, 512)], 1024)

            def up_down(w_in, w_out):
                wi = w_in.rearrange("(k p) n -> p k n", p=P)
                wo = w_out.rearrange("(k p) n -> p k n", p=P)
                for f0, nf in HALVES:
                    with n.loop(sp, nf // 2, dict(split_ready=4)) as i:
                        for f in range(2):
                            for part in range(2):
                                unit(wi[:, :, ds(i * 256 + ((f0 + f) * P + part * FF), P)], 1024)
                    k = nf // 2
                    with n.loop(sp, KD // 2, dict(split_ready=4)) as i:
                        for d in range(2):
                            for part in range(2):
                                k0 = f0 + part * k
                                unit(wo[:, k0:k0 + k, ds(i * 256 + d * P, P)], k * P)

            def columns(w, tiles):
                view = w.rearrange("(k p) n -> p k n", p=P)
                with n.loop(sp, tiles // 4, dict(split_ready=4)) as i:
                    for j in range(4):
                        unit(view[:, :, ds(i * 512 + j * P, P)], 1024)

            sp.wait_ge(*n.next("zeroed"))
            for l in range(DEPTH):
                b = a["b_mod"][l].rearrange("(r c) -> r c", c=P)
                tile, row, cnt = VEC[f"b_mod{l}"]
                sp.dma_start(vrow[row:row + cnt, tile, :], b).then_inc(s["inputs_loaded"], 16)
            for name in ("c", "c_ctx", "c_2", "c_ctx_2"):
                tile, row, cnt = VEC[name]
                src = a[name] if name in ("c_ctx", "c_ctx_2") else a[name][0]
                sp.dma_start(vrow[row:row + cnt, tile, :], src.rearrange("(r c) -> r c", c=P)).then_inc(s["inputs_loaded"], 16)
            for name, src in (("b_ada", a["b_ada_2"].rearrange("l (r c) -> (l r) c", c=P)), ("sgu", a["sgu_norm_2"].rearrange("l (r c) -> (l r) c", c=P)),
                              ("qlora", a["q_lora_norm_2"].rearrange("l (r c) -> (l r) c", c=P)), ("kvlora", a["kv_lora_norm_2"]),
                              ("qn", a["q_norm_2"][:, 0:P]), ("kn", a["k_norm_2"][:, 0:P])):
                tile, row, cnt = VEC[name]
                sp.dma_start(vrow[row:row + cnt, tile, :], src).then_inc(s["inputs_loaded"], 16)
            for name, src in (("qr", a["q_norm_2"][:, P:QK_DIM]), ("kr", a["k_norm_2"][:, P:QK_DIM])):
                tile, row, cnt = VEC[name]
                for e in range(2):
                    sp.dma_start(vrow[row:row + cnt, tile, e * HD:(e + 1) * HD], src).then_inc(s["inputs_loaded"], 16)
            for name in ("ln_g", "ln_b"):
                tile, row, cnt = VEC[name]
                sp.dma_start(vrow[row:row + cnt, tile, :], a[name].rearrange("l j (r c) -> (l j r) c", c=P)).then_inc(s["inputs_loaded"], 16)
            sp.dma_start(sinks, a["wa_sinks"][0].unsqueeze(0).broadcast_to([P, HEADS])).then_inc(s["inputs_loaded"], 16)
            sp.dma_start(tables[:, :], a["tables"]).then_inc(s["inputs_loaded"], 16)
            for g, name in enumerate(("x", "ctx")):
                sp.dma_start(xtok[:, 2 * g:2 * g + 2, :],
                             a[name][0].rearrange("(t p) d -> p t d", p=P)).then_inc(s["inputs_loaded"], 16)

            for l in range(DEPTH):
                mods(a["w_mod"][l], 18)
                up_down(a["ffn_w_in"][l, 0], a["ffn_w_out"][l, 0])
                if l == 0:
                    w = a["na_w_qkv"][0].rearrange("(k p) n -> p k n", p=P)
                    with n.loop(sp, 2, dict(split_ready=12)) as i:
                        for j in range(4):
                            for part in range(3):
                                unit(w[:, :, ds(i * 512 + (j * P + part * D), P)], 1024)
                    columns(a["na_w_o"][0], KD)
                else:
                    w = a["wa_w_qkv"][0].rearrange("(k p) n -> p k n", p=P)
                    kv = a["wa_kv"].rearrange("(k p) n -> p k n", p=P)
                    with n.loop(sp, 4, dict(split_ready=4)) as i:
                        for part in range(2):
                            unit(kv[:, :, ds(i * 256 + part * P, P)], 1024)
                        for q in range(2):
                            unit(w[:, :, ds(i * 256 + q * P, P)], 1024)
                    columns(a["wa_w_o"][0], KD)
                up_down(a["ffn_w_in"][l, 1], a["ffn_w_out"][l, 1])
            for l in range(DEPTH):
                mods(a["w_ada_2"][l], 12)
                w = a["w_in_2"][l].rearrange("(k p) n -> p k n", p=P)
                for j in range(9):
                    unit(w[:, :, j * P:(j + 1) * P], 1024)
                unit(a["w_kr"][l].rearrange("(k p) n -> p k n", p=P), 1024)
                columns(a["w_out_2"][l], KD)
                wg, wu = (a[x][l].rearrange("e r f -> (e r) f") for x in ("w_gate_2", "w_up_2"))
                wd = a["w_down_2"][l].rearrange("e (k p) d -> k p e d", p=P)
                with n.loop(sp, N_EXP, dict(split_ready=12)) as i:
                    for view in (wg, wu):
                        for q in range(4):
                            unit(view[ds(i * D + q * 2 * P, 2 * P), :].rearrange("(k p) f -> p k f", p=P), 1024)
                    for k in range(4):
                        unit(wd[k][:, ds(i, 1), :], 1024)
            sp.wait_ge(*n.next("out_ready"))
            sp.dma_start(out[0].rearrange("(t p) d -> p t d", p=P), outT[:, :, :]).then_inc(s["stored"], 16)
            sp.wait_ge(*n.next("stored", 16))

        @block.tensor
        def _(pe):
            n = Counts(s, {"split_ready:use": RING})
            use_no = [0]
            pe.sem_inc(s["units_done"], RING)
            for b in range(8):
                pe.sem_inc(s[f"bank_read{b}"], 1)

            def acquire(b):
                pe.wait_ge(*n.next(f"bank_read{b}:free"))

            def evacuated(b):
                pe.wait_ge(*n.peek(f"bank_read{b}:free", 1))

            def passed():
                pe.sem_inc(s["pe_passed"], 1)

            def unit():
                slot = use_no[0] % RING
                use_no[0] += 1
                pe.wait_ge(*n.next("split_ready:use"))
                return slot

            def mods(nblocks):
                loop = {"split_ready:use": 4, "bank_read0:free": 1, "bank_read4:free": 1}
                with n.loop(pe, nblocks, loop):
                    acquire(0)
                    for q in range(4):
                        slot = unit()
                        for kk in range(2):
                            for part, w in enumerate((whi, wlo)):
                                mm = pe.matmul(bank[0][:, :], cond[:, 2 * q + kk, :], w[:, slot, kk * 512:(kk + 1) * 512],
                                               start=(q + kk + part == 0), stop=(q == 3 and kk == 1 and part == 1))
                        mm.then_inc(s["units_done"], 1)
                    acquire(4)
                    evacuated(0)
                    passed()
                    for j in range(4):
                        mm = pe.transpose(bank[4][:, 4 * j:4 * j + 4], mrow[0:4, j * P:(j + 1) * P], tab("ident")[0:4, 0:4])
                    mm.then_inc(s["bank_ready4"], 1)

            def product(b, slot, kt, k0, hi, lo, cols, first, last, x_wait=False):
                for k in range(kt):
                    if x_wait:
                        pe.wait_ge(*n.next("x_ready"))
                    wh, wl = (w[:, slot, k * P:(k + 1) * P] for w in (whi, wlo))
                    o = bank[b][:, cols]
                    pe.matmul(o, wh, hi[:, k0 + k, cols], start=(first and k == 0), stop=False)
                    pe.matmul(o, wh, lo[:, k0 + k, cols], start=False, stop=False)
                    mm = pe.matmul(o, wl, hi[:, k0 + k, cols], start=False, stop=(last and k == kt - 1))
                mm.then_inc(s["units_done"], 1)

            def up_down(cols):
                for k in range(KD):
                    pe.wait_ge(*n.next("x_ready"))
                for half, (f0, nf) in enumerate(HALVES):
                    loop = {"split_ready:use": 4, **{f"bank_read{b}:free": 1 for b in range(4)}}
                    with n.loop(pe, nf // 2, loop):
                        for b in range(4):
                            acquire(b)
                            product(b, unit(), KD, 0, xhi, xlo, cols, True, True)
                    pe.wait_ge(*n.next("hidden_ready", nf))
                    with n.loop(pe, KD // 2, {"split_ready:use": 4, "bank_read0:free": 1, "bank_read1:free": 1}):
                        for b in range(2):
                            acquire(b)
                            for part in range(2):
                                product(b, unit(), nf // 2, part * (nf // 2), hhi, hlo, cols, part == 0, part == 1)

            def layer_norm(cols):
                pe.wait_ge(*n.next("h_ready"))
                acquire(4)
                for k in range(KD):
                    mm = pe.matmul(bank[4][:, cols], tab("mean_d"), h[:, k, cols], start=(k == 0), stop=(k == KD - 1))
                mm.then_inc(s["bank_ready4"], 1)
                acquire(5)
                for k in range(KD):
                    pe.wait_ge(*n.next("squared"))
                    mm = pe.matmul(bank[5][:, cols], tab("mean_d"), hm[:, k, cols], start=(k == 0), stop=(k == KD - 1))
                mm.then_inc(s["bank_ready5"], 1)

            def attend(plan, where=BLOCK1, out_bank=7):
                items, pvs, outs, out_cols = plan
                prob, pT, values, out_hi, out_lo = where

                def score(m):
                    it = items[m]
                    b = 4 + m % 2
                    acquire(b)
                    nk = it["nk"] * P
                    ops = it["ops"]
                    for j, (lhs, rhs) in enumerate(ops):
                        mm = pe.matmul(bank[b][:, 0:nk], lhs, rhs, start=(j == 0), stop=(j == len(ops) - 1 and it["bias"] is None))
                    if it["bias"] is not None:
                        if it["wait_bias"]:
                            pe.wait_ge(*n.next("bias_ready"))
                        mm = pe.matmul(bank[b][:, 0:S], it["bias"][0], it["bias"][1], start=False, stop=True)
                    mm.then_inc(s[f"bank_ready{b}"], 1)

                score(0)
                score(1)
                for m, it in enumerate(items):
                    pe.wait_ge(*n.next("p_ready"))
                    acquire(6)
                    for kt in range(it["nk"]):
                        mm = pe.transpose(bank[6][:, kt * P:(kt + 1) * P], prob[:, m % 2, kt * P:(kt + 1) * P], tab("ident"))
                    mm.then_inc(s["bank_ready6"], 1)
                    if m + 2 < len(items):
                        score(m + 2)
                    for pv in pvs.get(m, ()):
                        if m == len(items) - 1:
                            evacuated(6)
                        if pv["new"]:
                            acquire(out_bank)
                        rows, cols = pv["out"]
                        for kt in range(pv["nk"]):
                            mm = pe.matmul(bank[out_bank][rows, cols], values[:, pv["v0"] + kt, pv["vc"]], pT[:, pv["pg"], kt, :],
                                           start=(kt == 0), stop=(kt == pv["nk"] - 1), skip_group_check=True)
                        if pv["done"]:
                            mm.then_inc(s[f"bank_ready{out_bank}"], 1)

            def out_projection(cols):
                evacuated(7)
                with n.loop(pe, 2, {"split_ready:use": 4, **{f"bank_read{b}:free": 1 for b in range(4)}}):
                    for b in range(4):
                        acquire(b)
                        product(b, unit(), KD, 0, aohi, aolo, cols, True, True)

            pe.wait_ge(*n.next("inputs_loaded", N_LOADS * 16))
            acquire(4)
            for j in range(4):
                mm = pe.transpose(bank[4][:, j * P:(j + 1) * P], vrow[:, j, :], tab("ident"))
            mm.then_inc(s["bank_ready4"], 1)
            for k in range(KD):
                b = 5 + k % 2
                acquire(b)
                for t in range(4):
                    mm = pe.transpose(bank[b][:, t * P:(t + 1) * P], xtok[:, t, k * P:(k + 1) * P], tab("ident"))
                mm.then_inc(s[f"bank_ready{b}"], 1)
            pe.wait_ge(*n.next("cond_ready"))

            for l in range(DEPTH):
                ctx_too = l < DEPTH - 1
                cols = slice(0, T) if ctx_too else LAT
                mods(18)
                up_down(slice(0, T))
                layer_norm(slice(0, T))
                for k in range(KD):
                    pe.wait_ge(*n.next("x_ready"))
                if l == 0:
                    loop = {"split_ready:use": 12, "bank_read0:free": 4, "bank_read1:free": 4, "bank_read2:free": 4,
                            "bank_read4:free": 16, "bank_read5:free": 16, "bank_read6:free": 36,
                            "bank_read7:free": 4, "p_ready": 32, "bias_ready": 8}
                    with n.loop(pe, 2, loop):
                        for f in range(4):
                            for b in range(3):
                                acquire(b)
                                product(b, unit(), KD, 0, xhi, xlo, slice(0, T), True, True)
                            evacuated(2)
                            acquire(6)
                            for t in range(4):
                                mm = pe.transpose(bank[6][:, t * P:(t + 1) * P], vF[:, t * P:(t + 1) * P], tab("ident"))
                            mm.then_inc(s["bank_ready6"], 1)
                            for b in (0, 1, 6):
                                evacuated(b)
                            attend(NA)
                else:
                    loop = {"split_ready:use": 4, "bank_read0:free": 1, "bank_read1:free": 1, "bank_read2:free": 1,
                            "bank_read3:free": 1, "bank_read4:free": 4 + 2, "bank_read5:free": 4 + 1, "bank_read6:free": 8 + 1,
                            "bank_read7:free": 2, "p_ready": 8, "q_ready": 3}
                    with n.loop(pe, 4, loop):
                        for b in range(4):
                            acquire(b)
                            c = slice(0, T) if b < 2 else LAT
                            product(b, unit(), KD, 0, xhi, xlo, c, True, True)
                        evacuated(1)
                        acquire(6)
                        passed()
                        for t in range(4):
                            mm = pe.transpose(bank[6][:, t * P:t * P + HD], vF[0:HD, t * P:(t + 1) * P], tab("ident")[0:HD, 0:HD])
                        mm.then_inc(s["bank_ready6"], 1)
                        for j, (b, x) in enumerate(((0, kS[:, LAT]), (2, qS[:, 0, LAT]), (3, qS[:, 1, LAT]))):
                            evacuated(b)
                            rb = 4 + j % 2
                            acquire(rb)
                            pe.matmul(bank[rb][:, LAT], tab("rot"), x, start=True, stop=True).then_inc(s[f"bank_ready{rb}"], 1)
                        pe.wait_ge(*n.next("q_ready", 3))
                        pe.wait_ge(*n.peek("bank_read6:free", 1))
                        attend(WA)
                out_projection(cols)
                layer_norm(cols)
                up_down(cols)
                layer_norm(cols)

            def small_product(b, pairs, o=slice(0, T), rows=slice(0, P), acq=True, ready=True):
                if acq:
                    acquire(b)
                for j, (lhs, rhs) in enumerate(pairs):
                    mm = pe.matmul(bank[b][rows, o], lhs, rhs, start=(j == 0), stop=(j == len(pairs) - 1), skip_group_check=True)
                if ready:
                    mm.then_inc(s[f"bank_ready{b}"], 1)

            def rms_stat(cols):
                acquire(5)
                for k in range(KD):
                    pe.wait_ge(*n.next("squared"))
                    mm = pe.matmul(bank[5][:, cols], tab("mean_d"), hm[:, k, cols], start=(k == 0), stop=(k == KD - 1))
                mm.then_inc(s["bank_ready5"], 1)

            pe.wait_ge(*n.next("ctx_loaded", 16))
            for k in range(KD):
                b = 4 + k % 2
                acquire(b)
                for t in range(2):
                    mm = pe.transpose(bank[b][:, t * P:(t + 1) * P], xtok[:, t, k * P:(k + 1) * P], tab("ident"))
                mm.then_inc(s[f"bank_ready{b}"], 1)
            pe.wait_ge(*n.next("cond_ready"))
            for l in range(DEPTH):
                ctx_too = l < DEPTH - 1
                cols = slice(0, T) if ctx_too else LAT
                tts = range(4 if ctx_too else 2)
                mods(12)
                rms_stat(slice(0, T))
                for k in range(KD):
                    pe.wait_ge(*n.next("x_ready"))
                for j in range(10):
                    acquire(j % 4)
                    product(j % 4, unit(), KD, 0, xhi, xlo, cols if j < 8 else slice(0, T), True, True)
                pe.wait_ge(*n.next("small_loaded", 5 * 16))
                for b, tiles, m in ((4, 2, "mean_256"), (5, 2, "mean_256"), (6, 1, "mean_128")):
                    c = slice(0, T) if b == 6 else cols
                    acquire(b)
                    for j in range(tiles):
                        pe.wait_ge(*n.next("squared"))
                        mm = pe.matmul(bank[b][:, c], tab(m), sq[:, 2 * (b - 4) + j, c], start=(j == 0), stop=(j == tiles - 1))
                    mm.then_inc(s[f"bank_ready{b}"], 1)
                acquire(7)
                for hh in range(4):
                    mm = pe.transpose(bank[7][:, hh * P:(hh + 1) * P], wsgu[:, hh, :], tab("ident"))
                mm.then_inc(s["bank_ready7"], 1)
                pe.wait_ge(*n.next("norm_ready", 5))
                for tt in tts:
                    b = 4 + tt % 2
                    acquire(b)
                    for i in range(2):
                        mm = pe.transpose(bank[b][:, i * P:(i + 1) * P], px[:, 2 + i, tt * P:(tt + 1) * P], tab("ident"))
                    mm.then_inc(s[f"bank_ready{b}"], 1)
                evacuated(7)
                for tt in tts:
                    b = 4 + tt % 2
                    acquire(b)
                    if tt == 0:
                        evacuated(5)
                    for i in range(2):
                        o = bank[b][:, i * S:(i + 1) * S]
                        pe.matmul(o, vtok[:, tt, i * P:(i + 1) * P], wsT[:, 2 * i:2 * i + 2, :], start=True, stop=False, skip_group_check=True)
                        mm = pe.matmul(o, tab("ones")[0:1, :], bsgu[0:1, i * S:(i + 1) * S], start=False, stop=True, skip_group_check=True)
                    mm.then_inc(s[f"bank_ready{b}"], 1)
                for tt in tts:
                    b = 6 + tt % 2
                    acquire(b)
                    for i in range(2):
                        mm = pe.matmul(bank[b][:, i * S:(i + 1) * S], px[:, 4 + i, tt * P:(tt + 1) * P], tab("dft_d"),
                                       start=True, stop=True, skip_group_check=True)
                    mm.then_inc(s[f"bank_ready{b}"], 1)
                evacuated(6)
                evacuated(7)
                for i in range(2):
                    b = 4 + i
                    acquire(b)
                    for g in range(len(tts) // 2):
                        for part in range(2):
                            for t in range(2):
                                mm = pe.matmul(bank[b][:, g * S:(g + 1) * S], fd[:, 2 * g + t, i * S + part * P:i * S + (part + 1) * P],
                                               tab("dft_n", (2 * part + t) * S, (2 * part + t + 1) * S),
                                               start=(part + t == 0), stop=(part + t == 2), skip_group_check=True)
                    mm.then_inc(s[f"bank_ready{b}"], 1)
                for hh in range(4):
                    small_product(6 + hh % 2, [(wuq[:, k, hh * QK_DIM:hh * QK_DIM + P], px[:, 6 + k, cols]) for k in range(2)], cols)
                for i in range(2):
                    for e in range(2):
                        c0 = (2 * i + e) * QK_DIM + QK_NOPE
                        small_product(6 + i, [(wuq[:, k, c0:c0 + QK_ROPE], px[:, 6 + k, cols]) for k in range(2)], cols,
                                      slice(e * HD, (e + 1) * HD), e == 0, e == 1)
                for hh in range(4):
                    small_product(6 + hh % 2, [(wukv[:, hh * S:hh * S + P], px[:, 8, :])])
                for tt in range(4):
                    v_cols = wukv[:, :].rearrange("p (h c) -> p h c", c=S)[:, :, P:S]
                    small_product(6 + tt % 2, [(px[:, 8, tt * P:(tt + 1) * P], v_cols)])
                for side in range(2):
                    c = slice(0, T) if side else cols
                    pe.wait_ge(*n.next("squared", 5 if side else 6))
                    for hh in range(4):
                        r = sq[:, 4, c] if side else sq[:, 4 + hh // 2, c]
                        m = "half0" if side else f"half{hh % 2}"
                        small_product(4 + hh, [(tab("mean_192"), sq[:, hh, c]), (tab(m), r)], c)
                pe.wait_ge(*n.next("norm_ready", 8 + 8))
                for j, x in enumerate((qr[:, 0, LAT], qr[:, 1, LAT], kr[:, 0, LAT], kr[:, 1, LAT])):
                    small_product(4 + j, [(tab("rot"), x)], LAT)
                pe.wait_ge(*n.next("q_ready", 4))
                attend(mla_plan(ctx_too), BLOCK2)
                for k in range(4):
                    pe.wait_ge(*n.next("x_ready"))
                evacuated(7)
                with n.loop(pe, 2, {"split_ready:use": 4, **{f"bank_read{b}:free": 1 for b in range(4)}}):
                    for b in range(4):
                        acquire(b)
                        product(b, unit(), KD, 0, xhi, xlo, cols, True, True)
                rms_stat(cols)
                pe.wait_ge(*n.next("moe_in_ready", KD))
                small_product(4, [(wr[:, k, :], hm[:, k, cols]) for k in range(KD)], cols, slice(0, N_EXP))
                for tt in tts:
                    for half in range(2):
                        b = 6 + half
                        acquire(b)
                        for j in range(4):
                            mm = pe.transpose(bank[b][:, j * P:(j + 1) * P], hm[:, half * 4 + j, tt * P:(tt + 1) * P], tab("ident"))
                        mm.then_inc(s[f"bank_ready{b}"], 1)
                    if tt == 0:
                        evacuated(4)
                        acquire(5)
                        for t2 in tts:
                            mm = pe.transpose(bank[5][:, t2 * N_EXP:(t2 + 1) * N_EXP], tmp[0:N_EXP, 0, t2 * P:(t2 + 1) * P], tab("ident")[0:N_EXP, 0:N_EXP])
                        mm.then_inc(s["bank_ready5"], 1)
                pe.wait_ge(*n.next("softmax_in"))
                acquire(4)
                for tt in tts:
                    mm = pe.transpose(bank[4][0:N_EXP, tt * P:(tt + 1) * P], aff[:, tt, :], tab("ident"))
                mm.then_inc(s["bank_ready4"], 1)
                pe.wait_ge(*n.next("slots_ready"))
                acquire(5)
                for tt in tts:
                    mm = pe.transpose(bank[5][:, tt * N_EXP:(tt + 1) * N_EXP], tmp[0:N_EXP, 2, tt * P:(tt + 1) * P], tab("ident")[0:N_EXP, 0:N_EXP])
                mm.then_inc(s["bank_ready5"], 1)
                pe.wait_ge(*n.next("slots_ready"))
                evacuated(6)
                evacuated(7)
                for g in range(len(tts) // 2):
                    for k in range(KD):
                        small_product(4 + k % 4, [(htok[:, 2 * g + t, k * P:(k + 1) * P], oh[:, 2 * g + t, :, :]) for t in range(2)])
                for g in range(len(tts) // 2):
                    for c2 in range(2):
                        b = 4 + c2
                        acquire(b)
                        for c in range(2):
                            for t in range(2):
                                o = c * S + t * P
                                mm = pe.transpose(bank[b][:, o:o + P], ohw[:, 2 * g + t, (2 * c2 + c) * P:(2 * c2 + c + 1) * P], tab("ident"))
                        mm.then_inc(s[f"bank_ready{b}"], 1)
                with n.loop(pe, N_EXP, {"split_ready:use": 12, **{f"bank_read{b}:free": 1 for b in range(5)}, "est_ready": 1, "hid_ready": 1}):
                    pe.wait_ge(*n.next("est_ready"))
                    for b in range(2):
                        acquire(b)
                        for q in range(4):
                            slot = unit()
                            for kk in range(2):
                                for part, w in enumerate((whi, wlo)):
                                    mm = pe.matmul(bank[b][:, :], est[:, 2 * q + kk, :], w[:, slot, kk * 512:(kk + 1) * 512],
                                                   start=(q + kk + part == 0), stop=(q == 3 and kk == 1 and part == 1))
                            mm.then_inc(s["units_done"], 1)
                    pe.wait_ge(*n.next("hid_ready"))
                    acquire(4)
                    passed()
                    for j in range(4):
                        mm = pe.transpose(bank[4][:, j * 64:(j + 1) * 64], hid[0:64, j * P:(j + 1) * P], tab("ident")[0:64, 0:64])
                    mm.then_inc(s["bank_ready4"], 1)
                    evacuated(4)
                    acquire(2)
                    acquire(3)
                    for k in range(4):
                        slot = unit()
                        for half in range(2):
                            for part, w in enumerate((whi, wlo)):
                                mm = pe.matmul(bank[2 + half][:, :], hidT[:, k, :], w[:, slot, half * 512:(half + 1) * 512],
                                               start=(k + part == 0), stop=(k == 3 and part == 1))
                        mm.then_inc(s["units_done"], 1)
                pe.wait_ge(*n.next("y_loaded", 16 * 2 * len(tts)))
                for k in range(KD):
                    b = 4 + k % 4
                    acquire(b)
                    for g in range(len(tts) // 2):
                        for c in range(4):
                            mm = pe.matmul(bank[b][:, g * S:(g + 1) * S], yp[:, g, c, k * P:(k + 1) * P], st[:, g, c, :],
                                           start=(c == 0), stop=(c == 3), skip_group_check=True)
                    mm.then_inc(s[f"bank_ready{b}"], 1)

            pe.wait_ge(*n.next("h_ready", 7))
            for t in range(2):
                for half in range(2):
                    b = 4 + half
                    acquire(b)
                    for j in range(4):
                        k = half * 4 + j
                        mm = pe.transpose(bank[b][:, j * P:(j + 1) * P], h[:, k, t * P:(t + 1) * P], tab("ident"))
                    mm.then_inc(s[f"bank_ready{b}"], 1)

        @block.scalar
        def _(act):
            n = Counts(s, {"units_done": RING, **BANKS})
            split_no = [0]
            left = [-1]

            def own():
                if n.last is not None:
                    act.wait_ge(*n.last)

            def passed():
                act.sem_inc(s["act_passed"], 1)

            def split():
                if left[0] == 0:
                    return
                left[0] -= 1
                slot = split_no[0] % RING
                split_no[0] += 1
                act.wait_ge(*n.next(f"raw_full{slot}", 16))
                act.wait_ge(*n.next("units_done:free"))
                act.activation(whi[:, slot, :], raw[:, slot, :], ACT.Copy).then_inc(*n.mark("hi_ready"))

            def units(k):
                for _ in range(k):
                    split()
                act.wait_ge(*n.next("units_done", k))

            SPLIT4 = {**{f"raw_full{r}": 16 for r in range(RING)}, "units_done:free": 4, "units_done": 4, "hi_ready": 4}

            def strides(times=1, **more):
                return {**{k: x * times for k, x in SPLIT4.items()}, **more}

            def condition(name):
                tile, row, cnt = VEC[name]
                src = vec[:, tile, row:row + 2 * KD].rearrange("p (g k) -> p k g", g=2)
                own()
                act.activation(cs[:, :, :], src, ACT.Silu).then_inc(*n.mark("cs_ready"))

            def mods(nblocks):
                with n.loop(act, nblocks, strides(bank_read0=1, bank_read4=1)):
                    units(4)
                    act.activation(mrow[0:4, :], bank[0][0:4, :], ACT.Copy).then_inc(*n.mark("bank_read0"))
                    n.next("bank_read4")

            def split_input():
                for k in range(KD):
                    act.wait_ge(*n.next("hm_ready"))
                    act.activation(xhi[:, k, :], hm[:, k, :], ACT.Copy).then_inc(*n.mark("xhi_ready"))

            def up_down(cols):
                for f0, nf in HALVES:
                    with n.loop(act, nf // 2, strides(**{f"bank_read{b}": 1 for b in range(4)})):
                        for f in range(2):
                            units(2)
                            act.activation(tmp[:, f, cols], bank[2 * f][:, cols], ACT.Silu).then_inc(*n.mark(f"bank_read{2 * f}"))
                            n.next(f"bank_read{2 * f + 1}")
                    with n.loop(act, KD // 2, strides(bank_read0=1, bank_read1=1)):
                        for b in range(2):
                            units(2)
                            n.next(f"bank_read{b}")

            def layer_norm(cols):
                n.next("bank_read4")
                for k in range(KD):
                    act.wait_ge(*n.next("centered"))
                    act.activation(hm[:, k, cols], h[:, k, cols], ACT.Square).then_inc(*n.mark("squared"))
                act.wait_ge(*n.filled(5))
                act.activation(tmp[:, 0, cols], bank[5][:, cols], ACT.Sqrt, bias=eps_ln).then_inc(*n.mark("bank_read5"))

            def attend(plan, out_tile, where=BLOCK1, out_bank=7):
                items, pvs, outs, out_cols = plan
                prob, pT, values, out_hi, out_lo = where

                def exp(m):
                    it = items[m]
                    b = 4 + m % 2
                    act.wait_ge(*n.next("max_ready"))
                    own()
                    nk = it["nk"] * P
                    act.activation(prob[:, m % 2, 0:nk], bank[b][:, 0:nk], ACT.Exp, bias=small[:, m % 2:m % 2 + 1],
                                   accum_out=small[:, 2 + m % 2:3 + m % 2]).then_inc(*n.mark(f"bank_read{b}"))
                    if it["sink"]:
                        own()
                        passed()
                        act.activation(small[:, 4 + m % 2:5 + m % 2], sinks[:, ds(it["qhead"] + out_tile(0) * 2, 1)], ACT.Exp,
                                       bias=small[:, m % 2:m % 2 + 1]).then_inc(*n.mark("sink_exp"))

                exp(0)
                exp(1)
                for m, it in enumerate(items):
                    act.wait_ge(*n.filled(6))
                    src = bank[6][:, 0:it["nk"] * P].rearrange("p (k q) -> p k q", q=P)
                    act.activation(pT[:, it["pg"], 0:it["nk"], it["tt"] * P:(it["tt"] + 1) * P], src, ACT.Copy)\
                        .then_inc(*n.mark("bank_read6"))
                    if m + 2 < len(items):
                        exp(m + 2)
                    for qq in outs.get(m, ()):
                        act.wait_ge(*n.filled(out_bank))
                        cols = out_cols
                        passed()
                        act.activation(out_hi[:, ds(out_tile(qq), 1), cols], bank[out_bank][:, cols].unsqueeze(1), ACT.Copy)\
                            .then_inc(*n.mark("ao_hi"))
                        n.next(f"bank_read{out_bank}")

            def out_projection():
                with n.loop(act, 2, strides(**{f"bank_read{b}": 1 for b in range(4)})):
                    for b in range(4):
                        units(1)
                        n.next(f"bank_read{b}")

            act.wait_ge(*n.next("vec_ready"))
            n.next("bank_read4")
            for b in (5, 6):
                n.next(f"bank_read{b}", 4)
            condition("c")
            for _ in range(AHEAD):
                split()
            for l in range(DEPTH):
                ctx_too = l < DEPTH - 1
                cols = slice(0, T) if ctx_too else LAT
                mods(18)
                split_input()
                up_down(slice(0, T))
                layer_norm(slice(0, T))
                split_input()
                if l == 0:
                    more = {"bank_read0": 4, "bank_read1": 4, "bank_read2": 4, "bank_read4": 16,
                            "bank_read5": 16, "bank_read6": 36, "bank_read7": 4, 
                            "max_ready": 32, "ao_hi": 4}
                    with n.loop(act, 2, strides(3, **more)) as i:
                        for f in range(4):
                            units(1)
                            act.activation(qS[:, 0, :], bank[0][:, :], ACT.Copy, scale=HD ** -0.5).then_inc(*n.mark("bank_read0"))
                            units(1)
                            n.next("bank_read1")
                            units(1)
                            act.activation(vF[:, :], bank[2][:, :], ACT.Copy).then_inc(*n.mark("bank_read2"))
                            n.next("bank_read6")
                            attend(NA, lambda qq: i * 4 + f)
                else:
                    more = {"bank_read0": 1, "bank_read1": 1, "bank_read2": 1, "bank_read3": 1, "bank_read4": 6,
                            "bank_read5": 5, "bank_read6": 9, "bank_read7": 2, 
                            "max_ready": 8, "ao_hi": 2, "sink_exp": 8}
                    with n.loop(act, 4, strides(1, **more)) as i:
                        units(1)
                        act.activation(kS[:, :], bank[0][:, :], ACT.Copy).then_inc(*n.mark("bank_read0"))
                        units(1)
                        act.activation(vF[:, :], bank[1][:, :], ACT.Copy).then_inc(*n.mark("bank_read1"))
                        for q in range(2):
                            units(1)
                            act.activation(qS[:, q, LAT], bank[2 + q][:, LAT], ACT.Copy, scale=HD ** -0.5)\
                                .then_inc(*n.mark(f"bank_read{2 + q}"))
                        n.next("bank_read4", 2)
                        n.next("bank_read5")
                        n.next("bank_read6")
                        attend(WA, lambda qq: i * 2 + qq)
                out_projection()
                layer_norm(cols)
                split_input()
                up_down(cols)
                layer_norm(cols)

            def rms_stat(cols):
                act.wait_ge(*n.next("h_ready"))
                for k in range(KD):
                    act.activation(hm[:, k, cols], h[:, k, cols], ACT.Square).then_inc(*n.mark("squared"))
                act.wait_ge(*n.filled(5))
                act.activation(tmp[:, 0, cols], bank[5][:, cols], ACT.Sqrt, bias=eps_rms).then_inc(*n.mark("bank_read5"))

            def square(j, x, c):
                act.activation(sq[:, j, c], x, ACT.Square).then_inc(*n.mark("squared"))

            def root(b, j, c):
                act.wait_ge(*n.filled(b))
                act.activation(tmp[:, j, c], bank[b][:, c], ACT.Sqrt, bias=eps_rms).then_inc(*n.mark(f"bank_read{b}"))

            def copy(b, dst, src):
                act.wait_ge(*n.filled(b))
                act.activation(dst, src, ACT.Copy).then_inc(*n.mark(f"bank_read{b}"))

            n.next("h_ready", 7)
            condition("c_2")
            for b in (4, 5):
                n.next(f"bank_read{b}", 4)
            for l in range(DEPTH):
                ctx_too = l < DEPTH - 1
                cols = slice(0, T) if ctx_too else LAT
                tts = range(4 if ctx_too else 2)
                mods(12)
                rms_stat(slice(0, T))
                split_input()
                for j in range(10):
                    units(1)
                    c = cols if j < 8 else slice(0, T)
                    act.activation(px[:, j, c], bank[j % 4][:, c], ACT.Gelu_apprx_tanh if j < 4 else ACT.Copy)\
                        .then_inc(*n.mark(f"bank_read{j % 4}"))
                own()
                for j, t in enumerate((2, 3, 6, 7, 8)):
                    c = cols if t < 8 else slice(0, T)
                    square(j, px[:, t, c], c)
                for j in range(3):
                    root(4 + j, j, slice(0, T) if j == 2 else cols)
                n.next("bank_read7")
                for tt in tts:
                    n.next(f"bank_read{4 + tt % 2}", 2)
                for tt in tts:
                    copy(6 + tt % 2, fd[:, tt, :], bank[6 + tt % 2][:, :])
                act.wait_ge(*n.next("ya_ready"))
                for i in range(2):
                    act.activation(xhi[:, i, cols], px[:, i, cols], ACT.Copy).then_inc(*n.mark("xhi_ready"))
                for i in range(2):
                    act.wait_ge(*n.filled(4 + i))
                    act.activation(xhi[:, 2 + i, cols], bank[4 + i][:, cols], ACT.Copy).then_inc(*n.mark("xhi_ready"))
                    n.next(f"bank_read{4 + i}")
                for hh in range(4):
                    copy(6 + hh % 2, qn[:, hh, cols], bank[6 + hh % 2][:, cols])
                for i in range(2):
                    copy(6 + i, qr[:, i, cols], bank[6 + i][:, cols])
                for b in (6, 7):
                    n.next(f"bank_read{b}", 4)
                own()
                for hh in range(4):
                    square(hh, qn[:, hh, cols], cols)
                for i in range(2):
                    square(4 + i, qr[:, i, cols], cols)
                for hh in range(4):
                    root(4 + hh, hh, cols)
                act.wait_ge(*n.next("norm_ready", 5 + 8))
                for hh in range(4):
                    square(hh, kn[:, hh, :], slice(0, T))
                square(4, px[:, 9, :], slice(0, T))
                for hh in range(4):
                    root(4 + hh, hh, slice(0, T))
                n.next("norm_ready", 8)
                for b in range(4, 8):
                    n.next(f"bank_read{b}")
                attend(mla_plan(ctx_too), lambda hh: 4 + hh, BLOCK2)
                with n.loop(act, 2, strides(**{f"bank_read{b}": 1 for b in range(4)})):
                    for b in range(4):
                        units(1)
                        n.next(f"bank_read{b}")
                rms_stat(cols)
                n.next("bank_read4")
                for tt in tts:
                    for b in (6, 7):
                        copy(b, htok[:, tt, (b - 6) * 512:(b - 5) * 512], bank[b][:, :])
                    if tt == 0:
                        n.next("bank_read5")
                act.wait_ge(*n.next("logits_moved"))
                nt = len(tts)
                act.activation(aff[:, 0:nt, :], aff[:, 0:nt, :], ACT.Exp).then_inc(*n.mark("softmax_exp"))
                for b in (4, 5):
                    n.next(f"bank_read{b}")
                for g in range(nt // 2):
                    for k in range(KD):
                        b = 4 + k % 4
                        if k % 2:
                            copy(b, xsT[:, k, :, g * CAP:(g + 1) * CAP], bank[b][:, :].rearrange("p (e s) -> p e s", s=CAP))
                        else:
                            n.next(f"bank_read{b}")
                for g in range(nt // 2):
                    for c2 in range(2):
                        copy(4 + c2, st[:, g, 2 * c2:2 * c2 + 2, :], bank[4 + c2][:, :].rearrange("p (c t) -> p c t", t=S))

                def expert(i):
                    act.wait_ge(*n.next("slots_used"))
                    passed()
                    act.activation(est[:, :, 0:64].unsqueeze(2), xsT[:, :, ds(i, 1), :], ACT.Copy).then_inc(*n.mark("est_hi"))
                    units(4)
                    act.activation(tmp[0:64, 0, :], bank[0][64:P, :], ACT.Copy).then_inc(*n.mark("gate_low"))
                    n.next("bank_read0")
                    act.wait_ge(*n.next("gate_in"))
                    act.activation(tmp[0:64, 1, :], tmp[0:64, 1, :], ACT.Silu).then_inc(*n.mark("gate_ready"))
                    units(4)
                    act.activation(tmp[0:64, 2, :], bank[1][64:P, :], ACT.Copy).then_inc(*n.mark("up_low"))
                    n.next("bank_read1")
                    act.wait_ge(*n.filled(4))
                    act.activation(hidT[:, :, 0:64], bank[4][:, 0:256].rearrange("p (j c) -> p j c", c=64), ACT.Copy)\
                        .then_inc(*n.mark("hidT_hi"))
                    n.next("bank_read4")
                    units(4)
                    for half in range(2):
                        act.activation(tmp[0:64, 3 * (1 - half), :], bank[2 + half][64:P, :], ACT.Copy).then_inc(*n.mark("y_low"))
                        n.next(f"bank_read{2 + half}")

                grow = strides(3, slots_used=1, est_hi=1, gate_low=1, gate_in=1, gate_ready=1, up_low=1, hidT_hi=1, y_low=2,
                               **{f"bank_read{b}": 1 for b in range(5)})
                last = l == DEPTH - 1
                with n.loop(act, N_EXP - last, grow) as i:
                    expert(i)
                if last:
                    left[0] = 12 - AHEAD
                    expert(N_EXP - 1)
                n.next("slots_used")
                for k in range(KD):
                    n.next(f"bank_read{4 + k % 4}")
                n.next("h_ready")

        @block.vector
        def _(dve):
            n = Counts(s, {"units_done": RING, "split_ready": RING, **BANKS})
            split_no = [0]
            left = [-1]
            dve.sem_inc(s["split_ready"], RING)

            def own():
                if n.last is not None:
                    dve.wait_ge(*n.last)

            def split():
                if left[0] == 0:
                    return
                left[0] -= 1
                slot = split_no[0] % RING
                split_no[0] += 1
                dve.wait_ge(*n.next("hi_ready"))
                dve.tensor_tensor(wlo[:, slot, :], raw[:, slot, :], whi[:, slot, :].bitcast(F32), ALU.subtract)\
                    .then_inc(*n.mark("split_ready"))

            def units(k):
                for _ in range(k):
                    split()
                dve.wait_ge(*n.next("units_done", k))

            def strides(times=1, **more):
                return {"hi_ready": 4 * times, "split_ready": 4 * times, "units_done": 4 * times, **more}

            def condition():
                dve.wait_ge(*n.next("cs_ready"))
                dve.tensor_copy(cond[:, :, 0:2], cs[:, :, :]).then_inc(*n.mark("dve"))
                own()
                dve.tensor_tensor(cond[:, :, 2:4], cs[:, :, :], cond[:, :, 0:2].bitcast(F32), ALU.subtract)\
                    .then_inc(*n.mark("cond_ready"))

            def mods(nblocks, bias, plus_one, halved):
                with n.loop(dve, nblocks, strides(bank_read0=1, bank_read4=1, dve=1)) as i:
                    units(4)
                    n.next("bank_read0")
                    dve.wait_ge(*n.filled(4))
                    dve.tensor_copy(mt[:, :], bank[4][:, 0:16]).then_inc(*n.mark("bank_read4"))
                    own()
                    four = mt[:, :].rearrange("p (j r) -> p j r", r=4)
                    dve.tensor_tensor(mod[:, ds(i * 4, 4), :], four[:, :, 0:2], four[:, :, 2:4], ALU.add).then_inc(*n.mark("dve"))
                w = 4 * nblocks
                dve.tensor_tensor(mod[:, 0:w, :], mod[:, 0:w, :], bias.unsqueeze(2).broadcast_to([P, w, 2]), ALU.add).then_inc(*n.mark("dve"))
                for j in plus_one:
                    own()
                    x = mod[:, j * KD:(j + 1) * KD, :]
                    dve.tensor_scalar(x, x, 1.0, None, ALU.add).then_inc(*n.mark("dve"))
                for j in halved:
                    own()
                    x = mod[:, j * KD:(j + 1) * KD, :]
                    dve.tensor_scalar(x, x, 0.5, None, ALU.mult).then_inc(*n.mark("dve"))

            def low(k):
                dve.wait_ge(*n.next("xhi_ready"))
                dve.tensor_tensor(xlo[:, k, :], hm[:, k, :], xhi[:, k, :].bitcast(F32), ALU.subtract).then_inc(*n.mark("x_ready"))

            def modulate(shift, scale):
                for k in range(KD + 1):
                    if k < KD:
                        for g, cols in enumerate(GROUPS):
                            own()
                            dve.tensor_scalar(hm[:, k, cols], h[:, k, cols], mcol(scale, k, g), mcol(shift, k, g),
                                              ALU.mult, ALU.add).then_inc(*n.mark("hm_ready" if g else "dve"))
                    if k:
                        low(k - 1)

            def scale_residual(cols):
                for k in range(KD):
                    own()
                    dve.tensor_scalar(h[:, k, cols], h[:, k, cols], ALPHA, None, ALU.mult).then_inc(*n.mark("dve"))

            def residual(b, gate, k, cols):
                groups = GROUPS if cols.stop == T else (LAT,)
                for g, gc in enumerate(groups):
                    own()
                    x = h[:, ds(k, 1), gc]
                    last = g == len(groups) - 1
                    dve.scalar_tensor_tensor(x, bank[b][:, gc].unsqueeze(1), mod[:, ds(gate * KD + k, 1), g], x, ALU.mult, ALU.add)\
                        .then_inc(*n.mark(f"bank_read{b}" if last else "dve"))

            def up_down(cols, gate):
                scale_residual(cols)
                more = 1 if cols.stop == T else 0
                for f0, nf in HALVES:
                    with n.loop(dve, nf // 2, strides(dve=2, hidden_ready=2, **{f"bank_read{b}": 1 for b in range(4)})) as i:
                        for f in range(2):
                            units(2)
                            dve.wait_ge(*n.next(f"bank_read{2 * f}"))
                            dve.tensor_tensor(tmp[:, 2 + f, cols], tmp[:, f, cols], bank[2 * f + 1][:, cols], ALU.mult)\
                                .then_inc(*n.mark(f"bank_read{2 * f + 1}"))
                            own()
                            x = tmp[:, 2 + f, cols].unsqueeze(1)
                            dve.tensor_copy(hhi[:, ds(i * 2 + f, 1), cols], x).then_inc(*n.mark("dve"))
                            own()
                            dve.tensor_tensor(hlo[:, ds(i * 2 + f, 1), cols], x, hhi[:, ds(i * 2 + f, 1), cols].bitcast(F32),
                                              ALU.subtract).then_inc(*n.mark("hidden_ready"))
                    with n.loop(dve, KD // 2, strides(dve=2 * more, bank_read0=1, bank_read1=1)) as i:
                        for b in range(2):
                            units(2)
                            residual(b, gate, i * 2 + b, cols)
                own()
                dve.sem_inc(*n.mark("h_ready"))

            def layer_norm(cols, l, j):
                n.next("bank_read5")
                dve.wait_ge(*n.filled(4))
                own()
                dve.tensor_copy(tmp[:, 1, cols], bank[4][:, cols]).then_inc(*n.mark("bank_read4"))
                for k in range(KD):
                    own()
                    dve.tensor_tensor(h[:, k, cols], h[:, k, cols], tmp[:, 1, cols], ALU.subtract).then_inc(*n.mark("centered"))
                dve.wait_ge(*n.peek("bank_read5"))
                own()
                dve.reciprocal(tmp[:, 1, cols], tmp[:, 0, cols]).then_inc(*n.mark("dve"))
                for k in range(KD):
                    i = (l * 3 + j) * KD + k
                    own()
                    dve.scalar_tensor_tensor(h[:, k, cols], h[:, k, cols], v("ln_g", i, 1), tmp[:, 1, cols], ALU.mult, ALU.mult)\
                        .then_inc(*n.mark("dve"))
                    own()
                    dve.tensor_scalar(h[:, k, cols], h[:, k, cols], v("ln_b", i, 1), None, ALU.add).then_inc(*n.mark("dve"))

            def attend(plan, out_tile, where=BLOCK1, out_bank=7):
                items, pvs, outs, out_cols = plan
                prob, pT, values, out_hi, out_lo = where

                def most(m):
                    it = items[m]
                    b = 4 + m % 2
                    dve.wait_ge(*n.filled(b))
                    own()
                    x = small[:, m % 2:m % 2 + 1]
                    dve.tensor_reduce(x, bank[b][:, 0:it["nk"] * P], AXX, ALU.max, negate=True)\
                        .then_inc(*n.mark("dve" if it["sink"] else "max_ready"))
                    if it["sink"]:
                        own()
                        dve.tensor_tensor(x, x, nsinks[:, ds(it["qhead"] + out_tile(0) * 2, 1)], ALU.min).then_inc(*n.mark("max_ready"))

                def normalise(m):
                    it = items[m]
                    dve.wait_ge(*n.next(f"bank_read{4 + m % 2}"))
                    total = small[:, 2 + m % 2:3 + m % 2]
                    own()
                    if it["sink"]:
                        dve.wait_ge(*n.next("sink_exp"))
                        dve.tensor_tensor(total, total, small[:, 4 + m % 2:5 + m % 2], ALU.add).then_inc(*n.mark("dve"))
                        own()
                    dve.reciprocal(total, total).then_inc(*n.mark("dve"))
                    own()
                    x = prob[:, m % 2, 0:it["nk"] * P]
                    dve.tensor_scalar(x, x, total, None, ALU.mult).then_inc(*n.mark("p_ready"))

                most(0)
                most(1)
                for m, it in enumerate(items):
                    normalise(m)
                    n.next("bank_read6")
                    if m + 2 < len(items):
                        most(m + 2)
                    for qq in outs.get(m, ()):
                        cols = out_cols
                        dve.wait_ge(*n.next("ao_hi"))
                        dve.tensor_tensor(out_lo[:, ds(out_tile(qq), 1), cols], bank[out_bank][:, cols].unsqueeze(1),
                                          out_hi[:, ds(out_tile(qq), 1), cols].bitcast(F32), ALU.subtract)\
                            .then_inc(*n.mark(f"bank_read{out_bank}"))

            def rotate(b, x):
                dve.wait_ge(*n.filled(b))
                own()
                dve.tensor_tensor(tmp[:, 1, LAT], bank[b][:, LAT], tab("sin"), ALU.mult).then_inc(*n.mark(f"bank_read{b}"))
                own()
                dve.tensor_tensor(x, x, tab("cos"), ALU.mult).then_inc(*n.mark("dve"))
                own()
                dve.tensor_tensor(x, x, tmp[:, 1, LAT], ALU.add).then_inc(*n.mark("q_ready"))

            def out_projection(cols):
                scale_residual(cols)
                more = 1 if cols.stop == T else 0
                with n.loop(dve, 2, strides(dve=4 * more, **{f"bank_read{b}": 1 for b in range(4)})) as i:
                    for b in range(4):
                        units(1)
                        residual(b, GATE2, i * 4 + b, cols)
                own()
                dve.sem_inc(*n.mark("h_ready"))

            dve.memset(cond[:, :, :].bitcast(F32), 0.0).then_inc(*n.mark("dve"))
            dve.memset(eps_ln, LN_EPS).then_inc(*n.mark("dve"))
            dve.memset(eps_rms, RMS_EPS).then_inc(*n.mark("dve"))
            dve.wait_ge(*n.filled(4))
            own()
            dve.tensor_copy(vec[:, :, :], bank[4][:, :].rearrange("p (j c) -> p j c", c=P)).then_inc(*n.mark("bank_read4"))
            own()
            dve.tensor_scalar(nsinks[:, :], sinks[:, :], -1.0, None, ALU.mult).then_inc(*n.mark("vec_ready"))
            for k in range(KD):
                b = 5 + k % 2
                dve.wait_ge(*n.filled(b))
                own()
                dve.tensor_copy(h[:, k, :], bank[b][:, :]).then_inc(*n.mark(f"bank_read{b}"))
            own()
            condition()
            for _ in range(AHEAD):
                split()
            for l in range(DEPTH):
                ctx_too = l < DEPTH - 1
                cols = slice(0, T) if ctx_too else LAT
                mods(18, v(f"b_mod{l}"), (SCALE1, SCALE2, SCALE3), (GATE1, GATE3))
                modulate(SHIFT1, SCALE1)
                up_down(slice(0, T), GATE1)
                layer_norm(slice(0, T), l, 0)
                modulate(SHIFT2, SCALE2)
                if l == 0:
                    more = {"bank_read0": 4, "bank_read1": 4, "bank_read2": 4, "bank_read4": 16,
                            "bank_read5": 16, "bank_read6": 36, "bank_read7": 4, 
                            "max_ready": 32, "p_ready": 32, "dve": 32, "ao_hi": 4}
                    with n.loop(dve, 2, strides(3, **more)) as i:
                        for f in range(4):
                            units(1)
                            n.next("bank_read0")
                            units(1)
                            dve.tensor_copy(kS[:, :], bank[1][:, :]).then_inc(*n.mark("bank_read1"))
                            units(1)
                            n.next("bank_read2")
                            dve.wait_ge(*n.filled(6))
                            dve.tensor_copy(vS[:, :, :], bank[6][:, :].rearrange("p (t c) -> p t c", c=P)).then_inc(*n.mark("bank_read6"))
                            attend(NA, lambda qq: i * 4 + f)
                else:
                    more = {"bank_read0": 1, "bank_read1": 1, "bank_read2": 1, "bank_read3": 1, "bank_read4": 6,
                            "bank_read5": 5, "bank_read6": 9, "bank_read7": 2, 
                            "max_ready": 8, "p_ready": 8, "ao_hi": 2, "sink_exp": 8, "q_ready": 3,
                            "dve": 8 + 16 + 3}
                    with n.loop(dve, 4, strides(1, **more)) as i:
                        units(4)
                        for b in range(4):
                            n.next(f"bank_read{b}")
                        dve.wait_ge(*n.filled(6))
                        own()
                        dve.tensor_copy(vS[:, :, 0:HD], bank[6][:, :].rearrange("p (t c) -> p t c", c=P)[:, :, 0:HD])\
                            .then_inc(*n.mark("bank_read6"))
                        for j, (b, x) in enumerate(((0, kS[:, LAT]), (2, qS[:, 0, LAT]), (3, qS[:, 1, LAT]))):
                            rb = 4 + j % 2
                            rotate(rb, x)
                        attend(WA, lambda qq: i * 2 + qq)
                out_projection(cols)
                layer_norm(cols, l, 1)
                modulate(SHIFT3, SCALE3)
                up_down(cols, GATE3)
                layer_norm(cols, l, 2)

            def rms_modulate(shift, scale, cols, split_too):
                own()
                dve.sem_inc(*n.mark("h_ready"))
                groups = [(g, c) for g, c in enumerate(GROUPS) if c.start < cols.stop]
                dve.wait_ge(*n.next("bank_read5"))
                own()
                dve.reciprocal(tmp[:, 1, cols], tmp[:, 0, cols]).then_inc(*n.mark("dve"))
                for k in range(KD + 1):
                    if k < KD:
                        for g, c in groups:
                            own()
                            dve.scalar_tensor_tensor(hm[:, k, c], h[:, k, c], mcol(scale, k, g), tmp[:, 1, c], ALU.mult, ALU.mult)\
                                .then_inc(*n.mark("dve"))
                            own()
                            dve.tensor_scalar(hm[:, k, c], hm[:, k, c], mcol(shift, k, g), None, ALU.add)\
                                .then_inc(*n.mark("dve" if (g, c) != groups[-1] else "hm_ready" if split_too else "moe_in_ready"))
                    if k and split_too:
                        low(k - 1)

            def copy(b, dst, src, key=None):
                dve.wait_ge(*n.filled(b))
                own()
                dve.tensor_copy(dst, src).then_inc(*n.mark(key or f"bank_read{b}"))

            def inverse(b, j, c):
                dve.wait_ge(*n.next(f"bank_read{b}"))
                own()
                dve.reciprocal(tmp[:, j, c], tmp[:, j, c]).then_inc(*n.mark("dve"))

            def normed(dst, src, weight, root, key="norm_ready"):
                own()
                dve.scalar_tensor_tensor(dst, src, weight, root, ALU.mult, ALU.mult).then_inc(*n.mark(key))

            for name in ("qn", "qr"):
                own()
                dve.tensor_scalar(v(name), v(name), QK_DIM ** -0.5, None, ALU.mult).then_inc(*n.mark("dve"))
            own()
            dve.sem_inc(*n.mark("h_ready"))
            for k in range(KD):
                b = 4 + k % 2
                copy(b, h[:, k, CTX], bank[b][:, 0:S])
            condition()
            for l in range(DEPTH):
                ctx_too = l < DEPTH - 1
                cols = slice(0, T) if ctx_too else LAT
                tts = range(4 if ctx_too else 2)
                nt = len(tts)
                mods(12, v("b_ada", l * 48, 48), (1, 4), ())
                rms_modulate(0, 1, slice(0, T), True)
                for j in range(10):
                    units(1)
                    n.next(f"bank_read{j % 4}")
                for j in range(3):
                    inverse(4 + j, j, slice(0, T) if j == 2 else cols)
                for i in range(2):
                    normed(px[:, 2 + i, cols], px[:, 2 + i, cols], v("sgu", 2 * l + i, 1), tmp[:, 0, cols])
                for i in range(2):
                    normed(px[:, 6 + i, cols], px[:, 6 + i, cols], v("qlora", 2 * l + i, 1), tmp[:, 1, cols])
                normed(px[:, 8, :], px[:, 8, :], v("kvlora", l, 1), tmp[:, 2, :])
                copy(7, wsT[:, :, :], bank[7][:, :].rearrange("p (h c) -> p h c", c=P))
                for tt in tts:
                    b = 4 + tt % 2
                    copy(b, vtok[:, tt, :], bank[b][:, 0:2 * P])
                for tt in tts:
                    b = 4 + tt % 2
                    dve.wait_ge(*n.filled(b))
                    for i in range(2):
                        for e in range(2):
                            rows = slice(e * HD, (e + 1) * HD)
                            x = px[rows, i, tt * P:(tt + 1) * P]
                            own()
                            dve.tensor_tensor(x, x, bank[b][rows, i * S + e * P:i * S + (e + 1) * P], ALU.mult)\
                                .then_inc(*n.mark(f"bank_read{b}" if i + e == 2 else "dve"))
                own()
                dve.sem_inc(*n.mark("ya_ready"))
                for tt in tts:
                    n.next(f"bank_read{6 + tt % 2}")
                for i in range(2):
                    dve.wait_ge(*n.next("xhi_ready"))
                    dve.tensor_tensor(xlo[:, i, cols], px[:, i, cols], xhi[:, i, cols].bitcast(F32), ALU.subtract).then_inc(*n.mark("x_ready"))
                for i in range(2):
                    dve.wait_ge(*n.next("xhi_ready"))
                    dve.tensor_tensor(xlo[:, 2 + i, cols], bank[4 + i][:, cols], xhi[:, 2 + i, cols].bitcast(F32), ALU.subtract)\
                        .then_inc(*n.mark(f"bank_read{4 + i}"))
                    own()
                    dve.sem_inc(*n.mark("x_ready"))
                n.next("bank_read6", 3)
                n.next("bank_read7", 3)
                for hh in range(4):
                    copy(6 + hh % 2, kn[:, hh, :], bank[6 + hh % 2][:, :])
                for tt in range(4):
                    copy(6 + tt % 2, vt[:, tt, :], bank[6 + tt % 2][:, :])
                for hh in range(4):
                    inverse(4 + hh, hh, cols)
                for hh in range(4):
                    rows = slice(hh % 2 * HD, hh % 2 * HD + HD)
                    normed(qn[:, hh, cols], qn[:, hh, cols], v("qn", l, 1), tmp[:, hh, cols])
                    x = qr[rows, hh // 2, cols]
                    normed(x, x, v("qr", l, 1)[rows, :], tmp[rows, hh, cols])
                for hh in range(4):
                    inverse(4 + hh, hh, slice(0, T))
                for hh in range(4):
                    rows = slice(hh % 2 * HD, hh % 2 * HD + HD)
                    normed(kn[:, hh, :], kn[:, hh, :], v("kn", l, 1), tmp[:, hh, :])
                    normed(kr[rows, hh // 2, :], px[rows, 9, :], v("kr", l, 1)[rows, :], tmp[rows, hh, :])
                for j, x in enumerate((qr[:, 0, LAT], qr[:, 1, LAT], kr[:, 0, LAT], kr[:, 1, LAT])):
                    rotate(4 + j, x)
                attend(mla_plan(ctx_too), lambda hh: 4 + hh, BLOCK2)
                more = 1 if ctx_too else 0
                with n.loop(dve, 2, strides(dve=4 * more, **{f"bank_read{b}": 1 for b in range(4)})) as i:
                    for b in range(4):
                        units(1)
                        residual(b, 2, i * 4 + b, cols)
                rms_modulate(3, 4, cols, False)
                copy(4, tmp[0:N_EXP, 0, cols], bank[4][0:N_EXP, cols])
                copy(5, aff[:, 0:nt, :], bank[5][:, 0:nt * N_EXP].rearrange("p (t e) -> p t e", e=N_EXP))
                for b in (6, 7):
                    n.next(f"bank_read{b}", nt)
                A = aff[:, 0:nt, :]
                peak, total = pos[:, 0, 0:nt], pos[:, 1, 0:nt]
                own()
                dve.tensor_reduce(peak, A, AXX, ALU.max).then_inc(*n.mark("dve"))
                own()
                dve.tensor_tensor(A, A, peak.unsqueeze(2).broadcast_to([P, nt, N_EXP]), ALU.subtract).then_inc(*n.mark("logits_moved"))
                dve.wait_ge(*n.next("softmax_exp"))
                dve.tensor_reduce(total, A, AXX, ALU.add).then_inc(*n.mark("dve"))
                own()
                dve.reciprocal(total, total).then_inc(*n.mark("dve"))
                own()
                dve.tensor_tensor(A, A, total.unsqueeze(2).broadcast_to([P, nt, N_EXP]), ALU.mult).then_inc(*n.mark("softmax_in"))
                copy(4, tmp[0:N_EXP, 1, cols], bank[4][0:N_EXP, cols])
                for g in range(nt // 2):
                    work = tmp[0:N_EXP, 1, GROUPS[g]]
                    for _ in range(CAP // 8):
                        own()
                        dve.max(top8[0:N_EXP, :], work).then_inc(*n.mark("dve"))
                        own()
                        dve.match_replace(work, top8[0:N_EXP, :], work, -1.0).then_inc(*n.mark("dve"))
                    taken, place = tmp[0:N_EXP, 3, GROUPS[g]], tmp[0:N_EXP, 2, GROUPS[g]]
                    own()
                    dve.tensor_scalar(taken, work, 0.0, None, ALU.is_lt).then_inc(*n.mark("dve"))
                    own()
                    dve.tensor_tensor_scan(place, tab("ones", 0, 1)[0:N_EXP, :].broadcast_to([N_EXP, S]), taken, 0.0, ALU.mult, ALU.add)\
                        .then_inc(*n.mark("dve"))
                    own()
                    dve.tensor_tensor(place, place, taken, ALU.mult).then_inc(*n.mark("dve"))
                    own()
                    dve.tensor_scalar(place, place, -1.0, None, ALU.add).then_inc(*n.mark("slots_ready" if g == nt // 2 - 1 else "dve"))
                copy(5, pos[:, 0:nt, :], bank[5][:, 0:nt * N_EXP].rearrange("p (t e) -> p t e", e=N_EXP))
                for tt in tts:
                    own()
                    dve.tensor_tensor(oh[:, tt, :, :], pos[:, tt, :].unsqueeze(2).broadcast_to([P, N_EXP, CAP]),
                                      tab("slots").unsqueeze(1).broadcast_to([P, N_EXP, CAP]), ALU.is_equal).then_inc(*n.mark("dve"))
                    own()
                    dve.tensor_tensor(ohw[:, tt, :].rearrange("p (e s) -> p e s", s=CAP), oh[:, tt, :, :],
                                      aff[:, tt, :].unsqueeze(2).broadcast_to([P, N_EXP, CAP]), ALU.mult)\
                        .then_inc(*n.mark("slots_ready" if tt == nt - 1 else "dve"))
                if not ctx_too:
                    own()
                    dve.memset(xsT[:, :, :, CAP:2 * CAP], 0.0).then_inc(*n.mark("dve"))
                for g in range(nt // 2):
                    for k in range(KD):
                        b = 4 + k % 4
                        if k % 2:
                            n.next(f"bank_read{b}")
                        else:
                            copy(b, xsT[:, k, :, g * CAP:(g + 1) * CAP], bank[b][:, :].rearrange("p (e s) -> p e s", s=CAP))
                n.next("bank_read4", nt // 2)
                n.next("bank_read5", nt // 2)
                own()
                dve.sem_inc(*n.mark("slots_used"))

                def expert(i):
                    dve.wait_ge(*n.next("est_hi"))
                    dve.tensor_tensor(est[:, :, 64:P].unsqueeze(2), xsT[:, :, ds(i, 1), :], est[:, :, 0:64].bitcast(F32).unsqueeze(2), ALU.subtract)\
                        .then_inc(*n.mark("est_ready"))
                    units(4)
                    dve.wait_ge(*n.next("gate_low"))
                    dve.tensor_tensor(tmp[0:64, 1, :], bank[0][0:64, :], tmp[0:64, 0, :], ALU.add).then_inc(*n.mark("bank_read0"))
                    own()
                    dve.sem_inc(*n.mark("gate_in"))
                    units(4)
                    dve.wait_ge(*n.next("up_low"))
                    dve.tensor_tensor(tmp[0:64, 2, :], bank[1][0:64, :], tmp[0:64, 2, :], ALU.add).then_inc(*n.mark("bank_read1"))
                    dve.wait_ge(*n.next("gate_ready"))
                    own()
                    dve.tensor_tensor(hid[0:64, :], tmp[0:64, 1, :], tmp[0:64, 2, :], ALU.mult).then_inc(*n.mark("hid_ready"))
                    dve.wait_ge(*n.next("hidT_hi"))
                    dve.tensor_tensor(hidT[:, :, 64:P], bank[4][:, 0:256].rearrange("p (j c) -> p j c", c=64),
                                      hidT[:, :, 0:64].bitcast(F32), ALU.subtract).then_inc(*n.mark("bank_read4"))
                    units(4)
                    dve.wait_ge(*n.next("y_free"))
                    for half in range(2):
                        dve.wait_ge(*n.next("y_low"))
                        dve.tensor_tensor(ysb[0:64, half * 512:(half + 1) * 512], bank[2 + half][0:64, :], tmp[0:64, 3 * (1 - half), :], ALU.add)\
                            .then_inc(*n.mark(f"bank_read{2 + half}"))
                    own()
                    dve.sem_inc(*n.mark("slots_used"))

                grow = strides(3, slots_used=1, est_hi=1, est_ready=1, gate_low=1, gate_in=1, gate_ready=1, up_low=1, hid_ready=1,
                               hidT_hi=1, y_free=1, y_low=2, **{f"bank_read{b}": 1 for b in range(5)})
                last = l == DEPTH - 1
                with n.loop(dve, N_EXP - last, grow) as i:
                    expert(i)
                if last:
                    left[0] = 12 - AHEAD
                    expert(N_EXP - 1)
                for k in range(KD):
                    b = 4 + k % 4
                    dve.wait_ge(*n.filled(b))
                    residual(b, 5, k, cols)
                own()
                dve.sem_inc(*n.mark("h_ready"))

            for t in range(2):
                for half in range(2):
                    b = 4 + half
                    dve.wait_ge(*n.filled(b))
                    own()
                    dve.tensor_copy(outT[:, t, half * 512:(half + 1) * 512], bank[b][:, :]).then_inc(*n.mark(f"bank_read{b}"))
            own()
            dve.sem_inc(*n.mark("out_ready"))

        @block.gpsimd
        def _(pool):
            n = Counts(s, BANKS)
            pool.memset(vrow[:, :, :], 0.0).then_inc(s["zeroed"], 1)
            pool.wait_ge(*n.next("inputs_loaded", N_LOADS * 16))
            pool.wait_ge(*n.next("x_ready", 2 * KD))
            rpb = a["rpb"]
            with n.loop(pool, 2, dict(bank_read7=4, bias_loaded=8 * 64, bias_ready=8)) as i:
                for f in range(4):
                    pool.wait_ge(*n.peek("bank_read7"))
                    for e in range(2):
                        for t in range(2):
                            for r2 in range(2):
                                r = 2 * t + r2
                                head = i * 8 + (2 * f + e)
                                row0 = NA_KH - 1 - r
                                rows = rpb[ds(head, 1), row0:row0 + ROWS, 0:GRID_W]
                                src = bass.AP(rpb.tensor, rows.offset, [[1, GRID_W], [RPB_W, ROWS], [1, GRID_W]])
                                pool.dma_start(bt[r2 * GRID_W:(r2 + 1) * GRID_W, e, t, :].rearrange("p (r c) -> p r c", c=GRID_W),
                                               src).then_inc(s["bias_loaded"], 16)
                    for e in range(2):
                        if e == 0:
                            pool.wait_ge(*n.next("bias_loaded", 8 * 16))
                        x = bt[:, e, :, :].rearrange("p t (r c) -> p (t r) c", c=GRID_W)
                        pool.tensor_tensor(x, x, tab("na_mask").unsqueeze(1).broadcast_to([P, 2 * ROWS, GRID_W]), ALU.add)\
                            .then_inc(*n.mark("bias_ready"))
                    n.next("bank_read7")
            pool.sem_inc(s["y_free"], 1)
            y_rows = ysb[0:2 * CAP, :]
            pool.wait_ge(*n.next("h_ready", 7))
            pool.dma_start(xtok[:, 0:2, :], a["ctx_2"][0].rearrange("(t p) d -> p t d", p=P)).then_inc(s["ctx_loaded"], 16)
            for l in range(DEPTH):
                if l:
                    pool.wait_ge(*n.next("h_ready", 3))
                for dst, src in (
                        (wuq[:, :, :], a["w_uq_2"][l].rearrange("(k p) n -> p k n", p=P)),
                        (wukv[:, :], a["w_ukv_2"][l]),
                        (wsgu[:, :, :], a["w_sgu_2"][l].rearrange("h p q -> p h q")),
                        (bsgu[0:1, :], a["b_sgu_2"][l].rearrange("h (o p) -> o h p", o=1)),
                        (wr[:, :, :], a["w_router_2"][l].rearrange("(k p) e -> p k e", p=P))):
                    pool.dma_start(dst, src).then_inc(s["small_loaded"], 16)
                groups = 2 if l < DEPTH - 1 else 1
                n.next("slots_used")
                with n.loop(pool, N_EXP, dict(slots_used=1, y_stored=16)) as i:
                    pool.wait_ge(*n.next("slots_used"))
                    pool.dma_start(yscr[ds(i, 1), :, :].rearrange("e s d -> (e s) d"), y_rows).then_inc(s["y_stored"], 16)
                    pool.wait_ge(*n.next("y_stored", 16))
                    pool.sem_inc(s["y_free"], 1)
                for g in range(groups):
                    for c in range(4):
                        pool.dma_start(yp[:, g, c, :], yscr[4 * c:4 * c + 4, g * CAP:(g + 1) * CAP, :]).then_inc(s["y_loaded"], 16)


def lay_out(inputs):
    arrays = {k: np.ascontiguousarray(v) for k, v in inputs.items()}
    arrays["rpb"] = np.pad(arrays.pop("na_rpb")[0], ((0, 0), (0, 0), (RPB_PAD, RPB_PAD)))
    kv = arrays["wa_w_qkv"][0][:, D:].reshape(D, 2, 4, 1, HD)
    arrays["wa_kv"] = np.ascontiguousarray(np.repeat(kv, 2, 3).transpose(0, 2, 1, 3, 4).reshape(D, 1024))
    arrays["w_kr"] = np.ascontiguousarray(np.repeat(arrays["w_in_2"][:, :, None, IN_W - QK_ROPE:], 2, 2).reshape(DEPTH, D, P))
    arrays["tables"] = make_tables()
    return arrays


def kernel(**inputs):
    import concourse.bacc as bacc
    from concourse.bass_utils import run_bass_kernel_spmd

    nc = bacc.Bacc("TRN2", target_bir_lowering=False, num_devices=1)
    arrays = lay_out(inputs)
    a = {k: nc.dram_tensor(f"in_{k}", x.shape, mybir.dt.from_np(x.dtype), kind="ExternalInput").ap() for k, x in arrays.items()}
    out = nc.dram_tensor("out_x", (1, S, D), F32, kind="ExternalOutput").ap()
    build(nc, a, out)
    r = run_bass_kernel_spmd(nc, [{f"in_{k}": x for k, x in arrays.items()}], core_ids=[0])
    return r.results[0]["out_x"]
```

```python
from contextlib import ExitStack, contextmanager

import numpy as np
import concourse.bass as bass
from concourse import mybir

F32 = mybir.dt.float32
F32R = mybir.dt.float32r
ALU = mybir.AluOpType
ACT = mybir.ActivationFunctionType
AXX = mybir.AxisListType.X
ds = bass.ds

P = 128
D = 1024
KD = D // P
S = 256
C = 256
T = S + C
LAT, CTX = slice(0, S), slice(S, T)
GROUPS = (LAT, CTX)
DEPTH = 2
FF = 2816
FT = FF // P
HALVES = ((0, 12), (12, 10))
GRID_W = 64
ROWS = S // GRID_W
HEADS = 16
HD = 64
NA_KH, NA_KW = 8, 16
RPB_PAD = 48
RPB_W = 2 * NA_KW - 1 + 2 * RPB_PAD
ALPHA = float((2 * DEPTH) ** 0.25)
LN_EPS, RMS_EPS = 1e-5, 1e-6
NEG = -1e30
RING = 4
AHEAD = 3
UNIT = 1024

IN_W = 1216
N_EXP = 16
CAP = 32
D_EXP = 512
QK_NOPE, QK_ROPE = 128, 64
MLA_HEADS = 4
QK_DIM = QK_NOPE + QK_ROPE


def table_layout():
    at, out = 0, {}
    for name, width in (("ident", P), ("mean_d", P), ("mean_256", P), ("mean_128", P), ("mean_192", P),
                        ("half0", P), ("half1", P), ("ones", P), ("rot", P), ("flip", P), ("cos", S),
                        ("sin", S), ("na_mask", GRID_W), ("wa_mask", 2 * S), ("dft_d", 2 * P),
                        ("dft_n", 4 * S), ("slots", CAP)):
        out[name] = (at, width)
        at += width
    return out, at


def make_tables():
    lay, width = table_layout()
    t = np.zeros((P, width), np.float32)

    def put(name, a):
        at, w = lay[name]
        t[:, at:at + w] = a

    p = np.arange(P)
    put("ident", np.eye(P))
    put("ones", 1.0)
    for name, n in (("mean_d", D), ("mean_256", 256), ("mean_128", 128), ("mean_192", QK_DIM)):
        put(name, 1.0 / n)
    for e in range(2):
        put(f"half{e}", np.repeat((p // HD == e)[:, None] / QK_DIM, P, 1))
    rot = np.zeros((P, P))
    for i in range(P):
        if i % 32 < 16:
            rot[i + 16, i] = -1.0
        else:
            rot[i - 16, i] = 1.0
    put("rot", rot)
    flip = np.zeros((P, P))
    flip[p, (p // GRID_W) * GRID_W + GRID_W - 1 - p % GRID_W] = 1.0
    put("flip", flip)
    tok = np.arange(S)
    freq = 10000.0 ** (-(p % 16) / 16.0)
    pos = np.where((p % HD < 32)[:, None], (tok // GRID_W)[None, :], (tok % GRID_W)[None, :])
    put("cos", np.cos(pos * freq[:, None]))
    put("sin", np.sin(pos * freq[:, None]))
    qc = GRID_W - 1 - p % GRID_W
    start = np.clip(qc - NA_KW // 2, 0, GRID_W - NA_KW)
    kc = np.arange(GRID_W)
    put("na_mask", np.where((kc >= start[:, None]) & (kc < start[:, None] + NA_KW), 0.0, NEG))
    put("wa_mask", np.concatenate([np.where(np.abs(i * P + p[:, None] - tok) <= 128, 0.0, NEG) for i in range(2)], 1))
    d = np.arange(HD)
    ang = 2 * np.pi * np.outer(d, d) / HD
    blk = np.zeros((P, 2 * P))
    for g in range(2):
        blk[g * HD:(g + 1) * HD, g * HD:(g + 1) * HD] = np.cos(ang) / 8
        blk[g * HD:(g + 1) * HD, P + g * HD:P + (g + 1) * HD] = -np.sin(ang) / 8
    put("dft_d", blk)
    ang = 2 * np.pi * ((tok[:, None] * tok[None, :]) % S) / S
    cs = np.stack([np.cos(ang), np.sin(ang)], 0) / 16
    put("dft_n", cs.reshape(2, 2, P, S).transpose(2, 0, 1, 3).reshape(P, 4 * S))
    put("slots", np.arange(CAP)[None, :])
    return t


VEC_TILES = (
    (("b_mod0", 72), ("c", 8), ("c_ctx", 8), ("c_2", 8), ("c_ctx_2", 8)),
    (("b_mod1", 72), ("sgu", 4), ("qlora", 4), ("kvlora", 2)),
    (("b_ada", 96), ("qn", 2), ("kn", 2), ("qr", 2), ("kr", 2)),
    (("ln_g", 48), ("ln_b", 48)),
)
VEC = {}
for _i, _tile in enumerate(VEC_TILES):
    _row = 0
    for _name, _n in _tile:
        VEC[_name] = (_i, _row, _n)
        _row += _n


class Counts:

    def __init__(self, sems, start=()):
        self.sems, self.n, self.var, self.last = sems, dict(start), {}, None

    def sem(self, key):
        return self.sems[key.split(":")[0]]

    def value(self, key, more=0):
        return self.n.get(key, 0) + self.var.get(key, 0) + more

    def next(self, key, k=1):
        self.n[key] = self.n.get(key, 0) + k
        return self.sem(key), self.value(key)

    def peek(self, key, more=0):
        return self.sem(key), self.value(key, more)

    def filled(self, b):
        return self.sems[f"bank_ready{b}"], self.value(f"bank_read{b}")

    def mark(self, key, k=1):
        self.last = self.next(key, k)
        return self.last[0], k

    @contextmanager
    def loop(self, eng, reps, strides):
        self.settle(eng)
        if reps == 1:
            yield 0
            return
        before = dict(self.n)
        with eng.Fori(0, reps) as i:
            self.var = {key: i * k for key, k in strides.items()}
            yield i
            self.settle(eng)
        self.var = {}
        for key, n in self.n.items():
            grown = n - before.get(key, 0)
            assert grown == strides.get(key, 0), (key, grown)
            self.n[key] = before.get(key, 0) + grown * reps

    def settle(self, eng):
        if self.last is not None:
            eng.wait_ge(*self.last)
        self.last = None


SEMS = (
    [f"raw_full{r}" for r in range(RING)]
    + ["hi_ready", "split_ready", "units_done"]
    + [f"bank_ready{b}" for b in range(8)]
    + [f"bank_read{b}" for b in range(8)]
    + ["act", "dve", "pe_passed", "act_passed",
       "zeroed", "inputs_loaded", "vec_ready", "cs_ready", "cond_ready", "mod_ready",
       "out_ready", "hm_ready", "scaled", "inverse_ready", "xhi_ready", "x_ready", "hidden_ready", "h_ready",
       "centered", "squared", "max_ready", "p_ready", "ao_hi", "stored",
       "bias_loaded", "bias_ready", "sink_ready", "sink_exp",
       "small_loaded", "ctx_loaded", "moe_in_ready", "q_ready", "ya_ready", "logits_moved", "softmax_in", "softmax_exp",
       "slots_ready", "slots_used", "est_hi", "est_ready", "gate_low", "gate_in", "gate_ready", "up_low", "hid_ready", "hidT_hi",
       "y_low", "y_stored", "y_free", "y_loaded"]
)



FIRST_BLOCKS = 6
RIDERS = (12, 18, 12, 12)


def ffn_loops(blocks):
    yield "up", 0, 0, 1, None
    done = 0
    for half, (_, nf) in enumerate(HALVES):
        for kind, first, reps in (("up", 1 - half, nf // 2), ("down", 0, KD // 2)):
            take = min(blocks - done, reps - first)
            if take:
                yield kind, half, first, take, done
                done += take
            if reps - first > take:
                yield kind, half, first + take, reps - first - take, None


N_LOADS = DEPTH + 4 + 2 + 1 + 2 + 1 + 6 + 4


def build(nc, a, out):
    lay, _ = table_layout()
    base = (nc.sbuf_base + 31) // 32 * 32
    top = [base]

    def at(name, shape, dt, offset):
        return nc.alloc_sbuf_tensor_at(name, shape, dt, offset=offset)

    def new(name, shape, dt=F32):
        t = at(name, shape, dt, top[0])
        top[0] += 4 * int(np.prod(shape[1:]))
        assert top[0] <= nc.sbuf_usable_end, (name, top[0], nc.sbuf_usable_end)
        return t

    raw = new("raw", [P, RING, UNIT])
    whi = new("whi", [P, RING, UNIT], F32R)
    wlo = new("wlo", [P, RING, UNIT], F32R)
    h = new("h", [P, KD, T])
    xin_at = top[0]
    xhi = new("xhi", [P, KD, T], F32R)
    xlo = new("xlo", [P, KD, T], F32R)
    big = top[0]
    top[0] += 64 * 1024
    tables = new("tables", [P, table_layout()[1]])
    vec = new("vec", [P, 4, P])
    mod = new("mod", [P, 3, 72, 2])
    cs = new("cs", [P, KD, 2])
    cond = new("cond", [P, KD, P], F32R)
    tmp = new("tmp", [P, 4, T])
    mt = new("mt", [P, 16])
    mb = new("mb", [P, KD, 2])
    small = new("small", [P, 64])
    eps_ln, eps_rms = small[:, 61:62], small[:, 62:63]
    sinks, nsinks = small[:, 8:24], small[:, 24:40]
    KB = 1024
    hsum = tmp[:, 3, :]
    vrow = at("vrow", [P, 4, P], F32, big)
    xtok = at("xtok", [P, 4, D], F32, big + 2 * KB)
    hhi = at("hhi", [P, 12, T], F32R, big)
    hlo = at("hlo", [P, 12, T], F32R, big + 24 * KB)
    hm = at("hm", [P, KD, T], F32, big + 48 * KB)
    mrow = at("mrow", [P, 512], F32, big + 48 * KB)
    aohi = at("aohi", [P, KD, T], F32R, big)
    aolo = at("aolo", [P, KD, T], F32R, big + 16 * KB)
    qS = at("qS", [P, 2, T], F32, big + 32 * KB)
    kS = at("kS", [P, T], F32, big + 36 * KB)
    vF = at("vF", [P, T], F32, big + 38 * KB)
    vS = at("vS", [P, 4, P], F32, big + 40 * KB)
    bt = [at(f"bt{i}", [P, 2, 2, S], F32, big + o * KB) for i, o in enumerate((42, 58))]
    prob = at("prob", [P, 2, T], F32, big + 46 * KB)
    pT = at("pT", [P, 2, 4, S], F32, big + 50 * KB)
    outT = at("outT", [P, 2, D], F32, big)
    px = at("px", [P, 10, T], F32, big)
    vtok = at("vtok", [P, 4, 2 * P], F32, big + 20 * KB)
    fd = at("fd", [P, 4, 4 * P], F32, big + 24 * KB)
    wsT = at("wsT", [P, 4, P], F32, big + 32 * KB)
    qn = at("qn", [P, 4, T], F32, big + 20 * KB)
    qr = at("qr", [P, 2, T], F32, big + 28 * KB)
    kn = at("kn", [P, 4, T], F32, big + 32 * KB)
    kr = at("kr", [P, 2, T], F32, big + 40 * KB)
    vt = at("vt", [P, 4, T], F32, big + 44 * KB)
    sq = at("sq", [P, 6, T], F32, big + 52 * KB)
    prob2 = at("prob2", [P, 2, T], F32, big + 52 * KB)
    pT2 = at("pT2", [P, 2, 4, S], F32, big + 56 * KB)
    xsT = at("xsT", [P, KD, N_EXP, 2 * CAP], F32, big)
    est = at("est", [P, KD, P], F32R, big + 32 * KB)
    hidT = at("hidT", [P, 4, P], F32R, big + 36 * KB)
    hid = at("hid", [P, D_EXP], F32, big + 38 * KB)
    ysb = at("ysb", [P, D], F32, big + 40 * KB)
    htok = at("htok", [P, 4, D], F32, xin_at)
    oh = at("oh", [P, 4, N_EXP, CAP], F32, xin_at + 16 * KB)
    ohw = at("ohw", [P, 4, N_EXP * CAP], F32, xin_at + 24 * KB)
    yp = at("yp", [P, 2, 4, D], F32, xin_at)
    small_at = top[0]
    wuq = new("wuq", [P, 2, 768])
    wukv = new("wukv", [P, D])
    wsgu = new("wsgu", [P, 4, P])
    bsgu = new("bsgu", [P, 4 * P])
    wr = new("wr", [P, KD, N_EXP])
    st = at("st", [P, 2, 4, S], F32, small_at)
    aff = new("aff", [P, 4, N_EXP])
    pos = new("pos", [P, 4, N_EXP])
    top8 = new("top8", [P, 8])
    yscr = nc.dram_tensor("y_scratch", (N_EXP, 2 * CAP, D), F32, kind="Internal").ap()

    def tab(name, *cols):
        at0, w = lay[name]
        return tables[:, at0:at0 + w] if not cols else tables[:, at0 + cols[0]:at0 + cols[1]]

    def v(name, i=0, n=None):
        tile, row, cnt = VEC[name]
        return vec[:, tile, row + i:row + i + (cnt - i if n is None else n)]

    MOD_IN = (0, 1, 0, 2)

    def mcol(m, j, k, g):
        return mod[:, MOD_IN[m], j * KD + k, g:g + 1]

    SHIFT1, SCALE1, GATE1, SHIFT2, SCALE2, GATE2, SHIFT3, SCALE3, GATE3 = range(9)

    with ExitStack() as ctx:
        s = {name: ctx.enter_context(nc.semaphore(name)) for name in SEMS}
        bank = [ctx.enter_context(nc.psum_tensor(f"bank{b}", [P, T], F32)) for b in range(8)]
        block = ctx.enter_context(nc.Block())
        BANKS = {f"bank_read{b}": 1 for b in range(8)}

        def heads_pair_plan(wa, buf=0):
            items, pvs, outs = [], {}, {}
            group = 0
            for qq in range(2 if wa else 1):
                for e in range(2):
                    rows = slice(e * HD, (e + 1) * HD)
                    for g in range(1 if wa else 2):
                        for tt in range(2):
                            t = 2 * g + tt
                            items.append(dict(
                                nk=4 if g == 0 else 2, key0=0 if g == 0 else S,
                                ops=[(qS[rows, qq, t * P:(t + 1) * P], kS[rows, 0 if g == 0 else S:T])],
                                bias=(None if g else (tab("ident"), tab("wa_mask", tt * S, (tt + 1) * S)) if wa
                                      else (tab("flip"), bt[buf][:, e, tt, :])),
                                wait_bias=(not wa and tt == 0), pg=group % 2, tt=tt, qhead=2 * qq + e, sink=wa))
                        m = len(items) - 1
                        v0 = 0 if g == 0 else 2
                        cols = slice(g * S, (g + 1) * S)
                        vc = slice(0, HD) if wa else rows
                        pvs.setdefault(m + 1, []).append(dict(
                            nk=items[-1]["nk"], pg=group % 2, v0=v0, vc=vc, out=(rows, cols),
                            new=(e == 0 and g == 0), done=(e == 1 and g == (0 if wa else 1))))
                        group += 1
                outs.setdefault(len(items), []).append(qq)
            n = len(items)
            last = {k: x for k, x in pvs.items() if k >= n}
            for k, x in last.items():
                pvs.setdefault(n - 1, []).extend(pvs.pop(k))
            last = {k: x for k, x in outs.items() if k >= n}
            for k in last:
                outs.setdefault(n - 1, []).extend(outs.pop(k))
            return items, pvs, outs, (LAT if wa else slice(0, T))

        def mla_plan(ctx_too):
            items, pvs, outs = [], {}, {}
            group = 0
            for hh in range(MLA_HEADS):
                rows = slice(hh % 2 * HD, hh % 2 * HD + HD)
                for g in range(2 if ctx_too else 1):
                    for tt in range(2):
                        q = slice((2 * g + tt) * P, (2 * g + tt + 1) * P)
                        keys = slice(0 if g == 0 else S, T)
                        items.append(dict(
                            nk=4 if g == 0 else 2, bias=None, wait_bias=False, pg=group % 2, tt=tt, sink=False,
                            ops=[(qn[:, hh, q], kn[:, hh, keys]), (qr[rows, hh // 2, q], kr[rows, hh // 2, keys])]))
                    pvs.setdefault(len(items), []).append(dict(
                        nk=items[-1]["nk"], pg=group % 2, v0=0 if g == 0 else 2, vc=slice(hh * P, (hh + 1) * P),
                        out=(slice(0, P), slice(g * S, (g + 1) * S)), new=(g == 0), done=(g == 1 or not ctx_too)))
                    group += 1
                outs.setdefault(len(items), []).append(hh)
            last = len(items) - 1
            for by_step in (pvs, outs):
                by_step.setdefault(last, []).extend(by_step.pop(last + 1, []))
            return items, pvs, outs, (slice(0, T) if ctx_too else LAT)

        NA, WA = [heads_pair_plan(False, buf) for buf in range(2)], heads_pair_plan(True)
        BLOCK1 = (prob, pT, vS, aohi, aolo)
        BLOCK2 = (prob2, pT2, vt, xhi, xlo)

        @block.sync
        def _(sp):
            n = Counts(s)
            unit_no = [0]

            def unit(src, width):
                slot = unit_no[0] % RING
                unit_no[0] += 1
                sp.wait_ge(*n.next("split_ready"))
                kt, cols = src.shape[1], src.shape[2]
                dst = raw[:, slot, 0:kt * cols].rearrange("p (k c) -> p k c", k=kt)
                sp.dma_start(dst, src).then_inc(s[f"raw_full{slot}"], 16)

            def blocks_of(w):
                return w.rearrange("(q k p) n -> q p k n", k=2, p=P)

            def mods(w, nblocks):
                view = blocks_of(w)
                with n.loop(sp, nblocks, dict(split_ready=4)) as i:
                    for q in range(4):
                        unit(view[q][:, :, ds(i * 512, 512)], 1024)

            def up_down(w_in, w_out, blocks, w, first):
                wi = w_in.rearrange("(k p) n -> p k n", p=P)
                wo = w_out.rearrange("(k p) n -> p k n", p=P)
                view = blocks_of(w)
                for kind, half, start, reps, m in ffn_loops(blocks):
                    f0, nf = HALVES[half]
                    with n.loop(sp, reps, dict(split_ready=4 if m is None else 8)) as i:
                        for q in range(4):
                            if m is not None:
                                unit(view[q][:, :, ds(i * 512 + (first + m) * 512, 512)], 1024)
                            if kind == "up":
                                f, part = q // 2, q % 2
                                unit(wi[:, :, ds(i * 256 + ((f0 + 2 * start + f) * P + part * FF), P)], 1024)
                            else:
                                d, part = q // 2, q % 2
                                k0 = f0 + part * (nf // 2)
                                unit(wo[:, k0:k0 + nf // 2, ds(i * 256 + (2 * start + d) * P, P)], nf // 2 * P)

            def columns(w, tiles):
                view = w.rearrange("(k p) n -> p k n", p=P)
                with n.loop(sp, tiles // 4, dict(split_ready=4)) as i:
                    for j in range(4):
                        unit(view[:, :, ds(i * 512 + j * P, P)], 1024)

            sp.wait_ge(*n.next("zeroed"))
            for l in range(DEPTH):
                b = a["b_mod"][l].rearrange("(r c) -> r c", c=P)
                tile, row, cnt = VEC[f"b_mod{l}"]
                sp.dma_start(vrow[row:row + cnt, tile, :], b).then_inc(s["inputs_loaded"], 16)
            for name in ("c", "c_ctx", "c_2", "c_ctx_2"):
                tile, row, cnt = VEC[name]
                src = a[name] if name in ("c_ctx", "c_ctx_2") else a[name][0]
                sp.dma_start(vrow[row:row + cnt, tile, :], src.rearrange("(r c) -> r c", c=P)).then_inc(s["inputs_loaded"], 16)
            for name, src in (("b_ada", a["b_ada_2"].rearrange("l (r c) -> (l r) c", c=P)), ("sgu", a["sgu_norm_2"].rearrange("l (r c) -> (l r) c", c=P)),
                              ("qlora", a["q_lora_norm_2"].rearrange("l (r c) -> (l r) c", c=P)), ("kvlora", a["kv_lora_norm_2"]),
                              ("qn", a["q_norm_2"][:, 0:P]), ("kn", a["k_norm_2"][:, 0:P])):
                tile, row, cnt = VEC[name]
                sp.dma_start(vrow[row:row + cnt, tile, :], src).then_inc(s["inputs_loaded"], 16)
            for name, src in (("qr", a["q_norm_2"][:, P:QK_DIM]), ("kr", a["k_norm_2"][:, P:QK_DIM])):
                tile, row, cnt = VEC[name]
                for e in range(2):
                    sp.dma_start(vrow[row:row + cnt, tile, e * HD:(e + 1) * HD], src).then_inc(s["inputs_loaded"], 16)
            for name in ("ln_g", "ln_b"):
                tile, row, cnt = VEC[name]
                sp.dma_start(vrow[row:row + cnt, tile, :], a[name].rearrange("l j (r c) -> (l j r) c", c=P)).then_inc(s["inputs_loaded"], 16)
            sp.dma_start(sinks, a["wa_sinks"][0].unsqueeze(0).broadcast_to([P, HEADS])).then_inc(s["inputs_loaded"], 16)
            sp.dma_start(tables[:, :], a["tables"]).then_inc(s["inputs_loaded"], 16)
            for g, name in enumerate(("x", "ctx")):
                sp.dma_start(xtok[:, 2 * g:2 * g + 2, :],
                             a[name][0].rearrange("(t p) d -> p t d", p=P)).then_inc(s["inputs_loaded"], 16)

            for l in range(DEPTH):
                if l == 0:
                    mods(a["w_mod"][0], FIRST_BLOCKS)
                    up_down(a["ffn_w_in"][0, 0], a["ffn_w_out"][0, 0], RIDERS[0], a["w_mod"][0], FIRST_BLOCKS)
                else:
                    up_down(a["ffn_w_in"][1, 0], a["ffn_w_out"][1, 0], RIDERS[2], a["w_ada_2"][0], 0)
                if l == 0:
                    w = a["na_w_qkv"][0].rearrange("(k p) n -> p k n", p=P)
                    with n.loop(sp, 2, dict(split_ready=12)) as i:
                        for j in range(4):
                            for part in range(3):
                                unit(w[:, :, ds(i * 512 + (j * P + part * D), P)], 1024)
                    columns(a["na_w_o"][0], KD)
                else:
                    w = a["wa_w_qkv"][0].rearrange("(k p) n -> p k n", p=P)
                    kv = a["wa_kv"].rearrange("(k p) n -> p k n", p=P)
                    with n.loop(sp, 4, dict(split_ready=4)) as i:
                        for part in range(2):
                            unit(kv[:, :, ds(i * 256 + part * P, P)], 1024)
                        for q in range(2):
                            unit(w[:, :, ds(i * 256 + q * P, P)], 1024)
                    columns(a["wa_w_o"][0], KD)
                up_down(a["ffn_w_in"][l, 1], a["ffn_w_out"][l, 1], RIDERS[2 * l + 1], a["w_ada_2"][1] if l else a["w_mod"][1], 0)
            for l in range(DEPTH):
                w = a["w_in_2"][l].rearrange("(k p) n -> p k n", p=P)
                for j in range(9):
                    unit(w[:, :, j * P:(j + 1) * P], 1024)
                unit(a["w_kr"][l].rearrange("(k p) n -> p k n", p=P), 1024)
                columns(a["w_out_2"][l], KD)
                wg, wu = (a[x][l].rearrange("e r f -> (e r) f") for x in ("w_gate_2", "w_up_2"))
                wd = a["w_down_2"][l].rearrange("e (k p) d -> k p e d", p=P)

                def gate_up(e):
                    for view in (wg, wu):
                        for q in range(4):
                            unit(view[ds(e * D + q * 2 * P, 2 * P), :].rearrange("(k p) f -> p k f", p=P), 1024)

                def down(e):
                    for k in range(4):
                        unit(wd[k][:, ds(e, 1), :], 1024)

                gate_up(0)
                with n.loop(sp, N_EXP - 1, dict(split_ready=12)) as i:
                    gate_up(i + 1)
                    down(i)
                down(N_EXP - 1)
            sp.wait_ge(*n.next("out_ready"))
            sp.dma_start(out[0].rearrange("(t p) d -> p t d", p=P), outT[:, :, :]).then_inc(s["stored"], 16)
            sp.wait_ge(*n.next("stored", 16))

        @block.tensor
        def _(pe):
            n = Counts(s, {"split_ready:use": RING})
            use_no = [0]
            pe.sem_inc(s["units_done"], RING)
            for b in range(8):
                pe.sem_inc(s[f"bank_read{b}"], 1)

            def acquire(b):
                pe.wait_ge(*n.next(f"bank_read{b}:free"))

            def evacuated(b):
                pe.wait_ge(*n.peek(f"bank_read{b}:free", 1))

            def passed():
                pe.sem_inc(s["pe_passed"], 1)

            def unit():
                slot = use_no[0] % RING
                use_no[0] += 1
                pe.wait_ge(*n.next("split_ready:use"))
                return slot

            def mods(nblocks):
                loop = {"split_ready:use": 4, "bank_read0:free": 1, "bank_read4:free": 1}
                with n.loop(pe, nblocks, loop):
                    acquire(0)
                    for q in range(4):
                        slot = unit()
                        for kk in range(2):
                            for part, w in enumerate((whi, wlo)):
                                mm = pe.matmul(bank[0][:, :], cond[:, 2 * q + kk, :], w[:, slot, kk * 512:(kk + 1) * 512],
                                               start=(q + kk + part == 0), stop=(q == 3 and kk == 1 and part == 1))
                        mm.then_inc(s["units_done"], 1)
                    acquire(4)
                    evacuated(0)
                    passed()
                    for j in range(4):
                        mm = pe.transpose(bank[4][:, 4 * j:4 * j + 4], mrow[0:4, j * P:(j + 1) * P], tab("ident")[0:4, 0:4])
                    mm.then_inc(s["bank_ready4"], 1)

            def product(b, slot, kt, k0, hi, lo, cols, first, last, x_wait=False):
                for k in range(kt):
                    if x_wait:
                        pe.wait_ge(*n.next("x_ready"))
                    wh, wl = (w[:, slot, k * P:(k + 1) * P] for w in (whi, wlo))
                    o = bank[b][:, cols]
                    pe.matmul(o, wh, hi[:, k0 + k, cols], start=(first and k == 0), stop=False)
                    pe.matmul(o, wh, lo[:, k0 + k, cols], start=False, stop=False)
                    mm = pe.matmul(o, wl, hi[:, k0 + k, cols], start=False, stop=(last and k == kt - 1))
                mm.then_inc(s["units_done"], 1)

            def mod_unit(q):
                if q == 0:
                    acquire(6)
                slot = unit()
                for kk in range(2):
                    for part, w in enumerate((whi, wlo)):
                        mm = pe.matmul(bank[6][:, :], cond[:, 2 * q + kk, :], w[:, slot, kk * 512:(kk + 1) * 512],
                                       start=(q + kk + part == 0), stop=(q == 3 and kk == 1 and part == 1))
                mm.then_inc(s["units_done"], 1)

            def mod_turn():
                acquire(7)
                evacuated(6)
                passed()
                for j in range(4):
                    mm = pe.transpose(bank[7][:, 4 * j:4 * j + 4], mrow[0:4, j * P:(j + 1) * P], tab("ident")[0:4, 0:4])
                    if j == 0:
                        mm.then_inc(s["bank_ready6"], 1)
                mm.then_inc(s["bank_ready7"], 1)

            def first_products(banks, cols, before):
                slots = []
                for b in banks:
                    acquire(b)
                    slots.append(unit())
                for k in range(KD):
                    pe.wait_ge(s["x_ready"], before + k + 1)
                    for b, slot in zip(banks, slots):
                        wh, wl = (w[:, slot, k * P:(k + 1) * P] for w in (whi, wlo))
                        o = bank[b][:, cols]
                        pe.matmul(o, wh, xhi[:, k, cols], start=(k == 0), stop=False)
                        pe.matmul(o, wh, xlo[:, k, cols], start=False, stop=False)
                        mm = pe.matmul(o, wl, xhi[:, k, cols], start=False, stop=(k == KD - 1))
                        if k == KD - 1:
                            mm.then_inc(s["units_done"], 1)

            def input_tiles():
                before = n.n.get("x_ready", 0)
                n.next("x_ready", KD)
                return before

            def up_down(cols, blocks, new_cond=False):
                before = input_tiles()
                for kind, half, start, reps, m in ffn_loops(blocks):
                    nf = HALVES[half][1]
                    m = m is not None
                    if kind == "down" and start == 0:
                        pe.wait_ge(*n.next("hidden_ready", nf))
                    used = [0, 1, 2, 3] if kind == "up" else [0, 1]
                    loop = {"split_ready:use": 8 if m else 4, **{f"bank_read{b}:free": 1 for b in used + [6, 7] * m}}
                    with n.loop(pe, reps, loop):
                        if kind == "up" and half == 0 and start == 0:
                            first_products(range(3), cols, before)
                            acquire(3)
                            product(3, unit(), KD, 0, xhi, xlo, cols, True, True)
                            if new_cond:
                                pe.wait_ge(*n.next("cond_ready"))
                            continue
                        for q in range(4):
                            if m:
                                mod_unit(q)
                            if kind == "up":
                                acquire(q)
                                product(q, unit(), KD, 0, xhi, xlo, cols, True, True)
                            else:
                                b, part = q // 2, q % 2
                                if part == 0:
                                    acquire(b)
                                product(b, unit(), nf // 2, part * (nf // 2), hhi, hlo, cols, part == 0, part == 1)
                        if m:
                            mod_turn()

            def layer_norm(cols):
                pe.wait_ge(*n.next("h_ready"))
                acquire(4)
                pe.matmul(bank[4][:, cols], tab("mean_d"), hsum[:, cols], start=True, stop=True).then_inc(s["bank_ready4"], 1)
                acquire(5)
                for k in range(KD):
                    pe.wait_ge(*n.next("squared"))
                    mm = pe.matmul(bank[5][:, cols], tab("mean_d"), hm[:, k, cols], start=(k == 0), stop=(k == KD - 1))
                mm.then_inc(s["bank_ready5"], 1)

            slots = {}

            def steps(products, m):
                todo = [(b, c, k) for b, c in products for k in range(KD)]
                each = len(products)
                for b, c, k in todo[m * each:(m + 1) * each]:
                    if k == 0:
                        acquire(b)
                        slots[b] = unit()
                    wh, wl = (w[:, slots[b], k * P:(k + 1) * P] for w in (whi, wlo))
                    o = bank[b][:, c]
                    pe.matmul(o, wh, xhi[:, k, c], start=(k == 0), stop=False)
                    pe.matmul(o, wh, xlo[:, k, c], start=False, stop=False)
                    mm = pe.matmul(o, wl, xhi[:, k, c], start=False, stop=(k == KD - 1))
                    if k == KD - 1:
                        mm.then_inc(s["units_done"], 1)

            def attend(plan, where=BLOCK1, out_bank=7, started=None, coming=()):
                items, pvs, outs, out_cols = plan
                prob, pT, values, out_hi, out_lo = where

                def score(m):
                    it = items[m]
                    b = 4 + m % 2
                    acquire(b)
                    nk = it["nk"] * P
                    ops = it["ops"]
                    for j, (lhs, rhs) in enumerate(ops):
                        mm = pe.matmul(bank[b][:, 0:nk], lhs, rhs, start=(j == 0), stop=(j == len(ops) - 1 and it["bias"] is None))
                    if it["bias"] is not None:
                        if it["wait_bias"]:
                            pe.wait_ge(*n.next("bias_ready"))
                        mm = pe.matmul(bank[b][:, 0:S], it["bias"][0], it["bias"][1], start=False, stop=True)
                    mm.then_inc(s[f"bank_ready{b}"], 1)

                score(0)
                score(1)
                if started:
                    started()
                for m, it in enumerate(items):
                    pe.wait_ge(*n.next("p_ready"))
                    acquire(6)
                    for kt in range(it["nk"]):
                        mm = pe.transpose(bank[6][:, kt * P:(kt + 1) * P], prob[:, m % 2, kt * P:(kt + 1) * P], tab("ident"))
                    mm.then_inc(s["bank_ready6"], 1)
                    if m + 2 < len(items):
                        score(m + 2)
                    steps(coming, m)
                    for pv in pvs.get(m, ()):
                        if m == len(items) - 1:
                            evacuated(6)
                        if pv["new"]:
                            acquire(out_bank)
                        rows, cols = pv["out"]
                        for kt in range(pv["nk"]):
                            mm = pe.matmul(bank[out_bank][rows, cols], values[:, pv["v0"] + kt, pv["vc"]], pT[:, pv["pg"], kt, :],
                                           start=(kt == 0), stop=(kt == pv["nk"] - 1), skip_group_check=True)
                        if pv["done"]:
                            mm.then_inc(s[f"bank_ready{out_bank}"], 1)

            def out_projection(cols):
                evacuated(7)
                with n.loop(pe, 2, {"split_ready:use": 4, **{f"bank_read{b}:free": 1 for b in range(4)}}):
                    for b in range(4):
                        acquire(b)
                        product(b, unit(), KD, 0, aohi, aolo, cols, True, True)

            pe.wait_ge(*n.next("inputs_loaded", N_LOADS * 16))
            acquire(4)
            for j in range(4):
                mm = pe.transpose(bank[4][:, j * P:(j + 1) * P], vrow[:, j, :], tab("ident"))
            mm.then_inc(s["bank_ready4"], 1)
            for k in range(KD):
                b = 5 + k % 2
                acquire(b)
                for t in range(4):
                    mm = pe.transpose(bank[b][:, t * P:(t + 1) * P], xtok[:, t, k * P:(k + 1) * P], tab("ident"))
                mm.then_inc(s[f"bank_ready{b}"], 1)
            pe.wait_ge(*n.next("cond_ready"))

            for l in range(DEPTH):
                ctx_too = l < DEPTH - 1
                cols = slice(0, T) if ctx_too else LAT
                if l == 0:
                    mods(FIRST_BLOCKS)
                up_down(slice(0, T), RIDERS[2 * l], new_cond=l > 0)
                layer_norm(slice(0, T))
                before = input_tiles()
                if l == 0:
                    triple = [(b, slice(0, T)) for b in range(3)]
                    first_products(range(3), slice(0, T), before)
                    for pair in range(KD):

                        def turn_values():
                            evacuated(2)
                            acquire(6)
                            for t in range(4):
                                mm = pe.transpose(bank[6][:, t * P:(t + 1) * P], vF[:, t * P:(t + 1) * P], tab("ident"))
                            mm.then_inc(s["bank_ready6"], 1)

                        evacuated(0)
                        evacuated(1)
                        attend(NA[pair % 2], started=turn_values, coming=triple if pair < KD - 1 else ())
                else:
                    four = [(0, slice(0, T)), (1, slice(0, T)), (2, LAT), (3, LAT)]

                    def key_head(coming):
                        evacuated(1)
                        acquire(6)
                        passed()
                        for t in range(4):
                            mm = pe.transpose(bank[6][:, t * P:t * P + HD], vF[0:HD, t * P:(t + 1) * P], tab("ident")[0:HD, 0:HD])
                        mm.then_inc(s["bank_ready6"], 1)
                        for j, (b, x) in enumerate(((0, kS[:, LAT]), (2, qS[:, 0, LAT]), (3, qS[:, 1, LAT]))):
                            evacuated(b)
                            rb = 4 + j % 2
                            acquire(rb)
                            pe.matmul(bank[rb][:, LAT], tab("rot"), x, start=True, stop=True).then_inc(s[f"bank_ready{rb}"], 1)
                        pe.wait_ge(*n.next("q_ready", 3))
                        pe.wait_ge(*n.peek("bank_read6:free", 1))
                        attend(WA, coming=coming)

                    first_products(range(2), slice(0, T), before)
                    for b in (2, 3):
                        acquire(b)
                        product(b, unit(), KD, 0, xhi, xlo, LAT, True, True)
                    loop = {"split_ready:use": 4, "bank_read0:free": 1, "bank_read1:free": 1, "bank_read2:free": 1,
                            "bank_read3:free": 1, "bank_read4:free": 4 + 2, "bank_read5:free": 4 + 1, "bank_read6:free": 8 + 1,
                            "bank_read7:free": 2, "p_ready": 8, "q_ready": 3}
                    with n.loop(pe, 3, loop):
                        key_head(four)
                    key_head(())
                out_projection(cols)
                layer_norm(cols)
                up_down(cols, RIDERS[2 * l + 1])
                layer_norm(cols)

            def small_product(b, pairs, o=slice(0, T), rows=slice(0, P), acq=True, ready=True):
                if acq:
                    acquire(b)
                for j, (lhs, rhs) in enumerate(pairs):
                    mm = pe.matmul(bank[b][rows, o], lhs, rhs, start=(j == 0), stop=(j == len(pairs) - 1), skip_group_check=True)
                if ready:
                    mm.then_inc(s[f"bank_ready{b}"], 1)

            def rms_stat(cols):
                acquire(5)
                for k in range(KD):
                    pe.wait_ge(*n.next("squared"))
                    mm = pe.matmul(bank[5][:, cols], tab("mean_d"), hm[:, k, cols], start=(k == 0), stop=(k == KD - 1))
                mm.then_inc(s["bank_ready5"], 1)

            def row_of(part):
                return tab("ident")[:, 32 * part:32 * part + 1].broadcast_to([P, P])

            pe.wait_ge(*n.next("ctx_loaded", 16))
            for k in range(KD):
                b = 4 + k % 2
                acquire(b)
                for t in range(2):
                    mm = pe.transpose(bank[b][:, t * P:(t + 1) * P], xtok[:, t, k * P:(k + 1) * P], tab("ident"))
                mm.then_inc(s[f"bank_ready{b}"], 1)
            for l in range(DEPTH):
                ctx_too = l < DEPTH - 1
                cols = slice(0, T) if ctx_too else LAT
                tts = range(4 if ctx_too else 2)
                rms_stat(slice(0, T))

                def fourier(i):
                    b = 4 + i
                    for g in range(len(tts) // 2):
                        for part in range(2):
                            for t in range(2):
                                mm = pe.matmul(bank[b][:, g * S:(g + 1) * S], fd[:, 2 * g + t, i * S + part * P:i * S + (part + 1) * P],
                                               tab("dft_n", (2 * part + t) * S, (2 * part + t + 1) * S),
                                               start=(part + t == 0), stop=(part + t == 2), skip_group_check=True)
                    mm.then_inc(s[f"bank_ready{b}"], 1)

                first_products(range(3), cols, input_tiles())
                for j in range(3, 10):
                    acquire(j % 4)
                    product(j % 4, unit(), KD, 0, xhi, xlo, cols if j < 8 else slice(0, T), True, True)
                pe.wait_ge(*n.next("small_loaded", 5 * 16))
                acquire(4)
                for part, (tiles, m) in enumerate(((2, "mean_256"), (2, "mean_256"), (1, "mean_128"))):
                    c = slice(0, T) if part == 2 else cols
                    for j in range(tiles):
                        pe.wait_ge(*n.next("squared"))
                        mm = pe.matmul(bank[4][32 * part:32 * part + 32, c], tab(m)[:, 0:32], sq[:, 2 * part + j, c],
                                       start=(j == 0), stop=(j == tiles - 1), skip_group_check=True)
                mm.then_inc(s["bank_ready4"], 1)
                acquire(7)
                for hh in range(4):
                    mm = pe.transpose(bank[7][:, hh * P:(hh + 1) * P], wsgu[:, hh, :], tab("ident"))
                mm.then_inc(s["bank_ready7"], 1)
                for tt in tts:
                    b = 6 + tt % 2
                    acquire(b)
                    for i in range(2):
                        mm = pe.matmul(bank[b][:, i * S:(i + 1) * S], px[:, 4 + i, tt * P:(tt + 1) * P], tab("dft_d"),
                                       start=True, stop=True, skip_group_check=True)
                    mm.then_inc(s[f"bank_ready{b}"], 1)
                pe.wait_ge(*n.next("inverse_ready"))
                for part in range(3):
                    small_product(5 + part, [(row_of(part)[0:96, :], tmp[0:96, 0, slice(0, T) if part == 2 else cols])],
                                  slice(0, T) if part == 2 else cols)
                acquire(4)
                fourier(0)
                for tt in tts:
                    b = 4 + tt % 2
                    acquire(b)
                    for i in range(2):
                        mm = pe.transpose(bank[b][:, i * P:(i + 1) * P], px[:, 2 + i, tt * P:(tt + 1) * P], tab("ident"))
                    mm.then_inc(s[f"bank_ready{b}"], 1)
                for tt in tts:
                    b = 4 + tt % 2
                    acquire(b)
                    if tt == 0:
                        evacuated(5)
                    for i in range(2):
                        o = bank[b][:, i * S:(i + 1) * S]
                        pe.matmul(o, vtok[:, tt, i * P:(i + 1) * P], wsT[:, 2 * i:2 * i + 2, :], start=True, stop=False, skip_group_check=True)
                        mm = pe.matmul(o, tab("ones")[0:1, :], bsgu[0:1, i * S:(i + 1) * S], start=False, stop=True, skip_group_check=True)
                    mm.then_inc(s[f"bank_ready{b}"], 1)
                acquire(5)
                fourier(1)
                for hh in range(4):
                    small_product(6 + hh % 2, [(wuq[:, k, hh * QK_DIM:hh * QK_DIM + P], px[:, 6 + k, cols]) for k in range(2)], cols)
                for i in range(2):
                    for e in range(2):
                        c0 = (2 * i + e) * QK_DIM + QK_NOPE
                        small_product(6 + i, [(wuq[:, k, c0:c0 + QK_ROPE], px[:, 6 + k, cols]) for k in range(2)], cols,
                                      slice(e * HD, (e + 1) * HD), e == 0, e == 1)
                for hh in range(4):
                    small_product(6 + hh % 2, [(wukv[:, hh * S:hh * S + P], px[:, 8, :])])
                for tt in range(4):
                    v_cols = wukv[:, :].rearrange("p (h c) -> p h c", c=S)[:, :, P:S]
                    small_product(6 + tt % 2, [(px[:, 8, tt * P:(tt + 1) * P], v_cols)])
                for side in range(2):
                    c = slice(0, T) if side else cols
                    pe.wait_ge(*n.next("squared", 5 if side else 6))
                    acquire(4 + side)
                    for hh in range(4):
                        r = sq[:, 4, c] if side else sq[:, 4 + hh // 2, c]
                        m = "half0" if side else f"half{hh % 2}"
                        small_product(4 + side, [(tab("mean_192")[:, 0:32], sq[:, hh, c]), (tab(m)[:, 0:32], r)], c,
                                      slice(32 * hh, 32 * hh + 32), False, hh == 3)
                for side in range(2):
                    c = slice(0, T) if side else cols
                    pe.wait_ge(*n.next("inverse_ready"))
                    for hh in range(4):
                        small_product(4 + hh, [(row_of(hh), tmp[:, side, c])], c)
                for j in range(4):
                    evacuated(4 + j)
                for j, x in enumerate((qr[:, 0, LAT], qr[:, 1, LAT], kr[:, 0, LAT], kr[:, 1, LAT])):
                    small_product(4 + j, [(tab("rot"), x)], LAT)
                pe.wait_ge(*n.next("q_ready", 4))
                attend(mla_plan(ctx_too), BLOCK2)
                for k in range(4):
                    pe.wait_ge(*n.next("x_ready"))
                evacuated(7)
                with n.loop(pe, 2, {"split_ready:use": 4, **{f"bank_read{b}:free": 1 for b in range(4)}}):
                    for b in range(4):
                        acquire(b)
                        product(b, unit(), KD, 0, xhi, xlo, cols, True, True)
                rms_stat(cols)
                pe.wait_ge(*n.next("moe_in_ready", KD))
                small_product(4, [(wr[:, k, :], hm[:, k, cols]) for k in range(KD)], cols, slice(0, N_EXP))
                for tt in tts:
                    for half in range(2):
                        b = 6 + half
                        acquire(b)
                        for j in range(4):
                            mm = pe.transpose(bank[b][:, j * P:(j + 1) * P], hm[:, half * 4 + j, tt * P:(tt + 1) * P], tab("ident"))
                        mm.then_inc(s[f"bank_ready{b}"], 1)
                    if tt == 0:
                        evacuated(4)
                        acquire(5)
                        for t2 in tts:
                            mm = pe.transpose(bank[5][:, t2 * N_EXP:(t2 + 1) * N_EXP], tmp[0:N_EXP, 0, t2 * P:(t2 + 1) * P], tab("ident")[0:N_EXP, 0:N_EXP])
                        mm.then_inc(s["bank_ready5"], 1)
                pe.wait_ge(*n.next("softmax_in"))
                acquire(4)
                for tt in tts:
                    mm = pe.transpose(bank[4][0:N_EXP, tt * P:(tt + 1) * P], aff[:, tt, :], tab("ident"))
                mm.then_inc(s["bank_ready4"], 1)
                pe.wait_ge(*n.next("slots_ready"))
                acquire(5)
                for tt in tts:
                    mm = pe.transpose(bank[5][:, tt * N_EXP:(tt + 1) * N_EXP], tmp[0:N_EXP, 2, tt * P:(tt + 1) * P], tab("ident")[0:N_EXP, 0:N_EXP])
                mm.then_inc(s["bank_ready5"], 1)
                pe.wait_ge(*n.next("slots_ready"))
                evacuated(6)
                evacuated(7)
                for g in range(len(tts) // 2):
                    for k in range(KD):
                        small_product(4 + k % 4, [(htok[:, 2 * g + t, k * P:(k + 1) * P], oh[:, 2 * g + t, :, :]) for t in range(2)])
                for g in range(len(tts) // 2):
                    for c2 in range(2):
                        b = 4 + c2
                        acquire(b)
                        for c in range(2):
                            for t in range(2):
                                o = c * S + t * P
                                mm = pe.transpose(bank[b][:, o:o + P], ohw[:, 2 * g + t, (2 * c2 + c) * P:(2 * c2 + c + 1) * P], tab("ident"))
                        mm.then_inc(s[f"bank_ready{b}"], 1)

                def up(b):
                    acquire(b)
                    for q in range(4):
                        slot = unit()
                        for kk in range(2):
                            for part, w in enumerate((whi, wlo)):
                                mm = pe.matmul(bank[b][:, :], est[:, 2 * q + kk, :], w[:, slot, kk * 512:(kk + 1) * 512],
                                               start=(q + kk + part == 0), stop=(q == 3 and kk == 1 and part == 1))
                        mm.then_inc(s["units_done"], 1)

                def turn():
                    pe.wait_ge(*n.next("hid_ready"))
                    acquire(4)
                    passed()
                    for j in range(4):
                        mm = pe.transpose(bank[4][:, j * 64:(j + 1) * 64], hid[0:64, j * P:(j + 1) * P], tab("ident")[0:64, 0:64])
                    mm.then_inc(s["bank_ready4"], 1)

                def down():
                    evacuated(4)
                    acquire(2)
                    acquire(3)
                    for k in range(4):
                        slot = unit()
                        for half in range(2):
                            for part, w in enumerate((whi, wlo)):
                                mm = pe.matmul(bank[2 + half][:, :], hidT[:, k, :], w[:, slot, half * 512:(half + 1) * 512],
                                               start=(k + part == 0), stop=(k == 3 and part == 1))
                        mm.then_inc(s["units_done"], 1)

                pe.wait_ge(*n.next("est_ready"))
                up(0)
                up(1)
                with n.loop(pe, N_EXP - 1, {"split_ready:use": 12, **{f"bank_read{b}:free": 1 for b in range(5)}, "est_ready": 1, "hid_ready": 1}):
                    pe.wait_ge(*n.next("est_ready"))
                    up(0)
                    turn()
                    up(1)
                    down()
                turn()
                down()
                pe.wait_ge(*n.next("y_loaded", 16 * 2 * len(tts)))
                for k in range(KD):
                    b = 4 + k % 4
                    acquire(b)
                    for g in range(len(tts) // 2):
                        for c in range(4):
                            mm = pe.matmul(bank[b][:, g * S:(g + 1) * S], yp[:, g, c, k * P:(k + 1) * P], st[:, g, c, :],
                                           start=(c == 0), stop=(c == 3), skip_group_check=True)
                    mm.then_inc(s[f"bank_ready{b}"], 1)

            pe.wait_ge(*n.next("h_ready", 7))
            for t in range(2):
                for half in range(2):
                    b = 4 + half
                    acquire(b)
                    for j in range(4):
                        k = half * 4 + j
                        mm = pe.transpose(bank[b][:, j * P:(j + 1) * P], h[:, k, t * P:(t + 1) * P], tab("ident"))
                    mm.then_inc(s[f"bank_ready{b}"], 1)

        @block.scalar
        def _(act):
            n = Counts(s, {"units_done": RING, **BANKS})
            split_no = [0]
            left = [-1]

            def own():
                if n.last is not None:
                    act.wait_ge(*n.last)

            def passed():
                act.sem_inc(s["act_passed"], 1)

            def split():
                if left[0] == 0:
                    return
                left[0] -= 1
                slot = split_no[0] % RING
                split_no[0] += 1
                act.wait_ge(*n.next(f"raw_full{slot}", 16))
                act.wait_ge(*n.next("units_done:free"))
                act.activation(whi[:, slot, :], raw[:, slot, :], ACT.Copy).then_inc(*n.mark("hi_ready"))

            def units(k):
                for _ in range(k):
                    split()
                act.wait_ge(*n.next("units_done", k))

            SPLIT4 = {**{f"raw_full{r}": 16 for r in range(RING)}, "units_done:free": 4, "units_done": 4, "hi_ready": 4}

            def strides(times=1, **more):
                return {**{k: x * times for k, x in SPLIT4.items()}, **more}

            def condition(name):
                tile, row, cnt = VEC[name]
                src = vec[:, tile, row:row + 2 * KD].rearrange("p (g k) -> p k g", g=2)
                own()
                act.activation(cs[:, :, :], src, ACT.Silu).then_inc(*n.mark("cs_ready"))

            def mods(nblocks):
                with n.loop(act, nblocks, strides(bank_read0=1, bank_read4=1)):
                    units(4)
                    act.activation(mrow[0:4, :], bank[0][0:4, :], ACT.Copy).then_inc(*n.mark("bank_read0"))
                    n.next("bank_read4")

            def split_input():
                for k in range(KD):
                    act.wait_ge(*n.next("hm_ready"))
                    act.activation(xhi[:, k, :], hm[:, k, :], ACT.Copy).then_inc(*n.mark("xhi_ready"))

            def mod_row():
                act.activation(mrow[0:4, :], bank[6][0:4, :], ACT.Copy).then_inc(*n.mark("bank_read6"))
                n.next("bank_read7")

            def input_of(src, scale, bias, cols, split_too=True):
                groups = [(g, c) for g, c in enumerate(GROUPS) if c.start < cols.stop]
                written = []
                for k in range(KD + 1):
                    if k < KD:
                        act.wait_ge(*n.next("scaled"))
                        for g, c in groups:
                            x = 1.0 if scale is None else scale(k, g)
                            act.activation(hm[:, k, c], src[:, k, c], ACT.Identity, bias=bias(k, g), scale=x)\
                                .then_inc(*n.mark("act" if split_too or (g, c) != groups[-1] else "moe_in_ready"))
                        written.append(n.peek("act"))
                    if k and split_too:
                        act.wait_ge(*written[k - 1])
                        act.activation(xhi[:, k - 1, :], hm[:, k - 1, :], ACT.Copy).then_inc(*n.mark("xhi_ready"))

            def modulated(m, scale):
                input_of(h, lambda k, g: mcol(m, scale, k, g), lambda k, g: mb[:, k, g:g + 1], slice(0, T))

            def up_down(cols, blocks):
                for kind, half, start, reps, m in ffn_loops(blocks):
                    m = m is not None
                    used = [0, 1, 2, 3] if kind == "up" else [0, 1]
                    with n.loop(act, reps, strides(1 + m, **{f"bank_read{b}": 1 for b in used + [6, 7] * m})):
                        for f in range(2):
                            if m and f:
                                units(3)
                                mod_row()
                                units(1)
                            else:
                                units(4 if m else 2)
                            if kind == "up":
                                act.activation(tmp[:, f, cols], bank[2 * f][:, cols], ACT.Silu).then_inc(*n.mark(f"bank_read{2 * f}"))
                                n.next(f"bank_read{2 * f + 1}")
                            else:
                                n.next(f"bank_read{f}")

            def layer_norm(cols):
                n.next("bank_read4")
                for k in range(KD):
                    act.wait_ge(*n.next("centered"))
                    act.activation(hm[:, k, cols], h[:, k, cols], ACT.Square).then_inc(*n.mark("squared"))
                act.wait_ge(*n.filled(5))
                act.activation(tmp[:, 0, cols], bank[5][:, cols], ACT.Sqrt, bias=eps_ln).then_inc(*n.mark("bank_read5"))

            def coming_units(k):
                def after(m):
                    if k and m in ((3, 6) if k == 3 else (2, 4, 6)):
                        units(1)
                    if k and m == 7:
                        split()
                return after

            def attend(plan, out_tile, where=BLOCK1, out_bank=7, after=lambda m: None):
                items, pvs, outs, out_cols = plan
                prob, pT, values, out_hi, out_lo = where

                def exp(m):
                    it = items[m]
                    b = 4 + m % 2
                    act.wait_ge(*n.next("max_ready"))
                    own()
                    nk = it["nk"] * P
                    act.activation(prob[:, m % 2, 0:nk], bank[b][:, 0:nk], ACT.Exp, bias=small[:, m % 2:m % 2 + 1],
                                   accum_out=small[:, 2 + m % 2:3 + m % 2]).then_inc(*n.mark(f"bank_read{b}"))
                    if it["sink"]:
                        own()
                        passed()
                        act.activation(small[:, 4 + m % 2:5 + m % 2], sinks[:, ds(it["qhead"] + out_tile(0) * 2, 1)], ACT.Exp,
                                       bias=small[:, m % 2:m % 2 + 1]).then_inc(*n.mark("sink_exp"))

                exp(0)
                exp(1)
                for m, it in enumerate(items):
                    act.wait_ge(*n.filled(6))
                    src = bank[6][:, 0:it["nk"] * P].rearrange("p (k q) -> p k q", q=P)
                    act.activation(pT[:, it["pg"], 0:it["nk"], it["tt"] * P:(it["tt"] + 1) * P], src, ACT.Copy)\
                        .then_inc(*n.mark("bank_read6"))
                    if m + 2 < len(items):
                        exp(m + 2)
                    after(m)
                    for qq in outs.get(m, ()):
                        act.wait_ge(*n.filled(out_bank))
                        cols = out_cols
                        passed()
                        act.activation(out_hi[:, ds(out_tile(qq), 1), cols], bank[out_bank][:, cols].unsqueeze(1), ACT.Copy)\
                            .then_inc(*n.mark("ao_hi"))
                        n.next(f"bank_read{out_bank}")

            def out_projection():
                with n.loop(act, 2, strides(**{f"bank_read{b}": 1 for b in range(4)})):
                    for b in range(4):
                        units(1)
                        n.next(f"bank_read{b}")

            act.wait_ge(*n.next("vec_ready"))
            n.next("bank_read4")
            for b in (5, 6):
                n.next(f"bank_read{b}", 4)
            condition("c")
            for _ in range(AHEAD):
                split()
            for l in range(DEPTH):
                ctx_too = l < DEPTH - 1
                cols = slice(0, T) if ctx_too else LAT
                if l == 0:
                    mods(FIRST_BLOCKS)
                    split_input()
                else:
                    modulated(1, SCALE1)
                    condition("c_2")
                up_down(slice(0, T), RIDERS[2 * l])
                layer_norm(slice(0, T))
                modulated(l, SCALE2)
                if l == 0:
                    units(3)
                    for pair in range(KD):
                        more = pair < KD - 1
                        act.activation(qS[:, 0, :], bank[0][:, :], ACT.Copy, scale=HD ** -0.5).then_inc(*n.mark("bank_read0"))
                        n.next("bank_read1")
                        act.activation(vF[:, :], bank[2][:, :], ACT.Copy).then_inc(*n.mark("bank_read2"))
                        n.next("bank_read6")
                        attend(NA[pair % 2], lambda qq: pair, after=coming_units(3 * more))
                        if more:
                            act.wait_ge(*n.next("units_done"))
                else:
                    def key_head(i, k):
                        act.activation(kS[:, :], bank[0][:, :], ACT.Copy).then_inc(*n.mark("bank_read0"))
                        act.activation(vF[:, :], bank[1][:, :], ACT.Copy).then_inc(*n.mark("bank_read1"))
                        for q in range(2):
                            act.activation(qS[:, q, LAT], bank[2 + q][:, LAT], ACT.Copy, scale=HD ** -0.5)\
                                .then_inc(*n.mark(f"bank_read{2 + q}"))
                        n.next("bank_read4", 2)
                        n.next("bank_read5")
                        n.next("bank_read6")
                        attend(WA, lambda qq: i * 2 + qq, after=coming_units(k))
                        if k:
                            act.wait_ge(*n.next("units_done"))

                    more = {"bank_read0": 1, "bank_read1": 1, "bank_read2": 1, "bank_read3": 1, "bank_read4": 6,
                            "bank_read5": 5, "bank_read6": 9, "bank_read7": 2,
                            "max_ready": 8, "ao_hi": 2, "sink_exp": 8}
                    units(4)
                    with n.loop(act, 3, strides(1, **more)) as i:
                        key_head(i, 4)
                    key_head(3, 0)
                out_projection()
                layer_norm(cols)
                modulated(l, SCALE3)
                up_down(cols, RIDERS[2 * l + 1])
                layer_norm(cols)

            def rms_stat(cols):
                act.wait_ge(*n.next("h_ready"))
                for k in range(KD):
                    act.activation(hm[:, k, cols], h[:, k, cols], ACT.Square).then_inc(*n.mark("squared"))
                act.wait_ge(*n.filled(5))
                act.activation(tmp[:, 0, cols], bank[5][:, cols], ACT.Sqrt, bias=eps_rms).then_inc(*n.mark("bank_read5"))

            def square(j, x, c):
                act.activation(sq[:, j, c], x, ACT.Square).then_inc(*n.mark("squared"))

            def root(b, j, c):
                act.wait_ge(*n.filled(b))
                act.activation(tmp[:, j, c], bank[b][:, c], ACT.Sqrt, bias=eps_rms).then_inc(*n.mark(f"bank_read{b}"))

            def copy(b, dst, src):
                act.wait_ge(*n.filled(b))
                act.activation(dst, src, ACT.Copy).then_inc(*n.mark(f"bank_read{b}"))

            n.next("h_ready", 7)
            for b in (4, 5):
                n.next(f"bank_read{b}", 4)
            for l in range(DEPTH):
                ctx_too = l < DEPTH - 1
                cols = slice(0, T) if ctx_too else LAT
                tts = range(4 if ctx_too else 2)
                rms_stat(slice(0, T))
                input_of(hm, None, lambda k, g: mcol(2 + l, 0, k, g), slice(0, T))
                for j in range(10):
                    units(1)
                    c = cols if j < 8 else slice(0, T)
                    act.activation(px[:, j, c], bank[j % 4][:, c], ACT.Gelu_apprx_tanh if j < 4 else ACT.Copy)\
                        .then_inc(*n.mark(f"bank_read{j % 4}"))
                own()
                for j, t in enumerate((2, 3, 6, 7, 8)):
                    c = cols if t < 8 else slice(0, T)
                    square(j, px[:, t, c], c)
                act.wait_ge(*n.filled(4))
                if ctx_too:
                    act.activation(tmp[0:96, 0, :], bank[4][0:96, :], ACT.Sqrt, bias=eps_rms[0:96, :]).then_inc(*n.mark("bank_read4"))
                else:
                    act.activation(tmp[64:96, 0, CTX], bank[4][64:96, CTX], ACT.Sqrt, bias=eps_rms[64:96, :]).then_inc(*n.mark("act"))
                    act.activation(tmp[0:96, 0, LAT], bank[4][0:96, LAT], ACT.Sqrt, bias=eps_rms[0:96, :]).then_inc(*n.mark("bank_read4"))
                n.next("bank_read7")
                for tt in tts:
                    copy(6 + tt % 2, fd[:, tt, :], bank[6 + tt % 2][:, :])
                for b in (5, 6, 7):
                    n.next(f"bank_read{b}")
                act.wait_ge(*n.filled(4))
                act.activation(xhi[:, 2, cols], bank[4][:, cols], ACT.Copy).then_inc(*n.mark("xhi_ready"))
                n.next("bank_read4")
                for tt in tts:
                    n.next(f"bank_read{4 + tt % 2}", 2)
                act.wait_ge(*n.filled(5))
                act.activation(xhi[:, 3, cols], bank[5][:, cols], ACT.Copy).then_inc(*n.mark("xhi_ready"))
                n.next("bank_read5")
                act.wait_ge(*n.next("ya_ready"))
                for i in range(2):
                    act.activation(xhi[:, i, cols], px[:, i, cols], ACT.Copy).then_inc(*n.mark("xhi_ready"))
                for hh in range(4):
                    copy(6 + hh % 2, qn[:, hh, cols], bank[6 + hh % 2][:, cols])
                for i in range(2):
                    copy(6 + i, qr[:, i, cols], bank[6 + i][:, cols])
                for b in (6, 7):
                    n.next(f"bank_read{b}", 4)
                own()
                for hh in range(4):
                    square(hh, qn[:, hh, cols], cols)
                for i in range(2):
                    square(4 + i, qr[:, i, cols], cols)
                root(4, 0, cols)
                for b in (6, 7):
                    act.wait_ge(*n.peek(f"bank_read{b}"))
                for hh in range(4):
                    square(hh, kn[:, hh, :], slice(0, T))
                square(4, px[:, 9, :], slice(0, T))
                root(5, 1, slice(0, T))
                for b in range(4, 8):
                    n.next(f"bank_read{b}", 3)
                attend(mla_plan(ctx_too), lambda hh: 4 + hh, BLOCK2)
                with n.loop(act, 2, strides(**{f"bank_read{b}": 1 for b in range(4)})):
                    for b in range(4):
                        units(1)
                        n.next(f"bank_read{b}")
                rms_stat(cols)
                input_of(hm, None, lambda k, g: mcol(2 + l, 3, k, g), cols, False)
                n.next("bank_read4")
                for tt in tts:
                    for b in (6, 7):
                        copy(b, htok[:, tt, (b - 6) * 512:(b - 5) * 512], bank[b][:, :])
                    if tt == 0:
                        n.next("bank_read5")
                act.wait_ge(*n.next("logits_moved"))
                nt = len(tts)
                act.activation(aff[:, 0:nt, :], aff[:, 0:nt, :], ACT.Exp).then_inc(*n.mark("softmax_exp"))
                for b in (4, 5):
                    n.next(f"bank_read{b}")
                for g in range(nt // 2):
                    for k in range(KD):
                        b = 4 + k % 4
                        if k % 2:
                            copy(b, xsT[:, k, :, g * CAP:(g + 1) * CAP], bank[b][:, :].rearrange("p (e s) -> p e s", s=CAP))
                        else:
                            n.next(f"bank_read{b}")
                for g in range(nt // 2):
                    for c2 in range(2):
                        copy(4 + c2, st[:, g, 2 * c2:2 * c2 + 2, :], bank[4 + c2][:, :].rearrange("p (c t) -> p c t", t=S))

                def tokens(e):
                    passed()
                    act.activation(est[:, :, 0:64].unsqueeze(2), xsT[:, :, ds(e, 1), :], ACT.Copy).then_inc(*n.mark("est_hi"))

                def hidden_high():
                    act.wait_ge(*n.filled(4))
                    act.activation(hidT[:, :, 0:64], bank[4][:, 0:256].rearrange("p (j c) -> p j c", c=64), ACT.Copy)\
                        .then_inc(*n.mark("hidT_hi"))
                    n.next("bank_read4")

                def gate(turned):
                    units(4)
                    act.activation(tmp[0:64, 0, :], bank[0][64:P, :], ACT.Copy).then_inc(*n.mark("gate_low"))
                    n.next("bank_read0")
                    act.wait_ge(*n.next("gate_in"))
                    act.activation(tmp[0:64, 1, :], tmp[0:64, 1, :], ACT.Silu).then_inc(*n.mark("gate_ready"))
                    if turned:
                        hidden_high()

                def up():
                    units(4)
                    act.activation(tmp[0:64, 2, :], bank[1][64:P, :], ACT.Copy).then_inc(*n.mark("up_low"))
                    n.next("bank_read1")

                def down():
                    units(4)
                    act.wait_ge(*n.next("y_free"))
                    for half in range(2):
                        act.activation(ysb[0:64, half * 512:(half + 1) * 512], bank[2 + half][64:P, :], ACT.Copy).then_inc(*n.mark("y_low"))
                        n.next(f"bank_read{2 + half}")

                grow = strides(3, est_hi=1, gate_low=1, gate_in=1, gate_ready=1, up_low=1, hidT_hi=1, y_low=2, y_free=1,
                               **{f"bank_read{b}": 1 for b in range(5)})
                act.wait_ge(*n.next("slots_used"))
                own()
                tokens(0)
                gate(False)
                up()
                tokens(1)
                with n.loop(act, N_EXP - 2, grow) as i:
                    gate(True)
                    up()
                    tokens(i + 2)
                    down()
                if l == DEPTH - 1:
                    left[0] = 16 - AHEAD
                gate(True)
                up()
                down()
                hidden_high()
                down()
                n.next("slots_used", N_EXP)
                for k in range(KD):
                    n.next(f"bank_read{4 + k % 4}")
                n.next("h_ready")

        @block.vector
        def _(dve):
            n = Counts(s, {"units_done": RING, "split_ready": RING, **BANKS})
            split_no = [0]
            left = [-1]
            dve.sem_inc(s["split_ready"], RING)

            def own():
                if n.last is not None:
                    dve.wait_ge(*n.last)

            def split():
                if left[0] == 0:
                    return
                left[0] -= 1
                slot = split_no[0] % RING
                split_no[0] += 1
                dve.wait_ge(*n.next("hi_ready"))
                dve.tensor_tensor(wlo[:, slot, :], raw[:, slot, :], whi[:, slot, :].bitcast(F32), ALU.subtract)\
                    .then_inc(*n.mark("split_ready"))

            def units(k):
                for _ in range(k):
                    split()
                dve.wait_ge(*n.next("units_done", k))

            def strides(times=1, **more):
                return {"hi_ready": 4 * times, "split_ready": 4 * times, "units_done": 4 * times, **more}

            def condition():
                dve.wait_ge(*n.next("cs_ready"))
                dve.tensor_copy(cond[:, :, 0:2], cs[:, :, :]).then_inc(*n.mark("dve"))
                own()
                dve.tensor_tensor(cond[:, :, 2:4], cs[:, :, :], cond[:, :, 0:2].bitcast(F32), ALU.subtract)\
                    .then_inc(*n.mark("cond_ready"))

            def mod_columns(b, m, j):
                dve.wait_ge(*n.filled(b))
                own()
                dve.tensor_copy(mt[:, :], bank[b][:, 0:16]).then_inc(*n.mark(f"bank_read{b}"))
                own()
                four = mt[:, :].rearrange("p (j r) -> p j r", r=4)
                dve.tensor_tensor(mod[:, MOD_IN[m], ds(j * 4, 4), :], four[:, :, 0:2], four[:, :, 2:4], ALU.add).then_inc(*n.mark("dve"))

            def mods(nblocks):
                with n.loop(dve, nblocks, strides(bank_read0=1, bank_read4=1, dve=1)) as i:
                    units(4)
                    n.next("bank_read0")
                    mod_columns(4, 0, i)

            def finish_mods(m, first, blocks, bias, plus_one=(), halved=()):
                x = mod[:, MOD_IN[m], 4 * first:4 * (first + blocks), :]
                b = bias[:, 4 * first:4 * (first + blocks)]
                own()
                dve.tensor_tensor(x, x, b.unsqueeze(2).broadcast_to([P, 4 * blocks, 2]), ALU.add).then_inc(*n.mark("dve"))
                for js, op, by in ((plus_one, ALU.add, 1.0), (halved, ALU.mult, 0.5)):
                    for j in js:
                        own()
                        x = mod[:, MOD_IN[m], j * KD:(j + 1) * KD, :]
                        dve.tensor_scalar(x, x, by, None, op).then_inc(*n.mark("dve"))

            def low(k):
                dve.wait_ge(*n.next("xhi_ready"))
                dve.tensor_tensor(xlo[:, k, :], hm[:, k, :], xhi[:, k, :].bitcast(F32), ALU.subtract).then_inc(*n.mark("x_ready"))

            def modulate(m, shift, scale):
                for k in range(KD + 1):
                    if k < KD:
                        for g, cols in enumerate(GROUPS):
                            own()
                            dve.tensor_scalar(hm[:, k, cols], h[:, k, cols], mcol(m, scale, k, g), mcol(m, shift, k, g),
                                              ALU.mult, ALU.add).then_inc(*n.mark("hm_ready" if g else "dve"))
                    if k:
                        low(k - 1)

            def scale_residual(cols, l, j):
                own()
                for k in range(KD):
                    if j is None:
                        dve.tensor_scalar(h[:, k, cols], h[:, k, cols], ALPHA, None, ALU.mult).then_inc(*n.mark("dve"))
                    else:
                        dve.tensor_scalar(h[:, k, cols], h[:, k, cols], v("ln_b", (l * 3 + j) * KD + k, 1), ALPHA, ALU.add, ALU.mult)\
                            .then_inc(*n.mark("dve"))

            def add_tile(k, cols):
                own()
                x = hsum[:, cols].unsqueeze(1)
                dve.tensor_tensor(x, x, h[:, ds(k, 1), cols], ALU.add).then_inc(*n.mark("dve"))

            def residual(b, m, gate, k, cols):
                groups = GROUPS if cols.stop == T else (LAT,)
                for g, gc in enumerate(groups):
                    own()
                    x = h[:, ds(k, 1), gc]
                    last = g == len(groups) - 1
                    dve.scalar_tensor_tensor(x, bank[b][:, gc].unsqueeze(1), mod[:, MOD_IN[m], ds(gate * KD + k, 1), g], x, ALU.mult, ALU.add)\
                        .then_inc(*n.mark(f"bank_read{b}" if last else "dve"))

            def up_down(cols, m, gate, blocks, to, first, norm):
                scale_residual(cols, *norm)
                more = 1 if cols.stop == T else 0
                for kind, half, start, reps, block in ffn_loops(blocks):
                    rides = block is not None
                    used = [0, 1, 2, 3] if kind == "up" else [0, 1]
                    adding = kind == "down" and half == 1
                    own_steps = 2 if kind == "up" else 2 * more + 2 * adding
                    if adding and start == 0:
                        own()
                        dve.memset(hsum[:, cols], 0.0).then_inc(*n.mark("dve"))
                    with n.loop(dve, reps, strides(1 + rides, dve=own_steps + rides, hidden_ready=2 if kind == "up" else 0,
                                                   **{f"bank_read{b}": 1 for b in used + [6, 7] * rides})) as i:
                        for f in range(2):
                            units(4 if rides else 2)
                            if rides and f:
                                n.next("bank_read6")
                            if kind == "down":
                                residual(f, m, gate, i * 2 + (2 * start + f), cols)
                                if adding:
                                    add_tile(i * 2 + (2 * start + f), cols)
                                continue
                            dve.wait_ge(*n.next(f"bank_read{2 * f}"))
                            dve.tensor_tensor(tmp[:, 2 + f, cols], tmp[:, f, cols], bank[2 * f + 1][:, cols], ALU.mult)\
                                .then_inc(*n.mark(f"bank_read{2 * f + 1}"))
                            own()
                            x = tmp[:, 2 + f, cols].unsqueeze(1)
                            hi, lo = (y[:, ds(i * 2 + (2 * start + f), 1), cols] for y in (hhi, hlo))
                            dve.tensor_copy(hi, x).then_inc(*n.mark("dve"))
                            own()
                            dve.tensor_tensor(lo, x, hi.bitcast(F32), ALU.subtract).then_inc(*n.mark("hidden_ready"))
                        if rides:
                            mod_columns(7, to, i + (first + block))
                own()
                dve.sem_inc(*n.mark("h_ready"))

            def layer_norm(cols, l, j, then=None, finish=None):
                n.next("bank_read5")
                dve.wait_ge(*n.filled(4))
                own()
                dve.tensor_copy(tmp[:, 1, cols], bank[4][:, cols]).then_inc(*n.mark("bank_read4"))
                own()
                for k in range(KD):
                    dve.tensor_tensor(h[:, k, cols], h[:, k, cols], tmp[:, 1, cols], ALU.subtract).then_inc(*n.mark("centered"))
                if finish:
                    finish()
                i = (l * 3 + j) * KD
                if then:
                    m, shift, scale = then
                    bias = v("ln_b", i, KD).unsqueeze(2).broadcast_to([P, KD, 2])
                    own()
                    dve.tensor_tensor(mb[:, :, :], bias, mod[:, MOD_IN[m], scale * KD:(scale + 1) * KD, :], ALU.mult).then_inc(*n.mark("dve"))
                    own()
                    dve.tensor_tensor(mb[:, :, :], mb[:, :, :], mod[:, MOD_IN[m], shift * KD:(shift + 1) * KD, :], ALU.add)\
                        .then_inc(*n.mark("dve"))
                own()
                dve.wait_ge(*n.peek("bank_read5"))
                dve.reciprocal(tmp[:, 1, cols], tmp[:, 0, cols]).then_inc(*n.mark("dve"))
                own()
                if then:
                    scaled_and_low(lambda k: dve.scalar_tensor_tensor(
                        h[:, k, cols], h[:, k, cols], v("ln_g", i + k, 1), tmp[:, 1, cols], ALU.mult, ALU.mult).then_inc(*n.mark("scaled")))
                else:
                    for k in range(KD):
                        dve.scalar_tensor_tensor(h[:, k, cols], h[:, k, cols], v("ln_g", i + k, 1), tmp[:, 1, cols], ALU.mult, ALU.mult)\
                            .then_inc(*n.mark("dve"))
                    own()
                    for k in range(KD):
                        dve.tensor_scalar(h[:, k, cols], h[:, k, cols], v("ln_b", i + k, 1), None, ALU.add).then_inc(*n.mark("dve"))

            def scaled_and_low(scaled):
                for k in range(KD + 2):
                    if k < KD:
                        scaled(k)
                    if k > 1:
                        low(k - 2)

            def coming_units(k):
                def after(m):
                    if k and m in ((3, 6) if k == 3 else (2, 4, 6)):
                        units(1)
                    if k and m == 7:
                        split()
                return after

            def attend(plan, out_tile, where=BLOCK1, out_bank=7, started=None, after=lambda m: None):
                items, pvs, outs, out_cols = plan
                prob, pT, values, out_hi, out_lo = where

                def most(m):
                    it = items[m]
                    b = 4 + m % 2
                    dve.wait_ge(*n.filled(b))
                    own()
                    x = small[:, m % 2:m % 2 + 1]
                    dve.tensor_reduce(x, bank[b][:, 0:it["nk"] * P], AXX, ALU.max, negate=True)\
                        .then_inc(*n.mark("dve" if it["sink"] else "max_ready"))
                    if it["sink"]:
                        own()
                        dve.tensor_tensor(x, x, nsinks[:, ds(it["qhead"] + out_tile(0) * 2, 1)], ALU.min).then_inc(*n.mark("max_ready"))

                def normalise(m):
                    it = items[m]
                    dve.wait_ge(*n.next(f"bank_read{4 + m % 2}"))
                    total = small[:, 2 + m % 2:3 + m % 2]
                    own()
                    if it["sink"]:
                        dve.wait_ge(*n.next("sink_exp"))
                        dve.tensor_tensor(total, total, small[:, 4 + m % 2:5 + m % 2], ALU.add).then_inc(*n.mark("dve"))
                        own()
                    dve.reciprocal(total, total).then_inc(*n.mark("dve"))
                    own()
                    x = prob[:, m % 2, 0:it["nk"] * P]
                    dve.tensor_scalar(x, x, total, None, ALU.mult).then_inc(*n.mark("p_ready"))

                most(0)
                most(1)
                if started:
                    started()
                for m, it in enumerate(items):
                    normalise(m)
                    n.next("bank_read6")
                    if m + 2 < len(items):
                        most(m + 2)
                    after(m)
                    for qq in outs.get(m, ()):
                        cols = out_cols
                        dve.wait_ge(*n.next("ao_hi"))
                        dve.tensor_tensor(out_lo[:, ds(out_tile(qq), 1), cols], bank[out_bank][:, cols].unsqueeze(1),
                                          out_hi[:, ds(out_tile(qq), 1), cols].bitcast(F32), ALU.subtract)\
                            .then_inc(*n.mark(f"bank_read{out_bank}"))

            def rotate(b, x):
                dve.wait_ge(*n.filled(b))
                own()
                dve.tensor_tensor(tmp[:, 1, LAT], bank[b][:, LAT], tab("sin"), ALU.mult).then_inc(*n.mark(f"bank_read{b}"))
                own()
                dve.tensor_tensor(x, x, tab("cos"), ALU.mult).then_inc(*n.mark("dve"))
                own()
                dve.tensor_tensor(x, x, tmp[:, 1, LAT], ALU.add).then_inc(*n.mark("q_ready"))

            def out_projection(cols, m):
                scale_residual(cols, m, 0)
                dve.memset(hsum[:, cols], 0.0).then_inc(*n.mark("dve"))
                more = 1 if cols.stop == T else 0
                with n.loop(dve, 2, strides(dve=4 * more + 4, **{f"bank_read{b}": 1 for b in range(4)})) as i:
                    for b in range(4):
                        units(1)
                        residual(b, m, GATE2, i * 4 + b, cols)
                        add_tile(i * 4 + b, cols)
                own()
                dve.sem_inc(*n.mark("h_ready"))

            dve.memset(cond[:, :, :].bitcast(F32), 0.0).then_inc(*n.mark("dve"))
            dve.memset(eps_ln, LN_EPS).then_inc(*n.mark("dve"))
            dve.memset(eps_rms, RMS_EPS).then_inc(*n.mark("dve"))
            dve.wait_ge(*n.filled(4))
            own()
            dve.tensor_copy(vec[:, :, :], bank[4][:, :].rearrange("p (j c) -> p j c", c=P)).then_inc(*n.mark("bank_read4"))
            own()
            dve.tensor_scalar(nsinks[:, :], sinks[:, :], -1.0, None, ALU.mult).then_inc(*n.mark("vec_ready"))
            for k in range(KD):
                b = 5 + k % 2
                dve.wait_ge(*n.filled(b))
                own()
                dve.tensor_copy(h[:, k, :], bank[b][:, :]).then_inc(*n.mark(f"bank_read{b}"))
            own()
            condition()
            for _ in range(AHEAD):
                split()
            for l in range(DEPTH):
                ctx_too = l < DEPTH - 1
                cols = slice(0, T) if ctx_too else LAT
                if l == 0:
                    mods(FIRST_BLOCKS)
                    finish_mods(0, 0, FIRST_BLOCKS, v("b_mod0"), (SCALE1,), (GATE1,))
                    modulate(0, SHIFT1, SCALE1)
                    up_down(slice(0, T), 0, GATE1, RIDERS[0], 0, FIRST_BLOCKS, (0, None))
                    finish = lambda: finish_mods(0, FIRST_BLOCKS, RIDERS[0], v("b_mod0"), (SCALE2, SCALE3), (GATE3,))
                else:
                    condition()
                    up_down(slice(0, T), 1, GATE1, RIDERS[2], 2, 0, (0, 2))
                    finish = lambda: finish_mods(2, 0, RIDERS[2], v("b_ada", 0, 48), (1, 4))
                layer_norm(slice(0, T), l, 0, (l, SHIFT2, SCALE2), finish)
                if l == 0:
                    units(3)
                    for pair in range(KD):
                        more = pair < KD - 1
                        n.next("bank_read0")
                        dve.tensor_copy(kS[:, :], bank[1][:, :]).then_inc(*n.mark("bank_read1"))
                        n.next("bank_read2")

                        def values():
                            dve.wait_ge(*n.filled(6))
                            dve.tensor_copy(vS[:, :, :], bank[6][:, :].rearrange("p (t c) -> p t c", c=P)).then_inc(*n.mark("bank_read6"))

                        attend(NA[pair % 2], lambda qq: pair, started=values, after=coming_units(3 * more))
                        if more:
                            dve.wait_ge(*n.next("units_done"))
                else:
                    def key_head(i, k):
                        for b in range(4):
                            n.next(f"bank_read{b}")
                        dve.wait_ge(*n.filled(6))
                        own()
                        dve.tensor_copy(vS[:, :, 0:HD], bank[6][:, :].rearrange("p (t c) -> p t c", c=P)[:, :, 0:HD])\
                            .then_inc(*n.mark("bank_read6"))
                        for j, (b, x) in enumerate(((0, kS[:, LAT]), (2, qS[:, 0, LAT]), (3, qS[:, 1, LAT]))):
                            rotate(4 + j % 2, x)
                        attend(WA, lambda qq: i * 2 + qq, after=coming_units(k))
                        if k:
                            dve.wait_ge(*n.next("units_done"))

                    more = {"bank_read0": 1, "bank_read1": 1, "bank_read2": 1, "bank_read3": 1, "bank_read4": 6,
                            "bank_read5": 5, "bank_read6": 9, "bank_read7": 2,
                            "max_ready": 8, "p_ready": 8, "ao_hi": 2, "sink_exp": 8, "q_ready": 3,
                            "dve": 8 + 16 + 3}
                    units(4)
                    with n.loop(dve, 3, strides(1, **more)) as i:
                        key_head(i, 4)
                    key_head(3, 0)
                out_projection(cols, l)
                layer_norm(cols, l, 1, (l, SHIFT3, SCALE3))
                up_down(cols, l, GATE3, RIDERS[2 * l + 1], 2 * l + 1, 0, (l, 1))
                if l == 0:
                    layer_norm(cols, 0, 2, (1, SHIFT1, SCALE1),
                               lambda: finish_mods(1, 0, RIDERS[1], v("b_mod1"), (SCALE1, SCALE2, SCALE3), (GATE1, GATE3)))
                else:
                    layer_norm(cols, 1, 2, None, lambda: finish_mods(3, 0, RIDERS[3], v("b_ada", 48, 48), (1, 4)))

            def rms_modulate(m, scale, cols, split_too):
                own()
                dve.sem_inc(*n.mark("h_ready"))
                groups = [(g, c) for g, c in enumerate(GROUPS) if c.start < cols.stop]
                dve.wait_ge(*n.next("bank_read5"))
                own()
                dve.reciprocal(tmp[:, 1, cols], tmp[:, 0, cols]).then_inc(*n.mark("dve"))
                own()

                def scaled(k):
                    for g, c in groups:
                        dve.scalar_tensor_tensor(hm[:, k, c], h[:, k, c], mcol(m, scale, k, g), tmp[:, 1, c], ALU.mult, ALU.mult)\
                            .then_inc(*n.mark("scaled" if (g, c) == groups[-1] else "dve"))

                if split_too:
                    scaled_and_low(scaled)
                else:
                    for k in range(KD):
                        scaled(k)

            def copy(b, dst, src, key=None):
                dve.wait_ge(*n.filled(b))
                own()
                dve.tensor_copy(dst, src).then_inc(*n.mark(key or f"bank_read{b}"))

            def inverse(b, j, c):
                dve.wait_ge(*n.next(f"bank_read{b}"))
                own()
                dve.reciprocal(tmp[:, j, c], tmp[:, j, c]).then_inc(*n.mark("inverse_ready"))

            for name in ("qn", "qr"):
                own()
                dve.tensor_scalar(v(name), v(name), QK_DIM ** -0.5, None, ALU.mult).then_inc(*n.mark("dve"))
            own()
            dve.sem_inc(*n.mark("h_ready"))
            for k in range(KD):
                b = 4 + k % 2
                copy(b, h[:, k, CTX], bank[b][:, 0:S])
            for l in range(DEPTH):
                ctx_too = l < DEPTH - 1
                cols = slice(0, T) if ctx_too else LAT
                tts = range(4 if ctx_too else 2)
                nt = len(tts)
                rms_modulate(2 + l, 1, slice(0, T), True)
                for j in range(10):
                    units(1)
                    n.next(f"bank_read{j % 4}")
                copy(7, wsT[:, :, :], bank[7][:, :].rearrange("p (h c) -> p h c", c=P))
                dve.wait_ge(*n.next("bank_read4"))
                own()
                if ctx_too:
                    dve.reciprocal(tmp[0:96, 0, :], tmp[0:96, 0, :]).then_inc(*n.mark("inverse_ready"))
                else:
                    dve.reciprocal(tmp[64:96, 0, CTX], tmp[64:96, 0, CTX]).then_inc(*n.mark("dve"))
                    dve.reciprocal(tmp[0:96, 0, LAT], tmp[0:96, 0, LAT]).then_inc(*n.mark("inverse_ready"))
                for tt in tts:
                    n.next(f"bank_read{6 + tt % 2}")
                dve.wait_ge(*n.filled(5))
                own()
                for i in range(2):
                    x = px[:, 2 + i, cols]
                    dve.scalar_tensor_tensor(x, x, v("sgu", 2 * l + i, 1), bank[5][:, cols], ALU.mult, ALU.mult)\
                        .then_inc(*n.mark("bank_read5" if i else "dve"))
                dve.wait_ge(*n.next("xhi_ready"))
                dve.tensor_tensor(xlo[:, 2, cols], bank[4][:, cols], xhi[:, 2, cols].bitcast(F32), ALU.subtract).then_inc(*n.mark("bank_read4"))
                for tt in tts:
                    b = 4 + tt % 2
                    copy(b, vtok[:, tt, :], bank[b][:, 0:2 * P])
                dve.wait_ge(*n.filled(6))
                for i in range(2):
                    x = px[:, 6 + i, cols]
                    dve.scalar_tensor_tensor(x, x, v("qlora", 2 * l + i, 1), bank[6][:, cols], ALU.mult, ALU.mult)\
                        .then_inc(*n.mark("bank_read6" if i else "dve"))
                dve.wait_ge(*n.filled(7))
                dve.scalar_tensor_tensor(px[:, 8, :], px[:, 8, :], v("kvlora", l, 1), bank[7][:, :], ALU.mult, ALU.mult)\
                    .then_inc(*n.mark("bank_read7"))
                for tt in tts:
                    b = 4 + tt % 2
                    dve.wait_ge(*n.filled(b))
                    for i in range(2):
                        for e in range(2):
                            rows = slice(e * HD, (e + 1) * HD)
                            x = px[rows, i, tt * P:(tt + 1) * P]
                            dve.tensor_tensor(x, x, bank[b][rows, i * S + e * P:i * S + (e + 1) * P], ALU.mult)\
                                .then_inc(*n.mark(f"bank_read{b}" if i + e == 2 else "dve"))
                own()
                dve.sem_inc(*n.mark("ya_ready"))
                dve.wait_ge(*n.next("xhi_ready"))
                dve.tensor_tensor(xlo[:, 3, cols], bank[5][:, cols], xhi[:, 3, cols].bitcast(F32), ALU.subtract).then_inc(*n.mark("bank_read5"))
                own()
                dve.sem_inc(*n.mark("x_ready", 2))
                for i in range(2):
                    dve.wait_ge(*n.next("xhi_ready"))
                    dve.tensor_tensor(xlo[:, i, cols], px[:, i, cols], xhi[:, i, cols].bitcast(F32), ALU.subtract).then_inc(*n.mark("x_ready"))
                n.next("bank_read6", 3)
                n.next("bank_read7", 3)
                for hh in range(4):
                    copy(6 + hh % 2, kn[:, hh, :], bank[6 + hh % 2][:, :])
                for tt in range(4):
                    copy(6 + tt % 2, vt[:, tt, :], bank[6 + tt % 2][:, :])
                inverse(4, 0, cols)
                inverse(5, 1, slice(0, T))
                own()
                for hh in range(4):
                    rows = slice(hh % 2 * HD, hh % 2 * HD + HD)
                    b = bank[4 + hh]
                    dve.wait_ge(*n.filled(4 + hh))
                    x = qn[:, hh, cols]
                    dve.scalar_tensor_tensor(x, x, v("qn", l, 1), b[:, cols], ALU.mult, ALU.mult).then_inc(*n.mark("dve"))
                    x = qr[rows, hh // 2, cols]
                    dve.scalar_tensor_tensor(x, x, v("qr", l, 1)[rows, :], b[rows, cols], ALU.mult, ALU.mult).then_inc(*n.mark(f"bank_read{4 + hh}"))
                for hh in range(4):
                    rows = slice(hh % 2 * HD, hh % 2 * HD + HD)
                    b = bank[4 + hh]
                    dve.wait_ge(*n.filled(4 + hh))
                    x = kn[:, hh, :]
                    dve.scalar_tensor_tensor(x, x, v("kn", l, 1), b[:, :], ALU.mult, ALU.mult).then_inc(*n.mark("dve"))
                    dve.scalar_tensor_tensor(kr[rows, hh // 2, :], px[rows, 9, :], v("kr", l, 1)[rows, :], b[rows, :], ALU.mult, ALU.mult)\
                        .then_inc(*n.mark(f"bank_read{4 + hh}"))
                for j, x in enumerate((qr[:, 0, LAT], qr[:, 1, LAT], kr[:, 0, LAT], kr[:, 1, LAT])):
                    rotate(4 + j, x)
                attend(mla_plan(ctx_too), lambda hh: 4 + hh, BLOCK2)
                more = 1 if ctx_too else 0
                with n.loop(dve, 2, strides(dve=4 * more, **{f"bank_read{b}": 1 for b in range(4)})) as i:
                    for b in range(4):
                        units(1)
                        residual(b, 2 + l, 2, i * 4 + b, cols)
                rms_modulate(2 + l, 4, cols, False)
                copy(4, tmp[0:N_EXP, 0, cols], bank[4][0:N_EXP, cols])
                copy(5, aff[:, 0:nt, :], bank[5][:, 0:nt * N_EXP].rearrange("p (t e) -> p t e", e=N_EXP))
                for b in (6, 7):
                    n.next(f"bank_read{b}", nt)
                A = aff[:, 0:nt, :]
                peak, total = pos[:, 0, 0:nt], pos[:, 1, 0:nt]
                own()
                dve.tensor_reduce(peak, A, AXX, ALU.max).then_inc(*n.mark("dve"))
                own()
                dve.tensor_tensor(A, A, peak.unsqueeze(2).broadcast_to([P, nt, N_EXP]), ALU.subtract).then_inc(*n.mark("logits_moved"))
                dve.wait_ge(*n.next("softmax_exp"))
                dve.tensor_reduce(total, A, AXX, ALU.add).then_inc(*n.mark("dve"))
                own()
                dve.reciprocal(total, total).then_inc(*n.mark("dve"))
                own()
                dve.tensor_tensor(A, A, total.unsqueeze(2).broadcast_to([P, nt, N_EXP]), ALU.mult).then_inc(*n.mark("softmax_in"))
                copy(4, tmp[0:N_EXP, 1, cols], bank[4][0:N_EXP, cols])
                for g in range(nt // 2):
                    work = tmp[0:N_EXP, 1, GROUPS[g]]
                    for _ in range(CAP // 8):
                        own()
                        dve.max(top8[0:N_EXP, :], work).then_inc(*n.mark("dve"))
                        own()
                        dve.match_replace(work, top8[0:N_EXP, :], work, -1.0).then_inc(*n.mark("dve"))
                    taken, place = tmp[0:N_EXP, 3, GROUPS[g]], tmp[0:N_EXP, 2, GROUPS[g]]
                    own()
                    dve.tensor_scalar(taken, work, 0.0, None, ALU.is_lt).then_inc(*n.mark("dve"))
                    own()
                    dve.tensor_tensor_scan(place, tab("ones", 0, 1)[0:N_EXP, :].broadcast_to([N_EXP, S]), taken, 0.0, ALU.mult, ALU.add)\
                        .then_inc(*n.mark("dve"))
                    own()
                    dve.tensor_tensor(place, place, taken, ALU.mult).then_inc(*n.mark("dve"))
                    own()
                    dve.tensor_scalar(place, place, -1.0, None, ALU.add).then_inc(*n.mark("slots_ready" if g == nt // 2 - 1 else "dve"))
                copy(5, pos[:, 0:nt, :], bank[5][:, 0:nt * N_EXP].rearrange("p (t e) -> p t e", e=N_EXP))
                for tt in tts:
                    own()
                    dve.tensor_tensor(oh[:, tt, :, :], pos[:, tt, :].unsqueeze(2).broadcast_to([P, N_EXP, CAP]),
                                      tab("slots").unsqueeze(1).broadcast_to([P, N_EXP, CAP]), ALU.is_equal).then_inc(*n.mark("dve"))
                    own()
                    dve.tensor_tensor(ohw[:, tt, :].rearrange("p (e s) -> p e s", s=CAP), oh[:, tt, :, :],
                                      aff[:, tt, :].unsqueeze(2).broadcast_to([P, N_EXP, CAP]), ALU.mult)\
                        .then_inc(*n.mark("slots_ready" if tt == nt - 1 else "dve"))
                if not ctx_too:
                    own()
                    dve.memset(xsT[:, :, :, CAP:2 * CAP], 0.0).then_inc(*n.mark("dve"))
                for g in range(nt // 2):
                    for k in range(KD):
                        b = 4 + k % 4
                        if k % 2:
                            n.next(f"bank_read{b}")
                        else:
                            copy(b, xsT[:, k, :, g * CAP:(g + 1) * CAP], bank[b][:, :].rearrange("p (e s) -> p e s", s=CAP))
                n.next("bank_read4", nt // 2)
                n.next("bank_read5", nt // 2)
                own()
                dve.sem_inc(*n.mark("slots_used"))

                def tokens(e):
                    dve.wait_ge(*n.next("est_hi"))
                    dve.tensor_tensor(est[:, :, 64:P].unsqueeze(2), xsT[:, :, ds(e, 1), :], est[:, :, 0:64].bitcast(F32).unsqueeze(2), ALU.subtract)\
                        .then_inc(*n.mark("est_ready"))

                def hidden_low():
                    dve.wait_ge(*n.next("hidT_hi"))
                    dve.tensor_tensor(hidT[:, :, 64:P], bank[4][:, 0:256].rearrange("p (j c) -> p j c", c=64),
                                      hidT[:, :, 0:64].bitcast(F32), ALU.subtract).then_inc(*n.mark("bank_read4"))

                def gate(turned):
                    units(4)
                    dve.wait_ge(*n.next("gate_low"))
                    own()
                    dve.tensor_tensor(tmp[0:64, 1, :], bank[0][0:64, :], tmp[0:64, 0, :], ALU.add).then_inc(*n.mark("bank_read0"))
                    own()
                    dve.sem_inc(*n.mark("gate_in"))
                    if turned:
                        hidden_low()

                def up():
                    units(4)
                    dve.wait_ge(*n.next("up_low"))
                    dve.tensor_tensor(tmp[0:64, 2, :], bank[1][0:64, :], tmp[0:64, 2, :], ALU.add).then_inc(*n.mark("bank_read1"))
                    dve.wait_ge(*n.next("gate_ready"))
                    own()
                    dve.tensor_tensor(hid[0:64, :], tmp[0:64, 1, :], tmp[0:64, 2, :], ALU.mult).then_inc(*n.mark("hid_ready"))

                def down():
                    units(4)
                    for half in range(2):
                        dve.wait_ge(*n.next("y_low"))
                        y = ysb[0:64, half * 512:(half + 1) * 512]
                        dve.tensor_tensor(y, bank[2 + half][0:64, :], y, ALU.add).then_inc(*n.mark(f"bank_read{2 + half}"))
                    own()
                    dve.sem_inc(*n.mark("slots_used"))

                grow = strides(3, slots_used=1, est_hi=1, est_ready=1, gate_low=1, gate_in=1, gate_ready=1, up_low=1, hid_ready=1,
                               hidT_hi=1, y_low=2, **{f"bank_read{b}": 1 for b in range(5)})
                tokens(0)
                gate(False)
                up()
                tokens(1)
                with n.loop(dve, N_EXP - 2, grow) as i:
                    gate(True)
                    up()
                    tokens(i + 2)
                    down()
                if l == DEPTH - 1:
                    left[0] = 16 - AHEAD
                gate(True)
                up()
                down()
                hidden_low()
                down()
                for k in range(KD):
                    b = 4 + k % 4
                    dve.wait_ge(*n.filled(b))
                    residual(b, 2 + l, 5, k, cols)
                own()
                dve.sem_inc(*n.mark("h_ready"))

            for t in range(2):
                for half in range(2):
                    b = 4 + half
                    dve.wait_ge(*n.filled(b))
                    own()
                    dve.tensor_copy(outT[:, t, half * 512:(half + 1) * 512], bank[b][:, :]).then_inc(*n.mark(f"bank_read{b}"))
            own()
            dve.sem_inc(*n.mark("out_ready"))

        @block.gpsimd
        def _(pool):
            n = Counts(s, BANKS)
            pool.memset(vrow[:, :, :], 0.0).then_inc(s["zeroed"], 1)
            pool.wait_ge(*n.next("inputs_loaded", N_LOADS * 16))
            pool.wait_ge(*n.next("x_ready", 2 * KD))
            n.next("bank_read7", RIDERS[0])
            rpb = a["rpb"]
            with n.loop(pool, 2, dict(bank_read7=4, bias_loaded=8 * 64, bias_ready=8)) as i:
                for f in range(4):
                    pool.wait_ge(*n.peek("bank_read7", -1))
                    for e in range(2):
                        for t in range(2):
                            for r2 in range(2):
                                r = 2 * t + r2
                                head = i * 8 + (2 * f + e)
                                row0 = NA_KH - 1 - r
                                rows = rpb[ds(head, 1), row0:row0 + ROWS, 0:GRID_W]
                                src = bass.AP(rpb.tensor, rows.offset, [[1, GRID_W], [RPB_W, ROWS], [1, GRID_W]])
                                pool.dma_start(bt[f % 2][r2 * GRID_W:(r2 + 1) * GRID_W, e, t, :].rearrange("p (r c) -> p r c", c=GRID_W),
                                               src).then_inc(s["bias_loaded"], 16)
                    for e in range(2):
                        if e == 0:
                            pool.wait_ge(*n.next("bias_loaded", 8 * 16))
                        x = bt[f % 2][:, e, :, :].rearrange("p t (r c) -> p (t r) c", c=GRID_W)
                        pool.tensor_tensor(x, x, tab("na_mask").unsqueeze(1).broadcast_to([P, 2 * ROWS, GRID_W]), ALU.add)\
                            .then_inc(*n.mark("bias_ready"))
                    n.next("bank_read7")
            pool.sem_inc(s["y_free"], 1)
            y_rows = ysb[0:2 * CAP, :]
            pool.wait_ge(*n.next("h_ready", 7))
            pool.dma_start(xtok[:, 0:2, :], a["ctx_2"][0].rearrange("(t p) d -> p t d", p=P)).then_inc(s["ctx_loaded"], 16)
            for l in range(DEPTH):
                if l:
                    pool.wait_ge(*n.next("h_ready", 3))
                for dst, src in (
                        (wuq[:, :, :], a["w_uq_2"][l].rearrange("(k p) n -> p k n", p=P)),
                        (wukv[:, :], a["w_ukv_2"][l]),
                        (wsgu[:, :, :], a["w_sgu_2"][l].rearrange("h p q -> p h q")),
                        (bsgu[0:1, :], a["b_sgu_2"][l].rearrange("h (o p) -> o h p", o=1)),
                        (wr[:, :, :], a["w_router_2"][l].rearrange("(k p) e -> p k e", p=P))):
                    pool.dma_start(dst, src).then_inc(s["small_loaded"], 16)
                groups = 2 if l < DEPTH - 1 else 1
                n.next("slots_used")
                for chunks in (range(3), range(3, 4)):
                    with n.loop(pool, 4 * len(chunks), dict(slots_used=1, y_stored=16)) as i:
                        pool.wait_ge(*n.next("slots_used"))
                        pool.dma_start(yscr[ds(i + 4 * chunks[0], 1), :, :].rearrange("e s d -> (e s) d"), y_rows)\
                            .then_inc(s["y_stored"], 16)
                        pool.wait_ge(*n.next("y_stored", 16))
                        pool.sem_inc(s["y_free"], 1)
                    for g in range(groups):
                        for c in chunks:
                            pool.dma_start(yp[:, g, c, :], yscr[4 * c:4 * c + 4, g * CAP:(g + 1) * CAP, :]).then_inc(s["y_loaded"], 16)


def lay_out(inputs):
    arrays = {k: np.ascontiguousarray(v) for k, v in inputs.items()}
    arrays["rpb"] = np.pad(arrays.pop("na_rpb")[0], ((0, 0), (0, 0), (RPB_PAD, RPB_PAD)))
    kv = arrays["wa_w_qkv"][0][:, D:].reshape(D, 2, 4, 1, HD)
    arrays["wa_kv"] = np.ascontiguousarray(np.repeat(kv, 2, 3).transpose(0, 2, 1, 3, 4).reshape(D, 1024))
    arrays["w_kr"] = np.ascontiguousarray(np.repeat(arrays["w_in_2"][:, :, None, IN_W - QK_ROPE:], 2, 2).reshape(DEPTH, D, P))
    arrays["tables"] = make_tables()
    return arrays


def kernel(**inputs):
    import concourse.bacc as bacc
    from concourse.bass_utils import run_bass_kernel_spmd

    nc = bacc.Bacc("TRN2", target_bir_lowering=False, num_devices=1)
    arrays = lay_out(inputs)
    a = {k: nc.dram_tensor(f"in_{k}", x.shape, mybir.dt.from_np(x.dtype), kind="ExternalInput").ap() for k, x in arrays.items()}
    out = nc.dram_tensor("out_x", (1, S, D), F32, kind="ExternalOutput").ap()
    build(nc, a, out)
    r = run_bass_kernel_spmd(nc, [{f"in_{k}": x for k, x in arrays.items()}], core_ids=[0])
    return r.results[0]["out_x"]
```
